# Optimizing a Trainium2 kernel written in Bass

```python
import jax
import jax.numpy as jnp
from jax import lax
import numpy as np

D_MODEL = 2048
BATCH = 1
SEQ = 512
DEPTH = 2
DEC_BATCH = 8
DEC_SEQ = 4
PAST_LEN = 512
PAGE_SIZE = 128

F32 = jnp.float32
GROUP_W = D_MODEL // 4
RET_HEADS = 4
RET_DV = GROUP_W // RET_HEADS
RET_DK = RET_DV // 2
RET_CHUNK = 128
SB_HEADS = 4
SB_HD = GROUP_W // SB_HEADS
SB_BLOCK = 128
DSA_HEADS = 4
DSA_HD = GROUP_W // DSA_HEADS
IDX_HEADS = 8
IDX_HD = 64
DSA_TOPK_MAX = 256
DSA_BLOCK = 128
DSA_CACHE_W = 2 * DSA_HD + IDX_HD
RW_HD = 64
RW_HEADS = GROUP_W // RW_HD
RW_DECAY_LORA = 96
RW_A_LORA = 96
SHIFT_W = 3 * GROUP_W + RW_DECAY_LORA + RW_A_LORA
RW_LN_EPS = 64e-5
NORM_EPS = 1e-6
ROPE_BASE = 10000.0
COL_SIZES = (
    ('ret_q', RET_HEADS * RET_DK), ('ret_k', RET_HEADS * RET_DK), ('ret_v', GROUP_W), ('ret_g', GROUP_W),
    ('sb_q', GROUP_W), ('sb_k', GROUP_W), ('sb_v', GROUP_W), ('sb_g', GROUP_W),
    ('dsa_q', GROUP_W), ('dsa_k', DSA_HD), ('dsa_v', DSA_HD), ('idx_q', IDX_HEADS * IDX_HD),
    ('idx_k', IDX_HD), ('idx_w', IDX_HEADS), ('dsa_g', GROUP_W),
    ('rw_shift', SHIFT_W), ('rw_g', GROUP_W),
)
IN_COLS = sum(n for _, n in COL_SIZES)

kernel_name = 'hybrid_ret_sb_dsa_rwkv7_step'

def _rmsnorm(x, g):
    xf = x.astype(F32)
    y = xf * lax.rsqrt(jnp.mean(xf * xf, axis=-1, keepdims=True) + NORM_EPS)
    return (y * g.astype(F32)).astype(x.dtype)

def _split_cols(p):
    out, off = {}, 0
    for name, n in COL_SIZES:
        out[name] = p[..., off:off + n]
        off += n
    return out

def _blocks(t, blk):
    n, L = t.shape[:2]
    return jnp.moveaxis(t.reshape(n, L // blk, blk, *t.shape[2:]), 1, 0)

def _unblocks(t):
    t = jnp.moveaxis(t, 0, 1)
    return t.reshape(t.shape[0], -1, *t.shape[3:])

def _rotary(x, pos):
    half = x.shape[-1] // 2
    inv = 1.0 / (ROPE_BASE ** (jnp.arange(half, dtype=F32) / half))
    ang = pos.astype(F32)[:, None] * inv[None, :]
    cos = jnp.cos(ang)[None, :, None, :]
    sin = jnp.sin(ang)[None, :, None, :]
    x1, x2 = x[..., :half], x[..., half:]
    return jnp.concatenate([x1 * cos - x2 * sin, x1 * sin + x2 * cos], axis=-1)

def _retention(q, k, v, pos, s0):
    n, L = q.shape[:2]
    chunk = RET_CHUNK if L % RET_CHUNK == 0 else L
    q = _rotary(q.astype(F32), pos)
    k = _rotary(k.astype(F32), pos) * (RET_DK ** -0.5)
    v = v.astype(F32)
    log_g = jnp.log1p(-jnp.exp2(-5.0 - jnp.arange(RET_HEADS, dtype=F32)))
    i = jnp.arange(chunk, dtype=F32)
    diff = i[:, None] - i[None, :]
    dmask = jnp.where(diff[None] >= 0, jnp.exp(jnp.maximum(diff, 0.0)[None] * log_g[:, None, None]), 0.0)
    q_dec = jnp.exp((i + 1.0)[:, None] * log_g[None, :])
    k_dec = jnp.exp((chunk - 1.0 - i)[:, None] * log_g[None, :])
    s_dec = jnp.exp(chunk * log_g)

    def step(S, inp):
        qc, kc, vc = inp
        att = jnp.einsum('nqhd,nkhd->nhqk', qc, kc) * dmask[None]
        o = (jnp.einsum('nhqk,nkhe->nqhe', att, vc)
             + jnp.einsum('nqhd,nhde->nqhe', qc, S) * q_dec[None, :, :, None])
        S = S * s_dec[None, :, None, None] + jnp.einsum('nkhd,nkhe->nhde', kc * k_dec[None, :, :, None], vc)
        return S, o

    S, o = lax.scan(step, s0.astype(F32), (_blocks(q, chunk), _blocks(k, chunk), _blocks(v, chunk)))
    o = _unblocks(o)
    o = o * lax.rsqrt(jnp.mean(o * o, axis=-1, keepdims=True) + NORM_EPS)
    return o.reshape(n, L, RET_HEADS * RET_DV), S

def _stick_breaking(q, k, v, q_pos, k_pos):
    n, Lq, H, d = q.shape
    blk = SB_BLOCK if Lq % SB_BLOCK == 0 else Lq
    k = k.astype(F32)
    v = v.astype(F32)
    scale = d ** -0.5

    def one(args):
        qi, pi = args
        z = jnp.einsum('nqhd,nkhd->nhqk', qi, k) * scale
        vis = (k_pos[None, :] < pi[:, None])[None, None]
        log_1mb = jnp.where(vis, jax.nn.log_sigmoid(-z), 0.0)
        rev = lax.cumsum(log_1mb, axis=3, reverse=True)
        after = jnp.concatenate([rev[..., 1:], jnp.zeros_like(rev[..., :1])], axis=-1)
        w = jnp.where(vis, jnp.exp(jax.nn.log_sigmoid(z) + after), 0.0)
        return jnp.einsum('nhqk,nkhd->nqhd', w, v)

    o = lax.map(one, (_blocks(q.astype(F32), blk), q_pos.reshape(Lq // blk, blk)))
    return _unblocks(o)

def _dsa(q, k, v, iq, ik, iw, q_pos, k_pos):
    n, Lq, H, d = q.shape
    Lk = k.shape[1]
    topk = min(DSA_TOPK_MAX, Lk // 4)
    blk = DSA_BLOCK if Lq % DSA_BLOCK == 0 else Lq
    k = k.astype(F32)
    v = v.astype(F32)
    ik = ik.astype(F32)
    gather = jax.vmap(lambda rows, idx: rows[idx])

    def one(args):
        qi, iqi, iwi, pi = args
        rel = jax.nn.relu(jnp.einsum('nqhe,nke->nqhk', iqi, ik) * (IDX_HD ** -0.5))
        score = jnp.einsum('nqhk,nqh->nqk', rel, iwi * (IDX_HEADS ** -0.5))
        vis = (k_pos[None, :] <= pi[:, None])[None]
        score = jnp.where(vis, score, -jnp.inf)
        _, idx = lax.top_k(score, topk)
        kg = gather(k, idx)
        vg = gather(v, idx)
        ok = (k_pos[idx] <= pi[None, :, None])[:, None]
        logits = jnp.einsum('nqhd,nqkd->nhqk', qi, kg) * (d ** -0.5)
        p = jax.nn.softmax(jnp.where(ok, logits, -jnp.inf), axis=-1)
        return jnp.einsum('nhqk,nqkd->nqhd', p, vg)

    o = lax.map(one, (_blocks(q.astype(F32), blk), _blocks(iq.astype(F32), blk),
                      _blocks(iw.astype(F32), blk), q_pos.reshape(Lq // blk, blk)))
    return _unblocks(o)

def _rwkv7(xs, s0, w0, w2, a0, a2, k_k, k_a, r_k, lnx_w, lnx_b):
    n, L, _ = xs.shape
    xs = xs.astype(F32)
    o1 = GROUP_W
    o2 = o1 + RW_DECAY_LORA
    o3 = o2 + GROUP_W
    o4 = o3 + GROUP_W
    r, wl, k, v, al = xs[..., :o1], xs[..., o1:o2], xs[..., o2:o3], xs[..., o3:o4], xs[..., o4:]
    w_raw = -jax.nn.softplus(-(w0 + jnp.tanh(wl) @ w2)) - 0.5
    decay = jnp.exp(-jnp.exp(w_raw))
    a = jax.nn.sigmoid(a0 + al @ a2)
    kk = k * k_k
    k = k * (1.0 + (a - 1.0) * k_a)
    hs = lambda t: t.reshape(n, L, RW_HEADS, RW_HD)
    r, decay, k, v, kk, a = hs(r), hs(decay), hs(k), hs(v), hs(kk), hs(a)
    kk = kk / jnp.maximum(jnp.sqrt(jnp.sum(kk * kk, axis=-1, keepdims=True)), 1e-12)

    def step(S, inp):
        rt, wt, kt, vt, kkt, at = inp
        sa = jnp.einsum('nhij,nhj->nhi', S, -kkt)
        S = (S * wt[:, :, None, :] + sa[..., None] * (kkt * at)[:, :, None, :]
             + vt[..., None] * kt[:, :, None, :])
        return S, jnp.einsum('nhij,nhj->nhi', S, rt)

    tm = lambda t: jnp.moveaxis(t, 1, 0)
    S, y = lax.scan(step, s0.astype(F32), (tm(r), tm(decay), tm(k), tm(v), tm(kk), tm(a)))
    y = jnp.moveaxis(y, 0, 1)
    mu = jnp.mean(y, axis=-1, keepdims=True)
    var = jnp.mean((y - mu) ** 2, axis=-1, keepdims=True)
    y = (y - mu) * lax.rsqrt(var + RW_LN_EPS)
    y = y * lnx_w.reshape(RW_HEADS, RW_HD) + lnx_b.reshape(RW_HEADS, RW_HD)
    y = y + jnp.sum(r * k * r_k, axis=-1, keepdims=True) * v
    return y.reshape(n, L, GROUP_W), S

def _layer(x, past, prm):
    shift_prev, ret_s0, wkv_s0, sb_past, dsa_past = past
    g, w_in, mu, w0, w2, a0, a2, k_k, k_a, r_k, lnx_w, lnx_b, w_out = prm
    n, L, _ = x.shape
    past_len = sb_past.shape[1]
    q_pos = past_len + jnp.arange(L, dtype=jnp.int32)
    k_pos = jnp.arange(past_len + L, dtype=jnp.int32)
    h = _rmsnorm(x, g)
    p = _split_cols(jnp.einsum('nld,dc->nlc', h, w_in))
    ret_o, ret_s = _retention(p['ret_q'].reshape(n, L, RET_HEADS, RET_DK),
                              p['ret_k'].reshape(n, L, RET_HEADS, RET_DK),
                              p['ret_v'].reshape(n, L, RET_HEADS, RET_DV), q_pos, ret_s0)
    sb_new = jnp.stack([p['sb_k'], p['sb_v']], axis=2).reshape(n, L, 2, SB_HEADS, SB_HD)
    sb_all = jnp.concatenate([sb_past.astype(sb_new.dtype), sb_new], axis=1)
    sb_o = _stick_breaking(p['sb_q'].reshape(n, L, SB_HEADS, SB_HD), sb_all[:, :, 0], sb_all[:, :, 1],
                           q_pos, k_pos).reshape(n, L, GROUP_W)
    dsa_new = jnp.concatenate([p['dsa_k'], p['dsa_v'], p['idx_k']], axis=-1)
    dsa_all = jnp.concatenate([dsa_past.astype(dsa_new.dtype), dsa_new], axis=1)
    dsa_o = _dsa(p['dsa_q'].reshape(n, L, DSA_HEADS, DSA_HD), dsa_all[..., :DSA_HD],
                 dsa_all[..., DSA_HD:2 * DSA_HD], p['idx_q'].reshape(n, L, IDX_HEADS, IDX_HD),
                 dsa_all[..., 2 * DSA_HD:], p['idx_w'], q_pos, k_pos).reshape(n, L, GROUP_W)
    ps = p['rw_shift']
    prev = jnp.concatenate([shift_prev[:, None].astype(ps.dtype), ps[:, :-1]], axis=1)
    rw_o, wkv_s = _rwkv7(ps + (prev - ps) * mu, wkv_s0, w0, w2, a0, a2, k_k, k_a, r_k, lnx_w, lnx_b)
    silu = lambda t: jax.nn.silu(t.astype(F32))
    mix = jnp.concatenate([ret_o * silu(p['ret_g']), sb_o * silu(p['sb_g']),
                           dsa_o * silu(p['dsa_g']), rw_o * silu(p['rw_g'])], axis=-1)
    x = x + jnp.einsum('nlc,cd->nld', mix, w_out)
    return x, (sb_new, dsa_new, ret_s, wkv_s, ps[:, -1])

def _gather_pages(cache_l, page_table):
    g = cache_l[page_table]
    return g.reshape(g.shape[0], g.shape[1] * g.shape[2], *g.shape[3:])

def setup_inputs(seed: int = 0) -> dict:
    key = jax.random.key(seed)
    ks = jax.random.split(key, 24)
    n_pages = PAST_LEN // PAGE_SIZE
    n_used = DEC_BATCH * n_pages
    n_pool = n_used + max(1, n_used // 4)
    nrm = lambda k, s, sc: sc * jax.random.normal(k, s, F32)
    x_prompt = nrm(ks[0], (BATCH, SEQ, D_MODEL), 1.0)
    x_sample = nrm(ks[1], (DEC_BATCH, DEC_SEQ, D_MODEL), 1.0)
    cache_sb_kv = nrm(ks[2], (DEPTH, n_pool, PAGE_SIZE, 2, SB_HEADS, SB_HD), 1.0)
    cache_dsa = nrm(ks[3], (DEPTH, n_pool, PAGE_SIZE, DSA_CACHE_W), 1.0)
    state_ret = nrm(ks[4], (DEPTH, DEC_BATCH, RET_HEADS, RET_DK, RET_DV), 0.5)
    state_wkv = nrm(ks[5], (DEPTH, DEC_BATCH, RW_HEADS, RW_HD, RW_HD), 0.3)
    state_shift = nrm(ks[6], (DEPTH, DEC_BATCH, SHIFT_W), 1.0)
    page_table = jax.random.permutation(ks[7], n_pool)[:n_used].reshape(DEC_BATCH, n_pages).astype(jnp.int32)
    norm_g = 1.0 + nrm(ks[8], (DEPTH, D_MODEL), 0.02)
    w_in = nrm(ks[9], (DEPTH, D_MODEL, IN_COLS), D_MODEL ** -0.5)
    shift_mu = jax.random.uniform(ks[10], (DEPTH, SHIFT_W), F32)
    rw_w0 = jax.random.uniform(ks[11], (DEPTH, GROUP_W), F32, -3.0, 0.0)
    rw_w2 = nrm(ks[12], (DEPTH, RW_DECAY_LORA, GROUP_W), 0.5 * RW_DECAY_LORA ** -0.5)
    rw_a0 = nrm(ks[13], (DEPTH, GROUP_W), 0.1)
    rw_a2 = nrm(ks[14], (DEPTH, RW_A_LORA, GROUP_W), 0.5 * RW_A_LORA ** -0.5)
    rw_kk = 0.85 + nrm(ks[15], (DEPTH, GROUP_W), 0.05)
    rw_ka = 1.0 + nrm(ks[16], (DEPTH, GROUP_W), 0.05)
    rw_rk = nrm(ks[17], (DEPTH, RW_HEADS, RW_HD), 0.1)
    rw_lnx_w = 1.0 + nrm(ks[18], (DEPTH, GROUP_W), 0.02)
    rw_lnx_b = nrm(ks[19], (DEPTH, GROUP_W), 0.01)
    w_out = nrm(ks[20], (DEPTH, D_MODEL, D_MODEL), D_MODEL ** -0.5)
    final_g = 1.0 + nrm(ks[21], (D_MODEL,), 0.02)
    return {'x_prompt': x_prompt, 'x_sample': x_sample, 'cache_sb_kv': cache_sb_kv, 'cache_dsa': cache_dsa,
            'state_ret': state_ret, 'state_wkv': state_wkv, 'state_shift': state_shift, 'page_table': page_table,
            'norm_g': norm_g, 'w_in': w_in, 'shift_mu': shift_mu, 'rw_w0': rw_w0, 'rw_w2': rw_w2,
            'rw_a0': rw_a0, 'rw_a2': rw_a2, 'rw_kk': rw_kk, 'rw_ka': rw_ka, 'rw_rk': rw_rk,
            'rw_lnx_w': rw_lnx_w, 'rw_lnx_b': rw_lnx_b, 'w_out': w_out, 'final_g': final_g}

def reference(x_prompt, x_sample, cache_sb_kv, cache_dsa, state_ret, state_wkv, state_shift, page_table,
              norm_g, w_in, shift_mu, rw_w0, rw_w2, rw_a0, rw_a2, rw_kk, rw_ka, rw_rk, rw_lnx_w, rw_lnx_b,
              w_out, final_g):
    n_p = x_prompt.shape[0]
    dt = x_prompt.dtype
    hp, hs = x_prompt, x_sample
    p_sb, p_dsa, p_ret, p_wkv, p_shift = [], [], [], [], []
    s_sb, s_dsa, s_ret, s_wkv, s_shift = [], [], [], [], []
    for l in range(DEPTH):
        prm = (norm_g[l], w_in[l], shift_mu[l], rw_w0[l], rw_w2[l], rw_a0[l], rw_a2[l], rw_kk[l], rw_ka[l],
               rw_rk[l], rw_lnx_w[l], rw_lnx_b[l], w_out[l])
        past_p = (jnp.zeros((n_p, SHIFT_W), dt), jnp.zeros((n_p, RET_HEADS, RET_DK, RET_DV), F32),
                  jnp.zeros((n_p, RW_HEADS, RW_HD, RW_HD), F32), jnp.zeros((n_p, 0, 2, SB_HEADS, SB_HD), dt),
                  jnp.zeros((n_p, 0, DSA_CACHE_W), dt))
        hp, st = _layer(hp, past_p, prm)
        p_sb.append(st[0]); p_dsa.append(st[1]); p_ret.append(st[2]); p_wkv.append(st[3]); p_shift.append(st[4])
        past_s = (state_shift[l], state_ret[l], state_wkv[l], _gather_pages(cache_sb_kv[l], page_table),
                  _gather_pages(cache_dsa[l], page_table))
        hs, st = _layer(hs, past_s, prm)
        s_sb.append(st[0]); s_dsa.append(st[1]); s_ret.append(st[2]); s_wkv.append(st[3]); s_shift.append(st[4])
    y_prompt = _rmsnorm(hp, final_g)
    y_sample = _rmsnorm(hs, final_g)
    return (y_prompt, y_sample,
            jnp.stack(p_sb), jnp.stack(p_dsa), jnp.stack(p_ret), jnp.stack(p_wkv), jnp.stack(p_shift),
            jnp.stack(s_sb), jnp.stack(s_dsa), jnp.stack(s_ret), jnp.stack(s_wkv), jnp.stack(s_shift))


_drawn_inputs = setup_inputs


def setup_inputs(seed=0):
    import zlib

    import numpy as np

    out = dict(_drawn_inputs(seed))
    spreads = {}
    factors = {'rw_kk': 3.144, 'rw_lnx_w': 6.727, 'rw_lnx_b': 24.228, 'final_g': 7.618}
    for name, (base, spread) in spreads.items():
        noise = np.random.default_rng([zlib.crc32(name.encode()), seed]).standard_normal(out[name].shape)
        drawn = base * np.exp(spread * noise) if base else spread * noise
        out[name] = jnp.asarray(drawn.astype(out[name].dtype))
    for name, factor in factors.items():
        out[name] = (out[name] * factor).astype(out[name].dtype)
    return out
```

```python
from contextlib import ExitStack, contextmanager

import numpy as np

import concourse.bass as bass
from concourse import mybir

F32 = mybir.dt.float32
I32 = mybir.dt.int32
ALU = mybir.AluOpType
ACT = mybir.ActivationFunctionType
AX = mybir.AxisListType

P = 128
D = 2048
KT = D // P
DEPTH = 2
NP = 512
NB = 8
DS = 4
NS = NB * DS
NT = NP + NS
QB = NP // P
TT = QB + 1
PAST = 512
PAGES = PAST // P
POOL = 40
GW = 512
DSA_W = 320
SHIFT_W = 1728
LORA = 96
TOPK = 128
TOPK_S = (PAST + DS) // 4
C = 64
NC = NP // C
H8 = 8
EPS = 1e-6
LN_EPS = 64e-5
NEG = -1e30
SB_SCALE = 128 ** -0.5
LOG_G = np.log1p(-np.exp2(-5.0 - np.arange(4)))

def _tiles(col, n):
    return [(col + P * i, P) for i in range(n)]

RET_TILES = _tiles(0, 12)
SB_TILES = _tiles(1536, 16)
DSA_TILES = _tiles(3584, 6) + [(4864, 64)] + _tiles(4352, 4) + [(4928, 8)] + _tiles(4936, 4)
RW_TILES = (_tiles(5448, 4) + [(5960, LORA)] + _tiles(6056, 8) + [(7080, LORA)] + _tiles(7176, 4))
SLOTS = 18

ROW_G, ROW_W0, ROW_A0, ROW_KK, ROW_KA, ROW_RK, ROW_LNW, ROW_LNB, ROW_MU = 0, 16, 20, 24, 28, 32, 36, 40, 44
PRM_ROWS = ROW_MU + 14


def constants():
    f = np.float32
    at, parts = {}, []

    def add(name, a):
        a = np.asarray(a, f).reshape(len(a), -1)
        full = np.zeros((P, a.shape[1]), f)
        full[: len(a)] = a
        at[name] = (sum(x.shape[1] for x in parts), a.shape[1])
        parts.append(full)

    i = np.arange(P)
    add("ident", np.eye(P))
    add("ones", np.ones((P, P)))
    add("head_ones", (i[:, None] // 64 == i[None] // 64))
    add("later", i[:, None] > i[None])
    add("before", i[:, None] < i[None])
    diff = i[None, :] - i[:, None]
    add("ret_mask", np.stack([np.where(diff >= 0, np.exp(np.maximum(diff, 0) * g), 0) for g in LOG_G], 1))
    t = np.arange(NS)
    same = t[:, None] // DS == t[None] // DS
    dt = t[None] - t[:, None]
    add("ret_mask_s", np.stack([np.where(same & (dt >= 0), np.exp(np.maximum(dt, 0) * g), 0) for g in LOG_G], 1))
    qdec = np.zeros((P, 2, 4)); kdec = np.zeros((P, 2, 4))
    qdec[:, 0] = np.exp((i[:, None] + 1) * LOG_G); kdec[:, 0] = np.exp((P - 1 - i[:, None]) * LOG_G)
    qdec[:NS, 1] = np.exp((t[:, None] % DS + 1) * LOG_G); kdec[:NS, 1] = np.exp((DS - 1 - t[:, None] % DS) * LOG_G)
    add("qdec", qdec); add("kdec", kdec)
    pos = np.zeros((P, TT), f)
    for a in range(QB):
        pos[:, a] = a * P + i
    pos[:NS, QB] = PAST + t % DS
    inv = (1.0 / (10000.0 ** (np.arange(32, dtype=f) / f(32)))).astype(f)
    ang = (pos[:, :, None] * inv).astype(f).astype(np.float64)
    add("cos", np.cos(ang)); add("sin", np.sin(ang))
    add("cosk", np.cos(ang) * 0.125); add("sink", np.sin(ang) * 0.125)
    add("seq_of", (t[:, None] // DS == np.arange(NB)[None]))
    add("before_s", same & (t[:, None] < t[None]))
    add("dsa_neg", np.where(i[None] <= i[:, None], 0, NEG))
    row = np.arange(P) % NS
    add("dsa_neg_s", np.where((row[:, None] // DS == t[None] // DS) & (t[None] <= row[:, None]), 0, NEG))
    rt = np.arange(NS) % DS
    add("spread", (rt[:, None, None] == row[None, None] % DS) & (np.arange(NB)[None, :, None] == row[None, None] // DS))
    j = np.arange(C)
    half = np.concatenate([j[:, None] < j[None], j[:, None] <= j[None]], 1)
    add("wy_mask", np.concatenate([half, half], 0))
    add("block16", j[:, None] // 16 == j[None] // 16)
    add("chunk_in", np.broadcast_to(np.arange(NP) % C != 0, (P, NP)))
    add("half0", (i % 2 == 0)[:, None]); add("half1", (i % 2 == 1)[:, None])
    return at, np.concatenate(parts, 1)


AT, TABLE = constants()


@contextmanager
def stage(nc, signals):
    with nc.Block() as block:
        yield block
    nc.gpsimd.sem_clear(range(signals[0].num, signals[-1].num + 1))
    nc.all_engine_barrier()


class Steps:

    def __init__(self, engine, sem):
        self.engine, self.sem, self.n = engine, sem, 0

    def __call__(self, instruction):
        self.n += 1
        instruction.then_inc(self.sem, 1)
        return self.n

    def wait(self):
        self.engine.wait_ge(self.sem, self.n)

    def then(self, instruction):
        self(instruction)
        self.wait()


class Loads:

    def __init__(self, engine, sem):
        self.engine, self.sem, self.n = engine, sem, 0

    def __call__(self, out, in_):
        self.n += 16
        self.engine.dma_start(out, in_).then_inc(self.sem, 16)

    def wait(self):
        self.engine.wait_ge(self.sem, self.n)


def inverse_root(act, logged, x, scale=1.0, at=0):
    act.activation(x, x, ACT.Ln, scale=scale).then_inc(logged, 1)
    act.wait_ge(logged, at + 1)
    return act.activation(x, x, ACT.Exp, scale=-0.5)


class Core:

    def __init__(self, tensors):
        self.consts = tensors["consts"]
        self.x_prompt = tensors["x_prompt"]
        self.x_sample = tensors["x_sample"]
        self.cache_sb_kv = tensors["cache_sb_kv"]
        self.cache_dsa = tensors["cache_dsa"]
        self.state_ret = tensors["state_ret"]
        self.state_wkv = tensors["state_wkv"]
        self.state_shift = tensors["state_shift"]
        self.page_table = tensors["page_table"]
        self.norm_g = tensors["norm_g"]
        self.w_in = tensors["w_in"]
        self.shift_mu = tensors["shift_mu"]
        self.rw_w0 = tensors["rw_w0"]
        self.rw_w2 = tensors["rw_w2"]
        self.rw_a0 = tensors["rw_a0"]
        self.rw_a2 = tensors["rw_a2"]
        self.rw_kk = tensors["rw_kk"]
        self.rw_ka = tensors["rw_ka"]
        self.rw_rk = tensors["rw_rk"]
        self.rw_lnx_w = tensors["rw_lnx_w"]
        self.rw_lnx_b = tensors["rw_lnx_b"]
        self.w_out = tensors["w_out"]
        self.final_g = tensors["final_g"]
        self.y_prompt = tensors["y_prompt"]
        self.y_sample = tensors["y_sample"]
        self.p_sb = tensors["p_sb"]
        self.p_dsa = tensors["p_dsa"]
        self.p_ret = tensors["p_ret"]
        self.p_wkv = tensors["p_wkv"]
        self.p_shift = tensors["p_shift"]
        self.s_sb = tensors["s_sb"]
        self.s_dsa = tensors["s_dsa"]
        self.s_ret = tensors["s_ret"]
        self.s_wkv = tensors["s_wkv"]
        self.s_shift = tensors["s_shift"]


def scope(nc, ctx):
    def sb(name, shape, dt=F32):
        return ctx.enter_context(nc.sbuf_tensor(name, shape, dt))

    def ps(name, shape):
        return ctx.enter_context(nc.psum_tensor(name, shape, F32))

    return sb, ps


def turn(nc, k, name, jobs):
    turned, kept_v, kept_s = k.signals[:3]
    R = 4
    with ExitStack() as ctx:
        _, ps = scope(nc, ctx)
        banks = ps(f"{name}_banks", [P, R, 512])
        with stage(nc, k.signals) as block:
            @block.tensor
            def _(pe):
                for n, (pieces, _) in enumerate(jobs):
                    if n >= R:
                        before = n - R
                        pe.wait_ge(kept_v if before % 2 == 0 else kept_s, before // 2 + 1)
                    at = 0
                    for piece in pieces:
                        rows, cols = piece.shape
                        last = pe.transpose(banks[0:cols, n % R, at:at + rows], piece, k.c("ident")[0:rows, 0:rows])
                        at += rows
                    last.then_inc(turned, 1)

            def copies(engine, copy, kept, odd):
                for n, (_, outs) in enumerate(jobs):
                    if n % 2 != odd:
                        continue
                    engine.wait_ge(turned, n + 1)
                    for m, (view, dst) in enumerate(outs):
                        last = copy(dst, view(banks[:, n % R, :]))
                    last.then_inc(kept, 1)

            @block.vector
            def _(dve):
                copies(dve, dve.tensor_copy, kept_v, 0)

            @block.scalar
            def _(act):
                copies(act, act.copy, kept_s, 1)


def project(nc, k, l, name, weights, tiles, source, psum, keep):
    R = 3
    product_ready, kept_prompt, kept_sample = k.signals[:3]
    loaded = k.signals[3:3 + R]
    w_l = weights[bass.ds(l, 1)].rearrange("a (k p) c -> p (a k) c", p=P)
    with stage(nc, k.signals) as block:
        @block.sync
        def _(sp):
            loads = [Loads(sp, s) for s in loaded]
            for i, (col, width, twice) in enumerate(tiles):
                if i >= R:
                    sp.wait_ge(product_ready, i - R + 1)
                loads[i % R](k.ring[:, i % R, :, 0:width], w_l[:, :, col:col + width])
                if twice:
                    loads[i % R](k.ring[:, i % R, :, width:2 * width], w_l[:, :, col:col + width])

        @block.tensor
        def _(pe):
            arrived = [0] * R
            for i, (col, width, twice) in enumerate(tiles):
                arrived[i % R] += 32 if twice else 16
                m = 2 * width if twice else width
                pe.wait_ge(loaded[i % R], arrived[i % R])
                if i >= 2:
                    pe.wait_ge(kept_prompt, i - 1)
                    pe.wait_ge(kept_sample, i - 1)
                for t in range(KT):
                    w = k.ring[:, i % R, t, 0:m]
                    pe.matmul(psum[0:m, i % 2, 0, :], w, source[:, t, 0:NP], start=(t == 0), stop=(t == KT - 1))
                    last = pe.matmul(psum[0:m, i % 2, 1, 0:NS], w, source[:, t, NP:NT], start=(t == 0), stop=(t == KT - 1))
                last.then_inc(product_ready, 1)

        def rows(tile):
            return 2 * tile[1] if tile[2] else tile[1]

        if keep is not None:
            @block.scalar
            def _(act):
                for i, tile in enumerate(tiles):
                    act.wait_ge(product_ready, i + 1)
                    act.copy(keep[0:rows(tile), i, 0:NP], psum[0:rows(tile), i % 2, 0, :]).then_inc(kept_prompt, 1)

            @block.vector
            def _(dve):
                for i, tile in enumerate(tiles):
                    dve.wait_ge(product_ready, i + 1)
                    dve.tensor_copy(keep[0:rows(tile), i, NP:NT], psum[0:rows(tile), i % 2, 1, 0:NS]).then_inc(kept_sample, 1)
        else:
            @block.vector
            def _(dve):
                for i in range(len(tiles)):
                    dve.wait_ge(product_ready, i + 1)
                    dve.tensor_tensor(k.xT[:, i, 0:NP], k.xT[:, i, 0:NP], psum[:, i % 2, 0, :], ALU.add).then_inc(kept_prompt, 1)
                    dve.tensor_tensor(k.xT[:, i, NP:NT], k.xT[:, i, NP:NT], psum[:, i % 2, 1, 0:NS], ALU.add).then_inc(kept_sample, 1)


def project_group(nc, k, l, name, tiles):
    with ExitStack() as ctx:
        _, ps = scope(nc, ctx)
        psum = ps(f"{name}_psum", [P, 2, 2, 512])
        project(nc, k, l, name, k.w_in, [(*t, t == (4864, 64)) for t in tiles], k.hT, psum, k.ft)


def project_out(nc, k, l):
    with ExitStack() as ctx:
        _, ps = scope(nc, ctx)
        psum = ps("out_psum", [P, 2, 2, 512])
        project(nc, k, l, "out", k.w_out, [(P * i, P, False) for i in range(KT)], k.mixT, psum, None)


def load_x(nc, k):
    with ExitStack() as ctx:
        sb, _ = scope(nc, ctx)
        rows = sb("x_rows", [P, 2, D])
        for a in range(TT):
            n = P if a < QB else NS
            arrived, = k.signals[:1]
            with stage(nc, k.signals) as block:
                @block.sync
                def _(sp):
                    src = k.x_prompt.rearrange("b t d -> (b t) d")[a * P:a * P + n] if a < QB else k.x_sample.rearrange("b t d -> (b t) d")
                    sp.dma_start(rows[0:n, a % 2, :], src).then_inc(arrived, 16)
                    sp.wait_ge(arrived, 16)
            turn(nc, k, f"xin{a}", [([rows[0:n, a % 2, P * (4 * q + i):P * (4 * q + i + 1)] for i in range(4)],
                 [(lambda b, n=n: b[:, 0:4 * n].rearrange("p (i t) -> p i t", t=n), k.xT[:, 4 * q:4 * q + 4, a * P:a * P + n])]) for q in range(4)])


def norm(nc, k, name, gains, out):
    squared, summed, scaled, powered, logged = k.signals[:5]
    with ExitStack() as ctx:
        sb, ps = scope(nc, ctx)
        sq = sb(f"{name}_sq", [P, 2, NT])
        rs = sb(f"{name}_rs", [P, NT])
        sums = ps(f"{name}_sums", [P, 2, 512])
        with stage(nc, k.signals) as block:
            @block.scalar
            def _(act):
                for t in range(KT):
                    if t >= 2:
                        act.wait_ge(summed, t - 1)
                    act.activation(sq[:, t % 2, :], k.xT[:, t, :], ACT.Square).then_inc(squared, 1)
                act.wait_ge(scaled, 2)
                inverse_root(act, logged, rs[:, :]).then_inc(powered, 1)

            @block.tensor
            def _(pe):
                for t in range(KT):
                    pe.wait_ge(squared, t + 1)
                    pe.matmul(sums[:, 0, :], k.c("ones"), sq[:, t % 2, 0:NP], start=(t == 0), stop=(t == KT - 1))
                    pe.matmul(sums[:, 1, 0:NS], k.c("ones"), sq[:, t % 2, NP:NT], start=(t == 0), stop=(t == KT - 1)).then_inc(summed, 1)

            @block.vector
            def _(dve):
                dve.wait_ge(summed, KT)
                dve.tensor_scalar(rs[:, 0:NP], sums[:, 0, :], 1.0 / D, EPS, ALU.mult, ALU.add).then_inc(scaled, 1)
                dve.tensor_scalar(rs[:, NP:NT], sums[:, 1, 0:NS], 1.0 / D, EPS, ALU.mult, ALU.add).then_inc(scaled, 1)
                dve.wait_ge(powered, 1)
                for t in range(KT):
                    dve.scalar_tensor_tensor(out[:, t, :], k.xT[:, t, :], gains[:, t:t + 1], rs[:, :], ALU.mult, ALU.mult)


def load_parameters(nc, k, l):
    with ExitStack() as ctx:
        sb, _ = scope(nc, ctx)
        rows = sb("prm_rows", [PRM_ROWS, P])
        loaded, cleared = k.signals[:2]
        with stage(nc, k.signals) as block:
            @block.vector
            def _(dve):
                dve.memset(rows[:, :], 0.0).then_inc(cleared, 1)

            @block.sync
            def _(sp):
                sp.wait_ge(cleared, 1)
                load = Loads(sp, loaded)

                def full(row, ap, n):
                    load(rows[row:row + n, :], ap[bass.ds(l, 1)].rearrange("a (n p) -> (a n) p", p=P))

                full(ROW_G, k.norm_g, KT)
                for row, ap in ((ROW_W0, k.rw_w0), (ROW_A0, k.rw_a0), (ROW_KK, k.rw_kk), (ROW_KA, k.rw_ka),
                                (ROW_LNW, k.rw_lnx_w), (ROW_LNB, k.rw_lnx_b)):
                    full(row, ap, 4)
                load(rows[ROW_RK:ROW_RK + 4, :], k.rw_rk[bass.ds(l, 1)].rearrange("a (j h) d -> (a j) (h d)", h=2))
                mu = k.shift_mu[bass.ds(l, 1)]
                for first, col, n in ((0, 0, 4), (5, 608, 8)):
                    load(rows[ROW_MU + first:ROW_MU + first + n, :], mu[:, col:col + P * n].rearrange("a (n p) -> (a n) p", p=P))
                for slot, col in ((4, 512), (13, 1632)):
                    load(rows[ROW_MU + slot:ROW_MU + slot + 1, 0:LORA], mu[:, col:col + LORA])
                load.wait()
        turn(nc, k, "prm", [([rows[:, :]], [(lambda b: b[:, 0:PRM_ROWS], k.prm[:, :])])])


def spill_x(nc, k, back):
    moved, = k.signals[:1]
    with stage(nc, k.signals) as block:
        @block.sync
        def _(sp):
            a, b = k.x_spill.rearrange("p (k t) -> p k t", t=NT), k.xT[:, :, :]
            (sp.dma_start(b, a) if back else sp.dma_start(a, b)).then_inc(moved, 16)
            sp.wait_ge(moved, 16)


def store_y(nc, k):
    with ExitStack() as ctx:
        sb, _ = scope(nc, ctx)
        rows = sb("fg_rows", [KT, P])
        fg = sb("fg", [P, KT])
        yT = sb("yT", [P, KT, NT])
        y = sb("y", [P, D])
        moved, = k.signals[:1]
        with stage(nc, k.signals) as block:
            @block.sync
            def _(sp):
                sp.dma_start(rows[:, :], k.final_g.rearrange("(n p) -> n p", p=P)).then_inc(moved, 16)
                sp.wait_ge(moved, 16)
        turn(nc, k, "fgt", [([rows[:, :]], [(lambda b: b[:, 0:KT], fg[:, :])])])
        norm(nc, k, "final", fg, yT)
        for a in range(TT):
            n = P if a < QB else NS
            turn(nc, k, f"yout{a}", [([yT[:, 4 * q + i, a * P:a * P + n] for i in range(4)],
                 [(lambda b, n=n: b[0:n, :], y[0:n, 512 * q:512 * q + 512])]) for q in range(4)])
            with stage(nc, k.signals) as block:
                @block.sync
                def _(sp):
                    dst = k.y_prompt.rearrange("b t d -> (b t) d")[a * P:a * P + n] if a < QB else k.y_sample.rearrange("b t d -> (b t) d")
                    sp.dma_start(dst, y[0:n, :]).then_inc(moved, 16)
                    sp.wait_ge(moved, 16)


def gate(nc, k, first, g):
    opened, added, gated = k.signals[:3]
    with stage(nc, k.signals) as block:
        @block.scalar
        def _(act):
            for i in range(4):
                if i >= 2:
                    act.wait_ge(gated, i - 1)
                act.activation(k.scratch[:, i % 2, :], k.ft[:, g + i, :], ACT.Exp, scale=-1.0).then_inc(opened, 1)

        @block.vector
        def _(dve):
            step = Steps(dve, added)
            for i in range(4):
                e, m = k.scratch[:, i % 2, :], k.mixT[:, first + i, :]
                dve.wait_ge(opened, i + 1)
                step.then(dve.tensor_scalar(e, e, 1.0, None, ALU.add))
                step.then(dve.reciprocal(e, e))
                step.then(dve.tensor_tensor(e, e, k.ft[:, g + i, :], ALU.mult))
                dve.tensor_tensor(m, m, e, ALU.mult).then_inc(gated, 1)


def tokens(a):
    return (P, slice(a * P, a * P + P)) if a < QB else (NS, slice(NP, NT))


def side_by_side(n, width):
    return lambda b: b[:, 0:width * n].rearrange("p (i t) -> p i t", t=n)


def retention(nc, k, l):
    ft = k.ft
    with ExitStack() as ctx:
        sb, ps = scope(nc, ctx)
        qk = sb("ret_qk", [P, TT, 512])
        v = sb("ret_v", [P, TT, 512])
        rot = sb("ret_rot", [P, TT, 512])
        tmp = sb("ret_tmp", [P, TT, 4, 32])
        state = sb("ret_state", [P, 2, 2 * P])
        state_s = sb("ret_state_s", [P, NB, 2, P])
        qdz = sb("ret_qdz", [P, 2, 2, NS])
        qT, qdT, kz = ft[:, 0:2, :], ft[:, 2:4, :], ft[:, 4:8, :]
        jobs = []
        for a in range(TT):
            n, cols = tokens(a)
            jobs.append(([ft[:, s, cols] for s in range(4)], [(lambda b, n=n: b[0:n, :], qk[0:n, a, :])]))
            jobs.append(([ft[:, s, cols] for s in range(4, 8)], [(lambda b, n=n: b[0:n, :], v[0:n, a, :])]))
        turn(nc, k, "ret_in", jobs)

        turned, loaded = k.signals[:2]
        with stage(nc, k.signals) as block:
            @block.sync
            def _(sp):
                load = Loads(sp, loaded)
                for s in range(NB):
                    for par in range(2):
                        load(state_s[64 * par:64 * par + 64, s, :, :],
                             k.state_ret[bass.ds(l, 1), s].rearrange("a (j b) d e -> a b d j e", b=2)[0, par])
                load.wait()

            @block.vector
            def _(dve):
                step = Steps(dve, turned)
                dve.memset(state[:, :, :], 0.0)
                dve.memset(qdz[:, :, :, :], 0.0)
                dve.memset(kz[64:128, 0:2, :], 0.0)
                dve.memset(kz[0:64, 2:4, :], 0.0)
                for r0, (n, a0, a1) in enumerate(((P, 0, QB), (NS, QB, TT))):
                    w = a1 - a0
                    for part, (cos, sin) in enumerate((("cos", "sin"), ("cosk", "sink"))):
                        def halves(t):
                            h = t[0:n, a0:a1, 256 * part:256 * part + 256].rearrange("p a (h u d) -> p a h u d", h=4, u=2)
                            return h[:, :, :, 0, :], h[:, :, :, 1, :]

                        def table(name):
                            return k.c(name).rearrange("p (a d) -> p a d", d=32)[0:n, a0:a1].unsqueeze(2).to_broadcast([n, w, 4, 32])

                        def each(op, out, a, b, y):
                            for i in range(w):
                                last = dve.tensor_tensor(out[:, i], a[:, i], b[:, i], y)
                            op(last)

                        (x1, x2), (y1, y2) = halves(qk), halves(rot)
                        z = tmp[0:n, a0:a1]
                        each(step, y1, x1, table(cos), ALU.mult)
                        each(step.then, z, x2, table(sin), ALU.mult)
                        each(step, y2, x1, table(sin), ALU.mult)
                        each(step.then, y1, y1, z, ALU.subtract)
                        each(step.then, z, x2, table(cos), ALU.mult)
                        each(step.then, y2, y2, z, ALU.add)
                        dec = k.c("kdec" if part else "qdec").rearrange("p (r h) -> p r h", r=2)
                        for h in range(4):
                            col = slice(256 * part + 64 * h, 256 * part + 64 * h + 64)
                            step(dve.tensor_scalar(qk[0:n, a0:a1, col], rot[0:n, a0:a1, col], dec[0:n, r0, h:h + 1], None, ALU.mult))
        jobs = []
        for a in range(TT):
            n, cols = tokens(a)
            outs = [(side_by_side(n, 4), ft[:, 0:4, cols])]
            if a == QB:
                outs += [(lambda b, r=r: b[64 * r:64 * r + 64, 2 * NS:4 * NS].rearrange("p (i t) -> p i t", t=NS),
                          qdz[64 * r:64 * r + 64, r, :, :]) for r in range(2)]
            jobs.append(([t[0:n, a, P * i:P * i + P] for t in (rot, qk) for i in range(2)], outs))
            jobs.append(([rot[0:n, a, 256 + P * i:384 + P * i] for i in range(2)],
                         [(lambda b, n=n, r=r: b[64 * r:64 * r + 64, 0:2 * n].rearrange("p (i t) -> p i t", t=n),
                           kz[64 * r:64 * r + 64, 2 * r:2 * r + 2, cols]) for r in range(2)]))
        turn(nc, k, "ret_qk_T", jobs)

        scored, masked, made, kept, grown, carried, stored = k.signals[:7]
        with ExitStack() as inner:
            sb2, ps2 = scope(nc, inner)
            att = sb2("ret_att", [P, 2, 512])
            p_att, p_out, p_state = (ps2(f"ret_p_{x}", [P, 2, 512]) for x in ("att", "out", "state"))
            with stage(nc, k.signals) as block:
                @block.tensor
                def _(pe):
                    for c in range(QB):
                        tok = slice(c * P, c * P + P)
                        if c >= 2:
                            pe.wait_ge(masked, c - 1)
                            pe.wait_ge(carried, c - 1)
                            pe.wait_ge(kept, c - 1)
                        for h in range(4):
                            last = pe.matmul(p_att[:, c % 2, P * h:P * h + P], kz[:, 2 * (h % 2) + h // 2, tok],
                                             qT[:, h // 2, tok], start=True, stop=True)
                        last.then_inc(scored, 1)
                        for j in range(2):
                            last = pe.matmul(p_state[:, c % 2, 256 * j:256 * j + 256], qk[:, c, 256 + P * j:384 + P * j],
                                             v[:, c, 256 * j:256 * j + 256], start=True, stop=True)
                        last.then_inc(grown, 1)
                        pe.wait_ge(masked, c + 1)
                        if c >= 1:
                            pe.wait_ge(carried, c)
                        for h in range(4):
                            out = p_out[:, c % 2, P * h:P * h + P]
                            last = pe.matmul(out, v[:, c, P * h:P * h + P], att[:, c % 2, P * h:P * h + P], start=True, stop=(c == 0))
                            if c:
                                last = pe.matmul(out, state[:, h // 2, P * (h % 2):P * (h % 2) + P], qdT[:, h // 2, tok], start=False, stop=True)
                        last.then_inc(made, 1)

                @block.scalar
                def _(act):
                    for c in range(QB):
                        act.wait_ge(made, c + 1)
                        act.copy(k.mixT[:, 0:4, c * P:c * P + P], p_out[:, c % 2, :].rearrange("p (h t) -> p h t", h=4)).then_inc(kept, 1)

                @block.vector
                def _(dve):
                    for c in range(QB):
                        dve.wait_ge(scored, c + 1)
                        if c >= 2:
                            dve.wait_ge(made, c - 1)
                        dve.tensor_tensor(att[:, c % 2, :], p_att[:, c % 2, :], k.c("ret_mask"), ALU.mult).then_inc(masked, 1)
                        dve.wait_ge(grown, c + 1)
                        dve.wait_ge(made, c + 1)
                        for h in range(4):
                            r, j = h % 2, h // 2
                            s = state[64 * r:64 * r + 64, j, P * r:P * r + P]
                            g = p_state[64 * r:64 * r + 64, c % 2, 256 * j + P * r:256 * j + P * r + P]
                            last = dve.scalar_tensor_tensor(s, s, float(np.exp(P * LOG_G[h])), g, ALU.mult, ALU.add)
                        last.then_inc(carried, 1)

                @block.sync
                def _(sp):
                    store = Loads(sp, stored)
                    sp.wait_ge(carried, QB)
                    for h in range(4):
                        r, j = h % 2, h // 2
                        store(k.p_ret[bass.ds(l, 1), 0, h].rearrange("a d e -> (a d) e"), state[64 * r:64 * r + 64, j, P * r:P * r + P])
                    store.wait()

        scored, masked, made, grown, spread, advanced, copied, stored = k.signals[:8]
        with ExitStack() as inner:
            sb2, ps2 = scope(nc, inner)
            att = sb2("ret_att_s", [NS, 4, NS])
            vx = sb2("ret_vx", [NS, 2, NB, P])
            p_att = ps2("ret_ps_att", [NS, 512])
            p_out = ps2("ret_ps_out", [P, 512])
            p_state = ps2("ret_ps_state", [P, 2, 2, 512])
            with stage(nc, k.signals) as block:
                @block.tensor
                def _(pe):
                    for h in range(4):
                        last = pe.matmul(p_att[:, NS * h:NS * h + NS], kz[:, 2 * (h % 2) + h // 2, NP:NT], qT[:, h // 2, NP:NT], start=True, stop=True)
                    last.then_inc(scored, 1)
                    pe.wait_ge(masked, 1)
                    for h in range(4):
                        pe.matmul(p_out[:, NS * h:NS * h + NS], v[0:NS, QB, P * h:P * h + P], att[:, h, :], start=True, stop=False, skip_group_check=True)
                        for s in range(NB):
                            last = pe.matmul(p_out[:, NS * h + DS * s:NS * h + DS * s + DS], state_s[:, s, h // 2, :],
                                             qdz[:, h % 2, h // 2, DS * s:DS * s + DS], start=False, stop=(s == NB - 1), skip_group_check=True)
                    last.then_inc(made, 1)
                    for h in range(4):
                        pe.wait_ge(spread, h + 1)
                        if h >= 2:
                            pe.wait_ge(advanced, h - 1)
                        for q in range(2):
                            last = pe.matmul(p_state[:, h % 2, q, :], qk[0:NS, QB, 256 + P * (h // 2):384 + P * (h // 2)],
                                             vx[:, h % 2, 4 * q:4 * q + 4, :], start=True, stop=True)
                        last.then_inc(grown, 1)

                @block.scalar
                def _(act):
                    act.wait_ge(made, 1)
                    act.copy(k.mixT[:, 0:4, NP:NT], p_out[:, 0:4 * NS].rearrange("p (h t) -> p h t", h=4)).then_inc(copied, 1)

                @block.vector
                def _(dve):
                    dve.wait_ge(scored, 1)
                    dve.tensor_tensor(att[:, :, :], p_att[:, 0:4 * NS].rearrange("p (h t) -> p h t", h=4),
                                      k.c("ret_mask_s")[0:NS].rearrange("p (h t) -> p h t", h=4), ALU.mult).then_inc(masked, 1)
                    for h in range(5):
                        if h < 4:
                            if h >= 2:
                                dve.wait_ge(grown, h - 1)
                            dve.tensor_tensor(vx[:, h % 2, :, :], v[0:NS, QB, P * h:P * h + P].unsqueeze(1).to_broadcast([NS, NB, P]),
                                              k.c("seq_of")[0:NS].unsqueeze(2).to_broadcast([NS, NB, P]), ALU.mult).then_inc(spread, 1)
                        if h == 0:
                            dve.wait_ge(made, 1)
                            continue
                        g, r = h - 1, (h - 1) % 2
                        dve.wait_ge(grown, g + 1)
                        for q in range(2):
                            s = state_s[64 * r:64 * r + 64, 4 * q:4 * q + 4, g // 2, :]
                            last = dve.scalar_tensor_tensor(s, s, float(np.exp(DS * LOG_G[g])),
                                                            p_state[64 * r:64 * r + 64, g % 2, q, :].rearrange("p (s e) -> p s e", e=P), ALU.mult, ALU.add)
                        last.then_inc(advanced, 1)

                @block.sync
                def _(sp):
                    store = Loads(sp, stored)
                    sp.wait_ge(advanced, 4)
                    for s in range(NB):
                        for par in range(2):
                            store(k.s_ret[bass.ds(l, 1), s].rearrange("a (j b) d e -> a b d j e", b=2)[0, par], state_s[64 * par:64 * par + 64, s, :, :])
                    store.wait()

        head_norm(nc, k)
    gate(nc, k, 0, 8)


def head_norm(nc, k):
    squared, summed, scaled, powered, normed, logged = k.signals[:6]
    with ExitStack() as ctx:
        _, ps = scope(nc, ctx)
        sums = ps("hn_sums", [P, 2, 2, 512])
        with stage(nc, k.signals) as block:
            @block.scalar
            def _(act):
                for i in range(5):
                    if i >= 1:
                        act.wait_ge(scaled, 2 * i)
                        inverse_root(act, logged, k.scratch[:, (i - 1) % 2, :], at=i - 1).then_inc(powered, 1)
                    if i < 4:
                        if i >= 2:
                            act.wait_ge(normed, i - 1)
                        act.activation(k.scratch[:, i % 2, :], k.mixT[:, i, :], ACT.Square).then_inc(squared, 1)

            @block.tensor
            def _(pe):
                for i in range(4):
                    pe.wait_ge(squared, i + 1)
                    pe.matmul(sums[:, i % 2, 0, :], k.c("ones"), k.scratch[:, i % 2, 0:NP], start=True, stop=True)
                    pe.matmul(sums[:, i % 2, 1, 0:NS], k.c("ones"), k.scratch[:, i % 2, NP:NT], start=True, stop=True).then_inc(summed, 1)

            @block.vector
            def _(dve):
                for i in range(4):
                    r = k.scratch[:, i % 2, :]
                    dve.wait_ge(summed, i + 1)
                    dve.tensor_scalar(r[:, 0:NP], sums[:, i % 2, 0, :], 1.0 / P, EPS, ALU.mult, ALU.add).then_inc(scaled, 1)
                    dve.tensor_scalar(r[:, NP:NT], sums[:, i % 2, 1, 0:NS], 1.0 / P, EPS, ALU.mult, ALU.add).then_inc(scaled, 1)
                    dve.wait_ge(powered, i + 1)
                    dve.tensor_tensor(k.mixT[:, i, :], k.mixT[:, i, :], r, ALU.mult).then_inc(normed, 1)


def stick_breaking(nc, k, l):
    ft = k.ft
    with ExitStack() as ctx:
        sb, ps = scope(nc, ctx)
        kv = sb("sb_kv", [P, TT, 1024])
        jobs = []
        for a in range(TT):
            n, cols = tokens(a)
            for u in range(2):
                jobs.append(([ft[:, 4 + 4 * u + s, cols] for s in range(4)], [(lambda b, n=n: b[0:n, :], kv[0:n, a, 512 * u:512 * u + 512])]))
        turn(nc, k, "sb_in", jobs)

        scored, split, shrunk, logged, summed_up, weighted, exped, applied, kept, stored, own, stepped = k.signals[:12]
        units = [(h, b) for h in range(4) for b in range(QB)]
        starts = [sum(NP - P * c for c in range(b)) for b in range(QB + 1)]
        AREA = starts[QB]

        def blk(t, h, b, lo=0, hi=None):
            return t[:, h % 2, starts[b] + lo:(starts[b + 1] if hi is None else starts[b] + hi)]

        with ExitStack() as inner:
            sb2, ps2 = scope(nc, inner)
            mag = sb2("sb_mag", [P, 2, 512])
            low = sb2("sb_low", [P, 2, 512])
            logs = sb2("sb_logs", [P, 2, AREA])
            miss = sb2("sb_miss", [P, 2, AREA])
            p_z = ps2("sb_p_z", [P, 3, 512])
            p_after = ps2("sb_p_after", [P, 2, 512])
            p_out = ps2("sb_p_out", [P, 2, 512])
            with stage(nc, k.signals) as block:
                @block.sync
                def _(sp):
                    store = Loads(sp, stored)
                    for a in range(QB):
                        store(k.p_sb[bass.ds(l, 1), 0, a * P:a * P + P].rearrange("a t u h d -> (a t) (u h d)"), kv[:, a, :])
                    store(k.s_sb[bass.ds(l, 1)].rearrange("a n t u h d -> (a n t) (u h d)"), kv[0:NS, QB, :])
                    store.wait()

                @block.tensor
                def _(pe):
                    def scores(h):
                        for b in range(QB):
                            u = QB * h + b
                            if u >= 3:
                                pe.wait_ge(split, u - 2)
                            pe.matmul(p_z[:, u % 3, 0:NP - P * b], ft[:, 4 + h, P * b:P * b + P], ft[:, h, P * b:NP], start=True, stop=True).then_inc(scored, 1)

                    def after(h):
                        for b in range(QB):
                            u = QB * h + b
                            if b == 0:
                                pe.wait_ge(logged, QB * (h + 1))
                            if u >= 2:
                                pe.wait_ge(summed_up, u - 1)
                            out = p_after[:, u % 2, :]
                            last = pe.matmul(out[:, 0:NP - P * b], k.c("later"), blk(miss, h, b), start=True, stop=(b == QB - 1))
                            for c in range(b + 1, QB):
                                last = pe.matmul(out[:, P * (c - b):NP - P * b], k.c("ones"), blk(miss, h, c), start=False, stop=(c == QB - 1))
                            last.then_inc(weighted, 1)

                    def apply(h):
                        if h >= 2:
                            pe.wait_ge(kept, h - 1)
                        pe.wait_ge(exped, QB * (h + 1))
                        pe.wait_ge(own, h + 1)
                        for b in range(QB):
                            last = pe.matmul(p_out[:, h % 2, P * b:NP], kv[:, b, 512 + P * h:640 + P * h], blk(logs, h, b), start=(b == 0), stop=(b == QB - 1))
                        last.then_inc(applied, 1)

                    for h in range(4):
                        scores(h)
                        after(h)
                        if h >= 1:
                            apply(h - 1)
                    apply(3)

                @block.scalar
                def _(act):
                    def shrink(u):
                        h, b = units[u]
                        m = mag[:, u % 2, 0:NP - P * b]
                        act.wait_ge(split, u + 1)
                        act.activation(m, m, ACT.Exp, scale=-1.0).then_inc(shrunk, 1)
                        act.wait_ge(shrunk, 2 * u + 1)
                        act.activation(m, m, ACT.Ln, bias=1.0).then_inc(shrunk, 1)

                    def weights(u):
                        h, b = units[u]
                        w = blk(logs, h, b)
                        act.wait_ge(summed_up, u + 1)
                        act.activation(w, w, ACT.Exp).then_inc(exped, 1)

                    for h in range(4):
                        for b in range(QB):
                            shrink(QB * h + b)
                        for b in range(QB):
                            weights(QB * h + b)
                        if h >= 1:
                            act.wait_ge(applied, h)
                            act.copy(k.mixT[:, 4 + h - 1, 0:NP], p_out[:, (h - 1) % 2, :]).then_inc(kept, 1)
                    act.wait_ge(applied, 4)
                    act.copy(k.mixT[:, 7, 0:NP], p_out[:, 1, :]).then_inc(kept, 1)

                @block.gpsimd
                def _(pool):
                    for h in range(4):
                        pool.wait_ge(exped, QB * (h + 1))
                        for b in range(QB):
                            w = blk(logs, h, b, 0, P)
                            last = pool.tensor_tensor(w, w, k.c("before"), ALU.mult)
                        last.then_inc(own, 1)

                @block.vector
                def _(dve):
                    steps = Steps(dve, stepped)
                    for h in range(4):
                        for b in range(QB + 1):
                            if b < QB:
                                u, n = QB * h + b, NP - P * b
                                z = p_z[:, u % 3, 0:n]
                                if b == 0 and h >= 2:
                                    dve.wait_ge(applied, h - 1)
                                dve.wait_ge(scored, u + 1)
                                steps.then(dve.tensor_scalar(low[:, u % 2, 0:n], z, SB_SCALE, None, ALU.mult))
                                dve.scalar_tensor_tensor(mag[:, u % 2, 0:n], low[:, u % 2, 0:n], -1.0, low[:, u % 2, 0:n], ALU.mult, ALU.max).then_inc(split, 1)
                            if b >= 1:
                                u, n = QB * h + b - 1, NP - P * (b - 1)
                                x, g = blk(logs, h, b - 1), blk(miss, h, b - 1)
                                dve.wait_ge(shrunk, 2 * u + 2)
                                steps.then(dve.scalar_tensor_tensor(x, low[:, u % 2, 0:n], 0.0, mag[:, u % 2, 0:n], ALU.min, ALU.subtract))
                                steps.then(dve.tensor_tensor(g, x, low[:, u % 2, 0:n], ALU.subtract))
                                dve.tensor_tensor(g[:, 0:P], g[:, 0:P], k.c("before"), ALU.mult).then_inc(logged, 1)
                        for b in range(QB):
                            u, n = QB * h + b, NP - P * b
                            x = blk(logs, h, b)
                            dve.wait_ge(weighted, u + 1)
                            dve.tensor_tensor(x, x, p_after[:, u % 2, 0:n], ALU.add).then_inc(summed_up, 1)
        stick_samples(nc, k, l, kv)
    gate(nc, k, 4, 12)


def stick_samples(nc, k, l, kv):
    ft = k.ft
    COLS = 4 * NS
    cache = k.cache_sb_kv.rearrange("l n t u h d -> (l n) t u (h d)")
    with ExitStack() as ctx:
        sb, ps = scope(nc, ctx)
        pages = sb("sbs_pages", [P, 2, PAGES, 512])
        keys = sb("sbs_keys", [P, 3, 4, P])
        low = sb("sbs_low", [P, 5, COLS])
        mag = sb("sbs_mag", [P, 5, COLS])
        logs = sb("sbs_logs", [P, 5, COLS])
        miss = sb("sbs_miss", [P, 5, COLS])
        p_keys = ps("sbs_p_keys", [P, 3, 512])
        p_z = ps("sbs_p_z", [P, 2, 512])
        p_after = ps("sbs_p_after", [P, 2, 512])
        p_out = ps("sbs_p_out", [P, 512])
        loaded, turned, copied_s, copied_v, scored = k.signals[0:2], *k.signals[2:6]

        def load_pages(sp, which, used, each):
            loads = [Loads(sp, s) for s in loaded]
            for s in range(NB):
                if s >= 2:
                    sp.wait_ge(used, each * (s - 1))
                for p in range(PAGES):
                    page = sp.value_load(k.pages[0:1, PAGES * s + p:PAGES * s + p + 1], min_val=0, max_val=POOL - 1)
                    loads[s % 2](pages[:, s % 2, p, :], cache[bass.ds(l * POOL + page, 1), :, which].rearrange("a t x -> (a t) x"))

        with stage(nc, k.signals) as block:
            @block.sync
            def _(sp):
                load_pages(sp, 0, turned, PAGES)

            @block.tensor
            def _(pe):
                units = [(s, p) for s in range(NB) for p in range(PAGES)]
                for h in range(4):
                    pe.matmul(p_z[0:NS, 1, NS * h:NS * h + NS], ft[:, 4 + h, NP:NT], ft[:, h, NP:NT], start=True, stop=True)
                for u in range(len(units) + 1):
                    if u < len(units):
                        s, p = units[u]
                        if p == 0:
                            pe.wait_ge(loaded[s % 2], 16 * PAGES * (s // 2 + 1))
                        if u >= 3:
                            before = u - 3
                            pe.wait_ge(copied_v if before % 2 == 0 else copied_s, before // 2 + 1)
                        for h in range(4):
                            last = pe.transpose(p_keys[:, u % 3, P * h:P * h + P], pages[:, s % 2, p, P * h:P * h + P], k.c("ident"))
                        last.then_inc(turned, 1)
                    if u >= 1:
                        b = u - 1
                        s, p = units[b]
                        pe.wait_ge(copied_v if b % 2 == 0 else copied_s, b // 2 + 1)
                        for h in range(4):
                            col = COLS * p + NS * h + DS * s
                            last = pe.matmul(p_z[:, 0, col:col + DS], keys[:, b % 3, h, :], ft[:, h, NP + DS * s:NP + DS * s + DS], start=True, stop=True)
                        last.then_inc(scored, 1)

            def copies(engine, copy, copied, odd):
                for u in range(odd, NB * PAGES, 2):
                    engine.wait_ge(turned, u + 1)
                    if u >= 3:
                        engine.wait_ge(scored, u - 2)
                    copy(keys[:, u % 3, :, :], p_keys[:, u % 3, :].rearrange("p (h t) -> p h t", h=4)).then_inc(copied, 1)

            @block.vector
            def _(dve):
                copies(dve, dve.tensor_copy, copied_v, 0)

            @block.scalar
            def _(act):
                copies(act, act.copy, copied_s, 1)

        scaled, shrunk, missed, summed, weighted, done = k.signals[:6]
        paged = lambda t: t[:, 0:4, :]
        new = lambda t: t[0:NS, 4, :]
        z = (p_z[:, 0, :].rearrange("p (g c) -> p g c", g=4), p_z[0:NS, 1, 0:COLS])
        both = (paged, new)
        with stage(nc, k.signals) as block:
            @block.vector
            def _(dve):
                step = Steps(dve, done)
                for i, part in enumerate(both):
                    step.then(dve.tensor_scalar(part(low), z[i], SB_SCALE, None, ALU.mult))
                    dve.scalar_tensor_tensor(part(mag), part(low), -1.0, part(low), ALU.mult, ALU.max).then_inc(scaled, 1)
                for i, part in enumerate(both):
                    dve.wait_ge(shrunk, 2 * i + 2)
                    step.then(dve.scalar_tensor_tensor(part(logs), part(low), 0.0, part(mag), ALU.min, ALU.subtract))
                    last = dve.tensor_tensor(part(miss), part(logs), part(low), ALU.subtract)
                    if i == 0:
                        last.then_inc(missed, 1)
                    else:
                        step.then(last)
                m = k.c("before_s")[0:NS].unsqueeze(1).to_broadcast([NS, 4, NS])
                g = new(miss).rearrange("p (h q) -> p h q", h=4)
                dve.tensor_tensor(g, g, m, ALU.mult).then_inc(missed, 1)
                dve.wait_ge(summed, 1)
                dve.tensor_tensor(paged(logs), paged(logs), p_after[:, 0, :].rearrange("p (g c) -> p g c", g=4), ALU.add).then_inc(weighted, 1)
                dve.tensor_tensor(new(logs), new(logs), p_after[0:NS, 1, 0:COLS], ALU.add).then_inc(weighted, 1)
                dve.wait_ge(shrunk, 6)
                g = new(logs).rearrange("p (h q) -> p h q", h=4)
                dve.tensor_tensor(g, g, m, ALU.mult)

            @block.scalar
            def _(act):
                for i, part in enumerate(both):
                    act.wait_ge(scaled, i + 1)
                    act.activation(part(mag), part(mag), ACT.Exp, scale=-1.0).then_inc(shrunk, 1)
                    act.wait_ge(shrunk, 2 * i + 1)
                    act.activation(part(mag), part(mag), ACT.Ln, bias=1.0).then_inc(shrunk, 1)
                for i, part in enumerate(both):
                    act.wait_ge(weighted, i + 1)
                    act.activation(part(logs), part(logs), ACT.Exp).then_inc(shrunk, 1)

            @block.tensor
            def _(pe):
                pe.wait_ge(missed, 2)
                for p in range(PAGES):
                    out = p_after[:, 0, COLS * p:COLS * p + COLS]
                    pe.matmul(out, k.c("later"), miss[:, p, :], start=True, stop=False)
                    for q in range(p + 1, PAGES):
                        pe.matmul(out, k.c("ones"), miss[:, q, :], start=False, stop=False)
                    pe.matmul(out, k.c("ones")[0:NS], new(miss), start=False, stop=True)
                pe.matmul(p_after[0:NS, 1, 0:COLS], k.c("later")[0:NS, 0:NS], new(miss), start=True, stop=True).then_inc(summed, 1)

        applied, kept = k.signals[2:4]
        with stage(nc, k.signals) as block:
            @block.sync
            def _(sp):
                load_pages(sp, 1, applied, 1)

            @block.tensor
            def _(pe):
                for h in range(4):
                    pe.matmul(p_out[:, NS * h:NS * h + NS], kv[0:NS, QB, 512 + P * h:640 + P * h], new(logs)[:, NS * h:NS * h + NS],
                              start=(h == 0), stop=False, skip_group_check=True)
                for s in range(NB):
                    pe.wait_ge(loaded[s % 2], 16 * PAGES * (s // 2 + 1))
                    for p in range(PAGES):
                        for h in range(4):
                            col = slice(NS * h + DS * s, NS * h + DS * s + DS)
                            last = pe.matmul(p_out[:, col], pages[:, s % 2, p, P * h:P * h + P], logs[:, p, col], start=False, stop=(p == PAGES - 1), skip_group_check=True)
                    last.then_inc(applied, 1)

            @block.scalar
            def _(act):
                act.wait_ge(applied, NB)
                act.copy(k.mixT[:, 4:8, NP:NT], p_out[:, 0:COLS].rearrange("p (h t) -> p h t", h=4))


def take_top(dve, step, rounds, top, score, work):
    for r in range(rounds):
        src = score if r == 0 else work
        step.then(dve.max(top, src))
        step.then(dve.match_replace(work, top, src, NEG))


def sparse_attention(nc, k, l):
    ft = k.ft
    with ExitStack() as ctx:
        sb, ps = scope(nc, ctx)
        tm = sb("dsa_tm", [P, TT, DSA_W + 8])
        ikz = sb("dsa_ikz", [P, 2, NP])
        jobs = []
        for a in range(TT):
            n, cols = tokens(a)
            jobs.append(([ft[:, 4, cols], ft[:, 5, cols]], [(lambda b, n=n: b[0:n, 0:256], tm[0:n, a, 0:256])]))
            jobs.append(([ft[0:64, 6, cols], ft[0:8, 11, cols]], [(lambda b, n=n: b[0:n, 0:72], tm[0:n, a, 256:328])]))
        turn(nc, k, "dsa_in", jobs)

        stored, cleared, weighed = k.signals[:3]
        with stage(nc, k.signals) as block:
            @block.sync
            def _(sp):
                store = Loads(sp, stored)
                store(k.p_dsa[bass.ds(l, 1), 0].rearrange("a (n p) w -> p (a n) w", p=P), tm[:, 0:QB, 0:DSA_W])
                store(k.s_dsa[bass.ds(l, 1)].rearrange("a n t w -> (a n t) w"), tm[0:NS, QB, 0:DSA_W])
                store.wait()

            @block.gpsimd
            def _(pool):
                pool.memset(ikz[64:128, 0, :], 0.0)
                pool.memset(ikz[0:64, 1, :], 0.0)

            @block.vector
            def _(dve):
                for r in range(2):
                    dve.tensor_copy(ikz[64 * r:64 * r + 64, r, :], ft[64 * r:64 * r + 64, 6, 0:NP])
                dve.tensor_scalar(tm[:, 0:QB, 320:328], tm[:, 0:QB, 320:328], 8 ** -0.5, None, ALU.mult)
                dve.tensor_scalar(tm[0:NS, QB, 320:328], tm[0:NS, QB, 320:328], 8 ** -0.5, None, ALU.mult)

        sparse_prompt(nc, k, tm, ikz)
        sparse_samples(nc, k, l, tm)
    gate(nc, k, 8, 12)


def sparse_prompt(nc, k, tm, ikz):
    ft = k.ft
    with ExitStack() as ctx:
        sb, ps = scope(nc, ctx)
        rel = sb("dsa_rel", [P, 2, 512])
        score = sb("dsa_score", [P, 512])
        work = sb("dsa_work", [P, 512])
        top = sb("dsa_top", [P, 8])
        neg = sb("dsa_neg_row", [P, 2, 512])
        prob = sb("dsa_prob", [P, 2, 512])
        probT = sb("dsa_probT", [P, 2, 512])
        small = sb("dsa_small", [P, 2, 4])
        p_rel = ps("dsa_p_rel", [P, 2, 512])
        p_log = ps("dsa_p_log", [P, 2, 512])
        p_T = ps("dsa_p_T", [P, 2, 512])
        p_out = ps("dsa_p_out", [P, 2, 512])
        multiplied, rectified, added, looked, biased, exped, normed, turned, copied, applied, kept, own = k.signals[:12]
        with stage(nc, k.signals) as block:
            @block.tensor
            def _(pe):
                def index(q):
                    for h in range(8):
                        u = 8 * q + h
                        if u >= 2:
                            pe.wait_ge(rectified, u - 1)
                        pe.matmul(p_rel[:, u % 2, 0:P * (q + 1)], ft[:, 7 + h // 2, P * q:P * q + P], ikz[:, h % 2, 0:P * (q + 1)],
                                  start=True, stop=True).then_inc(multiplied, 1)

                for q in range(QB):
                    index(q)
                    for h in range(5):
                        u = 4 * q + h
                        if h < 4:
                            if u >= 2:
                                pe.wait_ge(biased, u - 1)
                            pe.matmul(p_log[:, u % 2, 0:P * (q + 1)], ft[:, h, P * q:P * q + P], ft[:, 4, 0:P * (q + 1)],
                                      start=True, stop=True).then_inc(looked, 1)
                        if h >= 1:
                            v = u - 1
                            pe.wait_ge(normed, v + 1)
                            if v >= 2:
                                pe.wait_ge(copied, v - 1)
                            for b in range(q + 1):
                                last = pe.transpose(p_T[:, v % 2, P * b:P * b + P], prob[:, v % 2, P * b:P * b + P], k.c("ident"))
                            last.then_inc(turned, 1)
                            pe.wait_ge(copied, v + 1)
                            if v >= 2:
                                pe.wait_ge(kept, v - 1)
                            for b in range(q + 1):
                                last = pe.matmul(p_out[:, v % 2, 0:P], tm[:, b, P:2 * P], probT[:, v % 2, P * b:P * b + P], start=(b == 0), stop=(b == q))
                            last.then_inc(applied, 1)

            @block.scalar
            def _(act):
                def rectify(q):
                    for h in range(8):
                        u = 8 * q + h
                        act.wait_ge(multiplied, u + 1)
                        if u >= 2:
                            act.wait_ge(added, u - 1)
                        act.activation(rel[:, u % 2, 0:P * (q + 1)], p_rel[:, u % 2, 0:P * (q + 1)], ACT.Relu, scale=0.125).then_inc(rectified, 1)

                for q in range(QB):
                    w = P * (q + 1)
                    rectify(q)
                    for h in range(5):
                        u = 4 * q + h
                        if h < 4:
                            act.wait_ge(biased, u + 1)
                            act.activation(prob[:, u % 2, 0:w], prob[:, u % 2, 0:w], ACT.Exp, bias=small[:, u % 2, 0:1],
                                           accum_out=small[:, u % 2, 1:2]).then_inc(exped, 1)
                        if h >= 1:
                            v = u - 1
                            act.wait_ge(turned, v + 1)
                            if v >= 2:
                                act.wait_ge(applied, v - 1)
                            act.copy(probT[:, v % 2, 0:w], p_T[:, v % 2, 0:w]).then_inc(copied, 1)
                            act.wait_ge(applied, v + 1)
                            act.copy(k.mixT[:, 8 + h - 1, P * q:P * q + P], p_out[:, v % 2, 0:P]).then_inc(kept, 1)

            @block.vector
            def _(dve):
                step = Steps(dve, own)
                for q in range(QB):
                    w = P * (q + 1)
                    s = score[:, 0:w]
                    for h in range(8):
                        u = 8 * q + h
                        dve.wait_ge(rectified, u + 1)
                        g = tm[:, q, 320 + h:321 + h]
                        if h == 0:
                            last = dve.tensor_scalar(s, rel[:, u % 2, 0:w], g, None, ALU.mult)
                        else:
                            last = dve.scalar_tensor_tensor(s, rel[:, u % 2, 0:w], g, s, ALU.mult, ALU.add)
                        last.then_inc(added, 1)
                        dve.wait_ge(added, u + 1)
                    d = score[:, P * q:w]
                    n = neg[:, q % 2, 0:w]
                    if q == 0:
                        step.then(dve.tensor_copy(n, k.c("dsa_neg")))
                    else:
                        step.then(dve.tensor_tensor(d, d, k.c("dsa_neg"), ALU.add))
                        take_top(dve, step, TOPK // 8, top[:, :], s, work[:, 0:w])
                        step.then(dve.tensor_tensor(n, work[:, 0:w], s, ALU.is_equal))
                        step.then(dve.tensor_scalar(n, n, NEG, None, ALU.mult))
                    for h in range(5):
                        u = 4 * q + h
                        if h < 4:
                            p, m = prob[:, u % 2, 0:w], small[:, u % 2, 0:1]
                            dve.wait_ge(looked, u + 1)
                            if u >= 2:
                                dve.wait_ge(turned, u - 1)
                            step.then(dve.scalar_tensor_tensor(p, p_log[:, u % 2, 0:w], SB_SCALE, n, ALU.mult, ALU.add))
                            dve.tensor_reduce(m, p, AX.X, ALU.max, negate=True).then_inc(biased, 1)
                        if h >= 1:
                            v = u - 1
                            dve.wait_ge(exped, v + 1)
                            step.then(dve.reciprocal(small[:, v % 2, 2:3], small[:, v % 2, 1:2]))
                            dve.tensor_scalar(prob[:, v % 2, 0:w], prob[:, v % 2, 0:w], small[:, v % 2, 2:3], None, ALU.mult).then_inc(normed, 1)


def sparse_samples(nc, k, l, tm):
    ft = k.ft
    WIDE = PAST + NS
    cache = k.cache_dsa.rearrange("l n t w -> (l n) t w")
    with ExitStack() as ctx:
        sb, ps = scope(nc, ctx)
        iq = sb("dss_iq", [P, NB, 2, 4, DS])
        qs = sb("dss_q", [P, NB, 4, NS])
        wv = sb("dss_wv", [NS, NB])
        wx = sb("dss_wx", [NS, NB, P])
        stored, loaded, own, zeroed = k.signals[:4]
        with stage(nc, k.signals) as block:
            @block.sync
            def _(sp):
                sp.dma_start(k.sample_w, tm[0:NS, QB, 320:328]).then_inc(stored, 16)
                sp.wait_ge(stored, 16)
                load = Loads(sp, loaded)
                for r in range(2):
                    for j in range(4):
                        load(wv[16 * r + 4 * j:16 * r + 4 * j + 4, :], k.sample_w.rearrange("(s t) h -> h t s", t=DS)[2 * j + r])

            @block.gpsimd
            def _(pool):
                pool.memset(iq[:, :, :, :, :], 0.0)
                pool.memset(qs[:, :, :, :], 0.0).then_inc(zeroed, 1)

            @block.vector
            def _(dve):
                dve.wait_ge(zeroed, 1)
                for s in range(NB):
                    tok = slice(NP + DS * s, NP + DS * s + DS)
                    for r in range(2):
                        dve.tensor_copy(iq[64 * r:64 * r + 64, s, r, :, :], ft[64 * r:64 * r + 64, 7:11, tok])
                    dve.tensor_copy(qs[:, s, :, DS * s:DS * s + DS], ft[:, 0:4, tok])
                dve.wait_ge(loaded, 16 * 8)
                dve.tensor_tensor(wx[:, :, :], k.c("spread")[0:NS].rearrange("p (s c) -> p s c", s=NB),
                                  wv[:, :].unsqueeze(2).to_broadcast([NS, NB, P]), ALU.mult)

        with ExitStack() as inner:
            sb2, ps2 = scope(nc, inner)
            score = sb2("dss_score", [P, WIDE])
            logit = sb2("dss_logit", [P, WIDE])
            with ExitStack() as first:
                sb3, ps3 = scope(nc, first)
                pages = sb3("dss_pages", [P, 2, PAGES, DSA_W + 64])
                keys = sb3("dss_keys", [P, 2, PAST])
                ikeys = sb3("dss_ikeys", [P, 2, PAST])
                rel = sb3("dss_rel", [NS, 2, WIDE])
                p_keys, p_ikeys, p_rel, p_reln, p_score, p_scoren, p_log = (ps3(f"dss_p{i}", [P, 512]) for i in range(7))
                loaded0, loaded1, turned, copied_v, copied_s, related, rectified, summed, looked, out = k.signals[:10]
                with stage(nc, k.signals) as block:
                    @block.sync
                    def _(sp):
                        loads = [Loads(sp, loaded0), Loads(sp, loaded1)]
                        for s in range(NB):
                            if s >= 2:
                                sp.wait_ge(turned, s - 1)
                            for p in range(PAGES):
                                page = sp.value_load(k.pages[0:1, PAGES * s + p:PAGES * s + p + 1], min_val=0, max_val=POOL - 1)
                                row = cache[bass.ds(l * POOL + page, 1)].rearrange("a t w -> (a t) w")
                                loads[s % 2](pages[:, s % 2, p, 0:DSA_W], row)
                                loads[s % 2](pages[:, s % 2, p, DSA_W:DSA_W + 64], row[:, 256:DSA_W])

                    @block.tensor
                    def _(pe):
                        for s in range(NB):
                            pe.wait_ge((loaded0, loaded1)[s % 2], 16 * 2 * PAGES * (s // 2 + 1))
                            if s >= 1:
                                pe.wait_ge(copied_v, s)
                                pe.wait_ge(copied_s, s)
                            for p in range(PAGES):
                                pe.transpose(p_keys[:, P * p:P * p + P], pages[:, s % 2, p, 0:P], k.c("ident"))
                                last = pe.transpose(p_ikeys[:, P * p:P * p + P], pages[:, s % 2, p, 256:384], k.c("ident"))
                            last.then_inc(turned, 1)
                            pe.wait_ge(copied_v, s + 1)
                            pe.wait_ge(copied_s, s + 1)
                            if s >= 1:
                                pe.wait_ge(rectified, 2 * s)
                            mine = iq[:, s].rearrange("p r j t -> p (r j t)")
                            pe.matmul(p_rel[0:NS, :], mine, ikeys[:, s % 2, :], start=True, stop=True)
                            pe.matmul(p_reln[0:NS, 0:NS], mine, ft[:, 6, NP:NT], start=True, stop=True).then_inc(related, 1)
                            pe.matmul(p_log[:, :], qs[:, s].rearrange("p h c -> p (h c)"), keys[:, s % 2, :], start=(s == 0), stop=(s == NB - 1)).then_inc(looked, 1)
                            pe.wait_ge(rectified, 2 * s + 2)
                            pe.matmul(p_score[:, :], wx[:, s, :], rel[:, s % 2, 0:PAST], start=(s == 0), stop=(s == NB - 1))
                            pe.matmul(p_scoren[:, 0:NS], wx[:, s, :], rel[:, s % 2, PAST:WIDE], start=(s == 0), stop=(s == NB - 1)).then_inc(summed, 1)
                        for s in range(NB):
                            last = pe.matmul(p_reln[:, 0:NS], qs[:, s].rearrange("p h c -> p (h c)"), ft[:, 4, NP:NT], start=(s == 0), stop=(s == NB - 1))
                        last.then_inc(summed, 1)

                    @block.vector
                    def _(dve):
                        for s in range(NB):
                            dve.wait_ge(turned, s + 1)
                            if s >= 2:
                                dve.wait_ge(looked, s - 1)
                            dve.tensor_copy(keys[:, s % 2, :], p_keys[:, :]).then_inc(copied_v, 1)
                        dve.wait_ge(summed, NB + 1)
                        dve.tensor_copy(score[:, 0:PAST], p_score[:, :])
                        dve.tensor_tensor(score[:, PAST:WIDE], p_scoren[:, 0:NS], k.c("dsa_neg_s"), ALU.add)
                        dve.tensor_scalar(logit[:, PAST:WIDE], p_reln[:, 0:NS], SB_SCALE, None, ALU.mult)

                    @block.scalar
                    def _(act):
                        for s in range(NB):
                            act.wait_ge(turned, s + 1)
                            if s >= 2:
                                act.wait_ge(related, s - 1)
                            act.copy(ikeys[:, s % 2, :], p_ikeys[:, :]).then_inc(copied_s, 1)
                            act.wait_ge(related, s + 1)
                            if s >= 2:
                                act.wait_ge(summed, s - 1)
                            act.activation(rel[:, s % 2, 0:PAST], p_rel[0:NS, :], ACT.Relu, scale=0.125).then_inc(rectified, 1)
                            act.activation(rel[:, s % 2, PAST:WIDE], p_reln[0:NS, 0:NS], ACT.Relu, scale=0.125).then_inc(rectified, 1)
                        act.wait_ge(looked, NB)
                        act.activation(logit[:, 0:PAST], p_log[:, :], ACT.Copy, scale=SB_SCALE)

            PAD = 7
            work = sb2("dss_work", [P, WIDE + PAD])
            top = sb2("dss_top", [P, 2, 8])
            small = sb2("dss_small", [P, 4])
            probT = sb2("dss_probT", [P, 5, P])
            vals = sb2("dss_vals", [P, 2, PAGES, P])
            p_T = ps2("dss_p_T", [P, 512])
            p_Tn = ps2("dss_p_Tn", [P, 512])
            p_out = ps2("dss_p_out", [P, 512])
            own, biased, exped, normed, turned, copied, loaded0, loaded1, applied = k.signals[:9]
            with stage(nc, k.signals) as block:
                @block.sync
                def _(sp):
                    loads = [Loads(sp, loaded0), Loads(sp, loaded1)]
                    for s in range(NB):
                        if s >= 2:
                            sp.wait_ge(applied, s - 1)
                        for p in range(PAGES):
                            page = sp.value_load(k.pages[0:1, PAGES * s + p:PAGES * s + p + 1], min_val=0, max_val=POOL - 1)
                            loads[s % 2](vals[:, s % 2, p, :], cache[bass.ds(l * POOL + page, 1)].rearrange("a t w -> (a t) w")[:, P:2 * P])

                @block.vector
                def _(dve):
                    step = Steps(dve, own)
                    take_top(dve, step, TOPK_S // 8, top[:, 0, :], score[:, :], work[:, 0:WIDE])
                    step.then(dve.max(top[:, 0, :], work[:, 0:WIDE]))
                    dve.memset(top[:, 1, 0:PAD], -NEG)
                    step(dve.memset(work[:, WIDE:WIDE + PAD], -NEG))
                    step.then(dve.tensor_copy(top[:, 1, PAD:8], top[:, 0, 0:1]))
                    step.then(dve.match_replace(work[:, :], top[:, 1, :], work[:, :], NEG))
                    step.then(dve.tensor_tensor(work[:, 0:WIDE], work[:, 0:WIDE], score[:, :], ALU.is_equal))
                    step.then(dve.scalar_tensor_tensor(logit[:, :], work[:, 0:WIDE], NEG, logit[:, :], ALU.mult, ALU.add))
                    dve.tensor_reduce(small[:, 0:1], logit[:, :], AX.X, ALU.max, negate=True).then_inc(biased, 1)
                    dve.wait_ge(exped, 1)
                    step.then(dve.reciprocal(small[:, 2:3], small[:, 1:2]))
                    dve.tensor_scalar(logit[:, :], logit[:, :], small[:, 2:3], None, ALU.mult).then_inc(normed, 1)
                    dve.wait_ge(turned, 1)
                    dve.tensor_copy(probT[:, 0:4, :], p_T[:, :].rearrange("p (g c) -> p g c", g=4)).then_inc(copied, 1)
                    dve.tensor_copy(probT[0:NS, 4, :], p_Tn[0:NS, 0:P]).then_inc(copied, 1)

                @block.scalar
                def _(act):
                    act.wait_ge(biased, 1)
                    act.activation(logit[:, :], logit[:, :], ACT.Exp, bias=small[:, 0:1], accum_out=small[:, 1:2]).then_inc(exped, 1)
                    act.wait_ge(applied, NB)
                    act.copy(k.mixT[:, 8:12, NP:NT], p_out[:, 0:P].rearrange("p (h t) -> p h t", h=4))

                @block.tensor
                def _(pe):
                    pe.wait_ge(normed, 1)
                    for g in range(4):
                        pe.transpose(p_T[:, P * g:P * g + P], logit[:, P * g:P * g + P], k.c("ident"))
                    pe.transpose(p_Tn[0:NS, 0:P], logit[:, PAST:WIDE], k.c("ident")).then_inc(turned, 1)
                    pe.wait_ge(copied, 2)
                    pe.matmul(p_out[:, 0:P], tm[0:NS, QB, P:2 * P], probT[0:NS, 4, :], start=True, stop=False, skip_group_check=True)
                    for s in range(NB):
                        pe.wait_ge((loaded0, loaded1)[s % 2], 16 * PAGES * (s // 2 + 1))
                        for p in range(PAGES):
                            def mine(t):
                                return t.rearrange("p (h c) -> p h c", h=4)[:, :, DS * s:DS * s + DS]
                            last = pe.matmul(mine(p_out[:, 0:P]), vals[:, s % 2, p, :], mine(probT[:, p, :]), start=False, stop=(p == PAGES - 1), skip_group_check=True)
                        last.then_inc(applied, 1)


R_SLOT, WL_SLOT, K_SLOT, V_SLOT, AL_SLOT, RG_SLOT = 0, 4, 5, 9, 13, 14
SHIFT_RUNS = ((0, 4, P, 0), (4, 1, LORA, 512), (5, 4, P, 608), (9, 4, P, 1120), (13, 1, LORA, 1632))
KK_SCALE = 2.0 ** 20


def rwkv(nc, k, l):
    with ExitStack() as ctx:
        sb, _ = scope(nc, ctx)
        k.bonus = sb("rw_bonus", [P, 4, NT])
        k.kr = sb("rw_kr", [P, 4, NC, 2, C])
        k.bk = sb("rw_bk", [P, 4, NC, 2, C])
        k.ends = sb("rw_ends", [P, 4, NC])
        k.y_sample_t = sb("rw_ys", [P, 4, NS])
        token_shift(nc, k, l)
        with ExitStack() as inner:
            rwkv_vectors(nc, k, l, inner)
            rwkv_samples(nc, k, l)
        rwkv_chunks(nc, k, l)
        rwkv_out(nc, k)
    gate(nc, k, 12, RG_SLOT)


def token_shift(nc, k, l):
    ft = k.ft
    with ExitStack() as ctx:
        sb, _ = scope(nc, ctx)
        rows = sb("ts_rows", [NB, SHIFT_W])
        last_p = sb("ts_last_p", [1, SHIFT_W])
        last_s = sb("ts_last_s", [NB, SHIFT_W])
        first = sb("ts_first", [P, 14, NB])
        diff = sb("ts_diff", [P, 4, NT])
        loaded, stepped = k.signals[:2]
        with stage(nc, k.signals) as block:
            @block.sync
            def _(sp):
                sp.dma_start(rows[:, :], k.state_shift[bass.ds(l, 1)].rearrange("a n w -> (a n) w")).then_inc(loaded, 16)
                sp.wait_ge(loaded, 16)
        jobs = []
        for slot, count, w, col in SHIFT_RUNS:
            jobs.append(([rows[:, col + w * i:col + w * i + w] for i in range(count)],
                         [(lambda b, w=w, n=count: b[0:w, 0:NB * n].rearrange("p (i s) -> p i s", s=NB), first[0:w, slot:slot + count, :])]))
        width = {s: (LORA if s in (WL_SLOT, AL_SLOT) else P) for s in range(14)}
        at = 0
        for slots in (range(0, 4), range(4, 8), range(8, 12), range(12, 14)):
            w = sum(width[s] for s in slots)
            jobs.append(([ft[0:width[s], s, NP - 1:NP] for s in slots], [(lambda b, w=w: b[0:1, 0:w], last_p[:, at:at + w])]))
            jobs.append(([ft[0:width[s], s, NP + DS - 1:NT:DS] for s in slots], [(lambda b, w=w: b[0:NB, 0:w], last_s[:, at:at + w])]))
            at += w
        turn(nc, k, "ts", jobs)
        with stage(nc, k.signals) as block:
            @block.sync
            def _(sp):
                store = Loads(sp, loaded)
                store(k.p_shift[bass.ds(l, 1)].rearrange("a n w -> (a n) w"), last_p[:, :])
                store(k.s_shift[bass.ds(l, 1)].rearrange("a n w -> (a n) w"), last_s[:, :])
                store.wait()

            @block.vector
            def _(dve):
                step = Steps(dve, stepped)
                for slot, n, w, col in SHIFT_RUNS:
                    x, d = ft[0:w, slot:slot + n, :], diff[0:w, 0:n, :]
                    seqs = lambda t, i: t[:, i, NP:NT].rearrange("p (s t) -> p s t", t=DS)
                    dve.tensor_tensor(d[:, :, 1:NP], x[:, :, 0:NP - 1], x[:, :, 1:NP], ALU.subtract)
                    dve.tensor_scalar(d[:, :, 0:1], x[:, :, 0:1], -1.0, None, ALU.mult)
                    for i in range(n):
                        dve.tensor_tensor(seqs(d, i)[:, :, 1:DS], seqs(x, i)[:, :, 0:DS - 1], seqs(x, i)[:, :, 1:DS], ALU.subtract)
                        last = dve.tensor_tensor(seqs(d, i)[:, :, 0], first[0:w, slot + i, :], seqs(x, i)[:, :, 0], ALU.subtract)
                    step.then(last)
                    for i in range(n):
                        last = dve.scalar_tensor_tensor(x[:, i, :], d[:, i, :], k.prm[0:w, ROW_MU + slot + i:ROW_MU + slot + i + 1], x[:, i, :], ALU.mult, ALU.add)
                    step.then(last)


def rwkv_vectors(nc, k, l, outer):
    ft = k.ft
    sb, _ = scope(nc, outer)
    logw = sb("rv_logw", [P, 4, NT])
    beta = sb("rv_beta", [P, 4, NT])
    kap = sb("rv_kap", [P, 4, NT])
    lora = sb("rv_lora", [LORA, 2, GW])
    minus = sb("rv_minus", [P, 8])
    with ExitStack() as ctx:
        sb2, ps = scope(nc, ctx)
        tmp = sb2("rv_tmp", [P, 2, NT])
        prod = ps("rv_prod", [P, 2, 2, 512])
        loaded, negated, doubled, stepped, opened, multiplied, halved = k.signals[:7]
        th = ft[0:LORA, WL_SLOT, :]
        with stage(nc, k.signals) as block:
            @block.sync
            def _(sp):
                load = Loads(sp, loaded)
                load(lora[:, 0, :], k.rw_w2[bass.ds(l, 1)].rearrange("a r c -> (a r) c"))
                load(lora[:, 1, :], k.rw_a2[bass.ds(l, 1)].rearrange("a r c -> (a r) c"))

            @block.scalar
            def _(act):
                act.activation(th, th, ACT.Exp, scale=2.0).then_inc(doubled, 1)
                act.wait_ge(negated, 2)
                for u in range(8):
                    act.wait_ge(multiplied, u + 1)
                    out, i = (logw, beta)[u % 2], u // 2
                    bias = minus[:, 4 * (u % 2) + i:4 * (u % 2) + i + 1]
                    act.activation(out[:, i, 0:NP], prod[:, u % 2, 0, :], ACT.Exp, scale=-1.0, bias=bias).then_inc(opened, 1)
                    act.activation(out[:, i, NP:NT], prod[:, u % 2, 1, 0:NS], ACT.Exp, scale=-1.0, bias=bias).then_inc(opened, 1)

            @block.tensor
            def _(pe):
                pe.wait_ge(loaded, 32)
                pe.wait_ge(halved, 1)
                for u in range(8):
                    if u >= 2:
                        pe.wait_ge(opened, 2 * (u - 1))
                    x = ft[0:LORA, (WL_SLOT, AL_SLOT)[u % 2], :]
                    w = lora[:, u % 2, P * (u // 2):P * (u // 2) + P]
                    pe.matmul(prod[:, u % 2, 0, :], w, x[:, 0:NP], start=True, stop=True)
                    pe.matmul(prod[:, u % 2, 1, 0:NS], w, x[:, NP:NT], start=True, stop=True).then_inc(multiplied, 1)

            @block.vector
            def _(dve):
                step = Steps(dve, stepped)
                dve.tensor_scalar(minus[:, 0:4], k.prm[:, ROW_W0:ROW_W0 + 4], -1.0, None, ALU.mult).then_inc(negated, 1)
                dve.tensor_scalar(minus[:, 4:8], k.prm[:, ROW_A0:ROW_A0 + 4], -1.0, None, ALU.mult).then_inc(negated, 1)
                dve.wait_ge(doubled, 1)
                step.then(dve.tensor_scalar(th, th, 1.0, None, ALU.add))
                step.then(dve.reciprocal(th, th))
                dve.tensor_scalar(th, th, -2.0, 1.0, ALU.mult, ALU.add).then_inc(halved, 1)
                for u in range(8):
                    x = (logw, beta)[u % 2][:, u // 2, :]
                    dve.wait_ge(opened, 2 * u + 2)
                    step.then(dve.tensor_scalar(x, x, 1.0, None, ALU.add))
                    step.then(dve.reciprocal(x, x))
                    if u % 2 == 0:
                        step.then(dve.tensor_scalar(x, x, -float(np.exp(-0.5)), None, ALU.mult))

        def col(row, i):
            return k.prm[:, row + i:row + i + 1]

        squared, summed, bounded, inverted, stepped, logged = k.signals[:6]
        with stage(nc, k.signals) as block:
            @block.vector
            def _(dve):
                step = Steps(dve, stepped)
                for i in range(4):
                    kx, t, z = ft[:, K_SLOT + i, :], tmp[:, 0, :], tmp[:, 1, :]
                    step.then(dve.tensor_scalar(kap[:, i, :], kx, col(ROW_KK, i), None, ALU.mult))
                    dve.tensor_tensor(t, kap[:, i, :], kap[:, i, :], ALU.mult).then_inc(squared, 1)
                    step.then(dve.tensor_scalar(z, beta[:, i, :], -1.0, col(ROW_KA, i), ALU.add, ALU.mult))
                    step.then(dve.scalar_tensor_tensor(kx, z, 1.0, kx, ALU.add, ALU.mult))
                    step.then(dve.scalar_tensor_tensor(z, ft[:, R_SLOT + i, :], col(ROW_RK, i), kx, ALU.mult, ALU.mult))
                    dve.wait_ge(summed, 2 * i + 1)
                    for a, b, part in ((0, NP, 0), (NP, NT, 1)):
                        dve.tensor_scalar(t[:, a:b], prod[:, 0, part, 0:b - a], 1e-24, None, ALU.max).then_inc(bounded, 1)
                    dve.wait_ge(inverted, i + 1)
                    step.then(dve.scalar_tensor_tensor(kap[:, i, :], kap[:, i, :], -KK_SCALE ** 0.5, t, ALU.mult, ALU.mult))
                    step.then(dve.scalar_tensor_tensor(beta[:, i, :], kap[:, i, :], -1.0, beta[:, i, :], ALU.mult, ALU.mult))
                    dve.wait_ge(summed, 2 * i + 2)
                    for a, b, part in ((0, NP, 0), (NP, NT, 1)):
                        last = dve.tensor_tensor(k.bonus[:, i, a:b], prod[:, 1, part, 0:b - a], ft[:, V_SLOT + i, a:b], ALU.mult)
                    step.then(last)

            @block.tensor
            def _(pe):
                for i in range(4):
                    for u in range(2):
                        if u == 0:
                            pe.wait_ge(squared, i + 1)
                        else:
                            pe.wait_ge(stepped, 7 * i + 4)
                        pe.matmul(prod[:, u, 0, :], k.c("head_ones"), tmp[:, u, 0:NP], start=True, stop=True)
                        pe.matmul(prod[:, u, 1, 0:NS], k.c("head_ones"), tmp[:, u, NP:NT], start=True, stop=True).then_inc(summed, 1)

            @block.scalar
            def _(act):
                for i in range(4):
                    act.wait_ge(bounded, 2 * i + 2)
                    inverse_root(act, logged, tmp[:, 0, :], scale=KK_SCALE, at=i).then_inc(inverted, 1)

        lam = sb2("rv_lam", [P, 2, NP])
        exps = sb2("rv_exps", [P, 2, 3, NP])
        summed, shifted, exped, used, ended = k.signals[:5]
        with stage(nc, k.signals) as block:
            @block.vector
            def _(dve):
                for i in range(5):
                    if i < 4:
                        w = logw[:, i, 0:NP]
                        if i >= 2:
                            dve.wait_ge(exped, 3 * (i - 1))
                        dve.tensor_tensor_scan(lam[:, i % 2, :], k.c("chunk_in"), w, 0.0, ALU.mult, ALU.add).then_inc(summed, 1)
                        dve.wait_ge(summed, i + 1)
                        dve.tensor_tensor(tmp[:, i % 2, 0:NP], lam[:, i % 2, :], w, ALU.subtract).then_inc(shifted, 1)
                    if i >= 1:
                        j = i - 1
                        up, down, before = (exps[:, j % 2, x, :].rearrange("p (c t) -> p c t", t=C) for x in range(3))
                        tok = lambda t: t[:, 0:NP].rearrange("p (c t) -> p c t", t=C)
                        dve.wait_ge(exped, 3 * j + 3)
                        dve.tensor_tensor(k.kr[:, j, :, 0, :], tok(kap[:, j, :]), before, ALU.mult)
                        dve.tensor_tensor(k.kr[:, j, :, 1, :], tok(ft[:, R_SLOT + j, :]), up, ALU.mult)
                        dve.tensor_tensor(k.bk[:, j, :, 0, :], tok(beta[:, j, :]), down, ALU.mult)
                        dve.tensor_tensor(k.bk[:, j, :, 1, :], tok(ft[:, K_SLOT + j, :]), down, ALU.mult)
                        dve.tensor_copy(k.ends[:, j, :], up[:, :, C - 1]).then_inc(used, 1)

            @block.scalar
            def _(act):
                for i in range(4):
                    if i >= 2:
                        act.wait_ge(used, i - 1)
                    act.wait_ge(summed, i + 1)
                    act.activation(exps[:, i % 2, 0, :], lam[:, i % 2, :], ACT.Exp).then_inc(exped, 1)
                    act.activation(exps[:, i % 2, 1, :], lam[:, i % 2, :], ACT.Exp, scale=-1.0).then_inc(exped, 1)
                    act.wait_ge(shifted, i + 1)
                    act.activation(exps[:, i % 2, 2, :], tmp[:, i % 2, 0:NP], ACT.Exp).then_inc(exped, 1)
                act.activation(logw[:, :, NP:NT], logw[:, :, NP:NT], ACT.Exp).then_inc(ended, 1)
    k.sample_sources = (ft[:, R_SLOT:R_SLOT + 4], logw, ft[:, K_SLOT:K_SLOT + 4], ft[:, V_SLOT:V_SLOT + 4], kap, beta)


def rwkv_samples(nc, k, l):
    HALF = 32
    with ExitStack() as ctx:
        sb, _ = scope(nc, ctx)
        rows = sb("rs_rows", [NS, 6, GW])
        turn(nc, k, "rs", [([t[:, i, NP:NT] for i in range(4)], [(lambda b: b[0:NS, :], rows[:, n, :])])
                           for n, t in enumerate(k.sample_sources)])
        vec = sb("rs_vec", [P, DS, 6, C])
        state = sb("rs_state", [P, HALF, C])
        tmp = sb("rs_tmp", [P, HALF, C])
        outer = sb("rs_outer", [P, HALF, C])
        mine = sb("rs_mine", [P, DS, HALF])
        other = sb("rs_other", [P, DS, HALF])
        sa = sb("rs_sa", [P, HALF])
        y = sb("rs_y", [P, DS, HALF])
        yrow = rows[:, 0, :]
        stored, loaded, stepped, grown, used, out, back = k.signals[:7]
        with stage(nc, k.signals) as block:
            @block.sync
            def _(sp):
                sp.dma_start(k.sample_rows, rows[:, :, :].rearrange("p v c -> p (v c)")).then_inc(stored, 16)
                load = Loads(sp, loaded)
                load(state[:, :, :], k.state_wkv[bass.ds(l, 1)].rearrange("a s h (b i) j -> (a s h b) i j", b=2))
                sp.wait_ge(stored, 16)
                for s in range(NB):
                    for half in range(2):
                        load(vec[16 * s + half:16 * s + 16:2], k.sample_rows.rearrange("(s t) (v h d) -> s h t v d", t=DS, v=6, h=H8)[s])
                sp.wait_ge(stepped, 8 * DS + 3)
                store = Loads(sp, out)
                store(k.s_wkv[bass.ds(l, 1)].rearrange("a s h (b i) j -> (a s h b) i j", b=2), state[:, :, :])
                for s in range(NB):
                    store(k.sample_y.rearrange("(s t) (g i) -> s g t i", t=DS, i=HALF)[s], y[16 * s:16 * s + 16])
                store.wait()
                sp.dma_start(yrow, k.sample_y).then_inc(back, 16)
                sp.wait_ge(back, 16)

            @block.vector
            def _(dve):
                step = Steps(dve, stepped)
                dve.wait_ge(loaded, 16 * (1 + 2 * NB))
                step.then(dve.tensor_scalar(mine[:, :, :], vec[:, :, 3, 0:HALF], k.c("half0"), None, ALU.mult))
                step.then(dve.tensor_scalar(other[:, :, :], vec[:, :, 3, HALF:C], k.c("half1"), None, ALU.mult))
                step.then(dve.tensor_tensor(mine[:, :, :], mine[:, :, :], other[:, :, :], ALU.add))
                over_i = lambda t, n: vec[:, t, n, :].unsqueeze(1).to_broadcast([P, HALF, C])
                S, Z = state[:, :, :], tmp[:, :, :]
                for t in range(DS):
                    step.then(dve.tensor_tensor(Z, S, over_i(t, 4), ALU.mult))
                    step.then(dve.tensor_reduce(sa[:, :], Z, AX.X, ALU.add))
                    step.then(dve.tensor_tensor(S, S, over_i(t, 1), ALU.mult))
                    step.then(dve.tensor_tensor(Z, sa[:, :].unsqueeze(2).to_broadcast([P, HALF, C]), over_i(t, 5), ALU.mult))
                    step.then(dve.tensor_tensor(S, S, Z, ALU.add))
                    dve.wait_ge(grown, t + 1)
                    step.then(dve.tensor_tensor(S, S, outer[:, :, :], ALU.add))
                    step.then(dve.tensor_tensor(Z, S, over_i(t, 0), ALU.mult))
                    step.then(dve.tensor_reduce(y[:, t, :], Z, AX.X, ALU.add))

            @block.gpsimd
            def _(pool):
                pool.wait_ge(stepped, 3)
                for t in range(DS):
                    if t >= 1:
                        pool.wait_ge(stepped, 3 + 8 * (t - 1) + 6)
                    pool.tensor_tensor(outer[:, :, :], mine[:, t, :].unsqueeze(2).to_broadcast([P, HALF, C]),
                                       vec[:, t, 2, :].unsqueeze(1).to_broadcast([P, HALF, C]), ALU.mult).then_inc(grown, 1)
        turn(nc, k, "rsy", [([yrow[:, P * i:P * i + P] for i in range(4)], [(side_by_side(NS, 4), k.y_sample_t[:, :, :])])])


def rwkv_chunks(nc, k, l):
    ft = k.ft
    with ExitStack() as ctx:
        sb, ps = scope(nc, ctx)
        state = sb("rc_state", [P, 4, P])
        vpad = sb("rc_vpad", [P, 4, 2 * C])
        bkz = sb("rc_bkz", [P, 2, 4, 2 * C])
        gm = sb("rc_gm", [P, H8, 2 * C])
        bkt = sb("rc_bkt", [P, H8, P])
        uvz = sb("rc_uvz", [P, H8, C])
        uv = sb("rc_uv", [P, H8, C])
        names = "n_block n_blockT n_rest n_restT n2 n2T n4 n4T n8T d1 d2 d3 d4 d4T r rT r1 r2T q1 invT x ys".split()
        m = {n: sb(f"rc_{n}", [C, H8, C]) for n in names}
        banks = ExitStack()
        _, ps = scope(nc, banks)
        p_g = ps("rc_p_g", [P, 2, 512])
        pa, pb, pc, pd, px, py = (ps(f"rc_p{i}", [P, 512]) for i in range(6))
        top = lambda t: t[0:C, :].rearrange("p (h c) -> p h c", h=H8)
        eye = k.c("ident")[0:C, 0:C].unsqueeze(1).to_broadcast([C, H8, C])
        blk = k.c("block16")[0:C].unsqueeze(1).to_broadcast([C, H8, C])
        cleared, = k.signals[:1]
        with stage(nc, k.signals) as block:
            @block.vector
            def _(dve):
                for t in (state, bkz, uvz):
                    dve.memset(t[:], 0.0)
                dve.memset(vpad[:, :, 0:C], 0.0)
                dve.tensor_copy(vpad[:, :, C:2 * C], ft[:, V_SLOT:V_SLOT + 4, 0:C])
        made, by_v, by_s, by_p, padded = k.signals[:5]
        for c in range(NC):
            with stage(nc, k.signals) as block:
                @block.tensor
                def _(pe):
                    done = Steps(pe, made)

                    def heads(out, lhs, rhs):
                        for h in range(H8):
                            last = pe.matmul(out[0:C, C * h:C * h + C], lhs[:, h, :], rhs[:, h, :], start=True, stop=True)
                        return last

                    for j in range(4):
                        src = vpad[:, j, :] if c == 0 else ft[:, V_SLOT + j, C * (c - 1):C * (c + 1)]
                        last = pe.transpose(pd[:, P * j:P * j + P], src, k.c("ident"))
                    done(last)
                    pe.wait_ge(padded, 2)
                    for h in range(H8):
                        last = pe.matmul(p_g[:, h // 4, P * (h % 4):P * (h % 4) + P], bkz[:, h % 2, h // 2, :],
                                         k.kr[:, h // 2, c].rearrange("p u t -> p (u t)"), start=True, stop=True)
                    done(last)
                    pe.wait_ge(by_v, 2)
                    for h in range(H8):
                        last = pe.transpose(pa[0:C, C * h:C * h + C], gm[0:C, h, 0:C], k.c("ident")[0:C, 0:C])
                    done(last)
                    for h in range(H8):
                        last = pe.transpose(p_g[:, h // 4, P * (h % 4):P * (h % 4) + P], bkz[:, h % 2, h // 2, :], k.c("ident"))
                    done(last)
                    pe.wait_ge(by_v, 5)
                    pe.wait_ge(by_p, 2)
                    done(heads(pb, m["n_blockT"], m["n_block"]))
                    done(heads(pc, m["n_block"], m["n_blockT"]))
                    pe.wait_ge(by_v, 6)
                    pe.wait_ge(by_s, 2)
                    done(heads(pa, m["n2T"], m["n2"]))
                    done(heads(pb, m["n2"], m["n2T"]))
                    done(heads(pc, m["n2T"], m["d1"]))
                    pe.wait_ge(by_v, 8)
                    pe.wait_ge(by_s, 3)
                    done(heads(pa, m["n4"], m["n4T"]))
                    done(heads(pb, m["n4T"], m["d2"]))
                    pe.wait_ge(by_v, 9)
                    pe.wait_ge(by_s, 4)
                    done(heads(pc, m["n8T"], m["d3"]))
                    pe.wait_ge(by_v, 10)
                    done(heads(pa, m["n_restT"], m["d4"]))
                    done(heads(pb, m["d4"], m["n_restT"]))
                    for h in range(H8):
                        last = pe.transpose(pc[0:C, C * h:C * h + C], m["d4"][:, h, :], k.c("ident")[0:C, 0:C])
                    done(last)
                    for j in range(4):
                        pe.matmul(px[0:C, P * j:P * j + P], k.kr[:, j, c, 0, :], state[:, j, :], start=(j == 0), stop=False, skip_group_check=True)
                    for h in range(H8):
                        last = pe.matmul(px[0:C, C * h:C * h + C], gm[:, h, 0:C], uvz[:, h, :], start=False, stop=(h == H8 - 1), skip_group_check=True)
                    done(last)
                    pe.wait_ge(by_v, 12)
                    pe.wait_ge(by_s, 6)
                    done(heads(pd, m["r"], m["rT"]))
                    pe.wait_ge(by_s, 7)
                    done(heads(pa, m["r2T"], m["r1"]))
                    pe.wait_ge(by_v, 13)
                    done(heads(pb, m["q1"], m["d4T"]))
                    pe.wait_ge(by_v, 14)
                    pe.wait_ge(by_s, 8)
                    done(heads(pc, m["invT"], m["x"]))
                    pe.wait_ge(by_v, 15)
                    for j in range(4):
                        pe.matmul(py[0:C, P * j:P * j + P], k.kr[:, j, c, 1, :], state[:, j, :], start=(j == 0), stop=False, skip_group_check=True)
                    for h in range(H8):
                        last = pe.matmul(py[0:C, C * h:C * h + C], gm[:, h, C:2 * C], uv[:, h, :], start=False, stop=(h == H8 - 1), skip_group_check=True)
                    done(last)
                    for h in range(H8):
                        last = pe.matmul(pd[:, C * h:C * h + C], bkt[:, h, :], uv[:, h, :], start=True, stop=True)
                    done(last)
                    pe.wait_ge(by_s, 9)
                    for j in range(4):
                        last = pe.transpose(pa[:, C * j:C * j + C], m["ys"][:, 2 * j:2 * j + 2, :].rearrange("p h i -> p (h i)"), k.c("ident")[0:C, 0:C])
                    done(last)

                @block.gpsimd
                def _(pool):
                    for r in range(2):
                        pool.tensor_copy(bkz[64 * r:64 * r + 64, r, :, :], k.bk[64 * r:64 * r + 64, :, c].rearrange("p j u t -> p j (u t)")).then_inc(padded, 1)
                    pool.wait_ge(by_v, 2)
                    pool.tensor_tensor(m["n_blockT"][:], gm[0:C, :, 0:C], blk, ALU.mult).then_inc(by_p, 1)
                    pool.wait_ge(by_p, 1)
                    pool.tensor_tensor(m["n_restT"][:], gm[0:C, :, 0:C], m["n_blockT"][:], ALU.subtract).then_inc(by_p, 1)

                @block.scalar
                def _(act):
                    done = Steps(act, by_s)

                    def keep(n, out, src):
                        act.wait_ge(made, n)
                        done(act.copy(out, src))

                    act.wait_ge(made, 4)
                    done(act.copy(bkt[:, :, :], p_g[:, :, :].rearrange("p b (h f) -> p (b h) f", h=4)))
                    keep(6, m["n2T"][:], top(pc))
                    keep(8, m["n4T"][:], top(pb))
                    keep(10, m["n8T"][:], top(pa))
                    keep(14, m["rT"][:], top(pb))
                    keep(15, m["d4T"][:], top(pc))
                    keep(17, m["r2T"][:], top(pd))
                    keep(16, m["x"][:], top(px))
                    keep(21, m["ys"][:], top(py))
                    act.wait_ge(made, 23)
                    done(act.copy(ft[:, R_SLOT:R_SLOT + 4, C * c:C * c + C], pa[:, 0:4 * C].rearrange("p (j t) -> p j t", j=4)))

                @block.vector
                def _(dve):
                    done = Steps(dve, by_v)
                    dve.wait_ge(made, 1)
                    dve.tensor_copy(uvz[C:P, :, :], pd[C:P, :].rearrange("p (h i) -> p h i", h=H8))
                    done(dve.tensor_copy(uv[C:P, :, :], pd[C:P, :].rearrange("p (h i) -> p h i", h=H8)))
                    dve.wait_ge(made, 2)
                    for b in range(2):
                        last = dve.tensor_tensor(gm[:, 4 * b:4 * b + 4, :], p_g[:, b, :].rearrange("p (h t) -> p h t", h=4),
                                                 k.c("wy_mask").unsqueeze(1).to_broadcast([P, 4, 2 * C]), ALU.mult)
                    done(last)
                    dve.wait_ge(made, 3)
                    done.then(dve.tensor_tensor(m["n_block"][:], top(pa), blk, ALU.mult))
                    done(dve.tensor_tensor(m["n_rest"][:], top(pa), m["n_block"][:], ALU.subtract))
                    done(dve.tensor_tensor(m["d1"][:], m["n_block"][:], eye, ALU.add))
                    dve.wait_ge(made, 5)
                    done(dve.tensor_copy(m["n2"][:], top(pb)))
                    dve.wait_ge(made, 7)
                    done(dve.tensor_copy(m["n4"][:], top(pa)))
                    dve.wait_ge(made, 9)
                    done.then(dve.tensor_tensor(m["d2"][:], top(pc), m["d1"][:], ALU.add))
                    dve.wait_ge(made, 11)
                    done.then(dve.tensor_tensor(m["d3"][:], top(pb), m["d2"][:], ALU.add))
                    dve.wait_ge(made, 12)
                    done(dve.tensor_tensor(m["d4"][:], top(pc), m["d3"][:], ALU.add))
                    dve.wait_ge(made, 13)
                    done(dve.tensor_copy(m["r"][:], top(pa)))
                    done.then(dve.tensor_tensor(m["r1"][:], top(pa), eye, ALU.add))
                    dve.wait_ge(made, 18)
                    done(dve.tensor_tensor(m["q1"][:], top(pa), m["r1"][:], ALU.add))
                    dve.wait_ge(made, 19)
                    done(dve.tensor_copy(m["invT"][:], top(pb)))
                    dve.wait_ge(made, 20)
                    done(dve.tensor_copy(uv[0:C, :, :], top(pc)))
                    dve.wait_ge(made, 22)
                    done.then(dve.tensor_tensor(state[:], state[:], pd[:, :].rearrange("p (j f) -> p j f", j=4), ALU.add))
                    done(dve.tensor_tensor(state[:], state[:], k.ends[:, :, c].unsqueeze(2).to_broadcast([P, 4, P]), ALU.mult))
        banks.close()
        outT = sb("rc_outT", [P, 4, P])
        turn(nc, k, "rc_state", [([state[:, j, :] for j in range(4)], [(lambda b: b[:, :].rearrange("p (j f) -> p j f", j=4), outT[:, :, :])])])
        with stage(nc, k.signals) as block:
            @block.sync
            def _(sp):
                store = Loads(sp, k.signals[0])
                for h in range(H8):
                    r = h % 2
                    store(k.p_wkv[bass.ds(l, 1), 0, h].rearrange("a i j -> (a i) j"), outT[C * r:C * r + C, h // 2, C * r:C * r + C])
                store.wait()

            @block.vector
            def _(dve):
                dve.tensor_copy(ft[:, R_SLOT:R_SLOT + 4, NP:NT], k.y_sample_t[:, :, :])


def rwkv_out(nc, k):
    ft = k.ft
    with ExitStack() as ctx:
        sb, ps = scope(nc, ctx)
        sq = sb("ro_sq", [P, NT])
        sums = ps("ro_sums", [P, 2, 2, 512])
        summed, centered, squared, scaled, powered, stepped, logged = k.signals[:7]
        halves = ((0, NP, 0), (NP, NT, 1))
        with stage(nc, k.signals) as block:
            @block.tensor
            def _(pe):
                for i in range(4):
                    if i >= 1:
                        pe.wait_ge(scaled, 2 * i)
                    for a, b, part in halves:
                        last = pe.matmul(sums[:, 0, part, 0:b - a], k.c("head_ones"), ft[:, R_SLOT + i, a:b], start=True, stop=True)
                    last.then_inc(summed, 1)
                    pe.wait_ge(squared, i + 1)
                    for a, b, part in halves:
                        last = pe.matmul(sums[:, 1, part, 0:b - a], k.c("head_ones"), sq[:, a:b], start=True, stop=True)
                    last.then_inc(summed, 1)

            @block.scalar
            def _(act):
                for i in range(4):
                    act.wait_ge(scaled, 2 * i + 2)
                    inverse_root(act, logged, sq[:, :], at=i).then_inc(powered, 1)

            @block.vector
            def _(dve):
                step = Steps(dve, stepped)
                for i in range(4):
                    y, out = ft[:, R_SLOT + i, :], k.mixT[:, 12 + i, :]
                    dve.wait_ge(summed, 2 * i + 1)
                    for a, b, part in halves:
                        last = dve.scalar_tensor_tensor(y[:, a:b], sums[:, 0, part, 0:b - a], -1.0 / C, y[:, a:b], ALU.mult, ALU.add)
                    step.then(last)
                    dve.tensor_tensor(sq[:, :], y, y, ALU.mult).then_inc(squared, 1)
                    dve.wait_ge(summed, 2 * i + 2)
                    for a, b, part in halves:
                        dve.tensor_scalar(sq[:, a:b], sums[:, 1, part, 0:b - a], 1.0 / C, LN_EPS, ALU.mult, ALU.add).then_inc(scaled, 1)
                    dve.wait_ge(powered, i + 1)
                    step.then(dve.scalar_tensor_tensor(y, y, k.prm[:, ROW_LNW + i:ROW_LNW + i + 1], sq[:, :], ALU.mult, ALU.mult))
                    step.then(dve.scalar_tensor_tensor(out, y, k.prm[:, ROW_LNB + i:ROW_LNB + i + 1], k.bonus[:, i, :], ALU.add, ALU.add))


INPUTS = ["x_prompt", "x_sample", "cache_sb_kv", "cache_dsa", "state_ret", "state_wkv", "state_shift", "page_table",
          "norm_g", "w_in", "shift_mu", "rw_w0", "rw_w2", "rw_a0", "rw_a2", "rw_kk", "rw_ka", "rw_rk",
          "rw_lnx_w", "rw_lnx_b", "w_out", "final_g"]
OUTPUTS = [("y_prompt", (1, NP, D)), ("y_sample", (NB, DS, D)),
           ("p_sb", (DEPTH, 1, NP, 2, 4, P)), ("p_dsa", (DEPTH, 1, NP, DSA_W)), ("p_ret", (DEPTH, 1, 4, 64, P)),
           ("p_wkv", (DEPTH, 1, H8, 64, 64)), ("p_shift", (DEPTH, 1, SHIFT_W)),
           ("s_sb", (DEPTH, NB, DS, 2, 4, P)), ("s_dsa", (DEPTH, NB, DS, DSA_W)), ("s_ret", (DEPTH, NB, 4, 64, P)),
           ("s_wkv", (DEPTH, NB, H8, 64, 64)), ("s_shift", (DEPTH, NB, SHIFT_W))]


def build(nc, tensors, groups="ABCD", probe=None):
    k = Core(tensors)
    with ExitStack() as ctx, nc.allow_non_contiguous_dma(reason="rows of a few values"):
        sb, _ = scope(nc, ctx)
        k.signals = [ctx.enter_context(nc.semaphore(f"signal_{i}")) for i in range(24)]
        k.table = sb("table", [P, TABLE.shape[1]])
        k.c = lambda name: k.table[:, AT[name][0]:AT[name][0] + AT[name][1]]
        k.prm = sb("prm", [P, PRM_ROWS])
        k.pages = sb("pages", [1, NB * PAGES], I32)
        k.scratch = sb("scratch", [P, 2, NT])
        k.mixT = sb("mixT", [P, KT, NT])
        k.x_spill = nc.dram_tensor("x_spill", (P, KT * NT), F32, kind="Internal").ap()
        k.sample_rows = nc.dram_tensor("sample_rows", (NS, 6 * GW), F32, kind="Internal").ap()
        k.sample_y = nc.dram_tensor("sample_y", (NS, GW), F32, kind="Internal").ap()
        k.sample_w = nc.dram_tensor("sample_w", (NS, 8), F32, kind="Internal").ap()
        arrived, = k.signals[:1]
        with stage(nc, k.signals) as block:
            @block.sync
            def _(sp):
                load = Loads(sp, arrived)
                load(k.table[:, :], k.consts)
                load(k.pages[:, :], k.page_table.rearrange("a b -> (a b)").unsqueeze(0))
                load.wait()

            @block.vector
            def _(dve):
                dve.memset(k.mixT[:, :, :], 0.0)

        with ExitStack() as own:
            k.xT = scope(nc, own)[0]("xT_in", [P, KT, NT])
            load_x(nc, k)
            spill_x(nc, k, back=False)

        with nc.Fori(0, DEPTH) as l:
            with ExitStack() as layer:
                sb2, _ = scope(nc, layer)
                k.ft = sb2("ft", [P, SLOTS, NT])
                with ExitStack() as most:
                    sb3, _ = scope(nc, most)
                    k.hT = sb3("hT", [P, KT, NT])
                    k.ring = sb3("ring", [P, 3, KT, P])
                    with ExitStack() as own:
                        k.xT = scope(nc, own)[0]("xT_norm", [P, KT, NT])
                        spill_x(nc, k, back=True)
                        load_parameters(nc, k, l)
                        norm(nc, k, "norm", k.prm[:, ROW_G:ROW_G + KT], k.hT)
                    for letter, name, tiles, mixer in (("A", "ret", RET_TILES, retention), ("B", "sb", SB_TILES, stick_breaking),
                                                       ("C", "dsa", DSA_TILES, sparse_attention)):
                        if letter in groups:
                            project_group(nc, k, l, name, tiles)
                            mixer(nc, k, l)
                    if "D" in groups:
                        project_group(nc, k, l, "rw", RW_TILES)
                if "D" in groups:
                    rwkv(nc, k, l)
                if probe is not None:
                    moved, = k.signals[:1]
                    with stage(nc, k.signals) as block:
                        @block.sync
                        def _(sp):
                            sp.dma_start(probe[bass.ds(l, 1)].rearrange("a p n -> (a p) n"), k.mixT[:, :, :].rearrange("p k t -> p (k t)")).then_inc(moved, 16)
                            sp.wait_ge(moved, 16)
                k.ring = sb2("ring_out", [P, 3, KT, P])
                k.xT = sb2("xT_out", [P, KT, NT])
                spill_x(nc, k, back=True)
                project_out(nc, k, l)
                spill_x(nc, k, back=False)
        with ExitStack() as own:
            k.xT = scope(nc, own)[0]("xT_last", [P, KT, NT])
            spill_x(nc, k, back=True)
            store_y(nc, k)


def kernel(**inputs):
    import numpy as _np
    import concourse.bacc as _bacc
    from concourse.bass_utils import run_bass_kernel_spmd as _run

    nc = _bacc.Bacc("TRN2", target_bir_lowering=False, num_devices=1)
    arrays, tensors = {"in_consts": TABLE}, {}
    for name in INPUTS:
        arrays["in_" + name] = _np.ascontiguousarray(inputs[name])
    for name, a in arrays.items():
        tensors[name[3:]] = nc.dram_tensor(name, a.shape, mybir.dt.from_np(a.dtype), kind="ExternalInput").ap()
    for name, shape in OUTPUTS:
        tensors[name] = nc.dram_tensor("out_" + name, shape, F32, kind="ExternalOutput").ap()
    build(nc, tensors)
    r = _run(nc, [arrays], core_ids=[0])
    return tuple(r.results[0]["out_" + name] for name, _ in OUTPUTS)
```

```python
from contextlib import ExitStack, contextmanager

import numpy as np

import concourse.bass as bass
from concourse import mybir

F32 = mybir.dt.float32
F32R = mybir.dt.float32r
I32 = mybir.dt.int32
ALU = mybir.AluOpType
ACT = mybir.ActivationFunctionType
AX = mybir.AxisListType

P = 128
D = 2048
KT = D // P
DEPTH = 2
NP = 512
NB = 8
DS = 4
NS = NB * DS
NT = NP + NS
QB = NP // P
TT = QB + 1
PAST = 512
PAGES = PAST // P
POOL = 40
GW = 512
DSA_W = 320
SHIFT_W = 1728
LORA = 96
TOPK = 128
TOPK_S = (PAST + DS) // 4
C = 64
NC = NP // C
H8 = 8
EPS = 1e-6
LN_EPS = 64e-5
NEG = -1e30
SB_SCALE = 128 ** -0.5
LOG_G = np.log1p(-np.exp2(-5.0 - np.arange(4)))

def _tiles(col, n):
    return [(col + P * i, P) for i in range(n)]

RET_TILES = _tiles(0, 12)
SB_TILES = _tiles(1536, 16)
DSA_TILES = _tiles(3584, 6) + [(4864, 64)] + _tiles(4352, 4) + [(4928, 8)] + _tiles(4936, 4)
RW_TILES = (_tiles(5448, 4) + [(5960, LORA)] + _tiles(6056, 8) + [(7080, LORA)] + _tiles(7176, 4))
SLOTS = 18

ROW_G, ROW_W0, ROW_A0, ROW_KK, ROW_KA, ROW_RK, ROW_LNW, ROW_LNB, ROW_MU = 0, 16, 20, 24, 28, 32, 36, 40, 44
PRM_ROWS = ROW_MU + 14


def constants():
    f = np.float32
    at, parts = {}, []

    def add(name, a):
        a = np.asarray(a, f).reshape(len(a), -1)
        full = np.zeros((P, a.shape[1]), f)
        full[: len(a)] = a
        at[name] = (sum(x.shape[1] for x in parts), a.shape[1])
        parts.append(full)

    i = np.arange(P)
    add("ident", np.eye(P))
    add("ones", np.ones((P, P)))
    add("head_ones", (i[:, None] // 64 == i[None] // 64))
    add("later", i[:, None] > i[None])
    add("before", i[:, None] < i[None])
    diff = i[None, :] - i[:, None]
    add("ret_mask", np.stack([np.where(diff >= 0, np.exp(np.maximum(diff, 0) * g), 0) for g in LOG_G], 1))
    t = np.arange(NS)
    same = t[:, None] // DS == t[None] // DS
    dt = t[None] - t[:, None]
    add("ret_mask_s", np.stack([np.where(same & (dt >= 0), np.exp(np.maximum(dt, 0) * g), 0) for g in LOG_G], 1))
    qdec = np.zeros((P, 2, 4)); kdec = np.zeros((P, 2, 4))
    qdec[:, 0] = np.exp((i[:, None] + 1) * LOG_G); kdec[:, 0] = np.exp((P - 1 - i[:, None]) * LOG_G)
    qdec[:NS, 1] = np.exp((t[:, None] % DS + 1) * LOG_G); kdec[:NS, 1] = np.exp((DS - 1 - t[:, None] % DS) * LOG_G)
    add("qdec", qdec); add("kdec", kdec)
    pos = np.zeros((P, TT), f)
    for a in range(QB):
        pos[:, a] = a * P + i
    pos[:NS, QB] = PAST + t % DS
    inv = (1.0 / (10000.0 ** (np.arange(32, dtype=f) / f(32)))).astype(f)
    ang = (pos[:, :, None] * inv).astype(f).astype(np.float64)
    add("cos", np.cos(ang)); add("sin", np.sin(ang))
    add("cosk", np.cos(ang) * 0.125); add("sink", np.sin(ang) * 0.125)
    add("seq_of", (t[:, None] // DS == np.arange(NB)[None]))
    add("before_s", same & (t[:, None] < t[None]))
    add("dsa_neg", np.where(i[None] <= i[:, None], 0, NEG))
    row = np.arange(P) % NS
    add("dsa_neg_s", np.where((row[:, None] // DS == t[None] // DS) & (t[None] <= row[:, None]), 0, NEG))
    rt = np.arange(NS) % DS
    add("spread", (rt[:, None, None] == row[None, None] % DS) & (np.arange(NB)[None, :, None] == row[None, None] // DS))
    j, u = i[:, None] % C, np.arange(C)[None]
    add("block_before", (j < u) & (j // 16 == u // 16))
    add("block_earlier", j // 16 < u // 16)
    add("chunk_before", j < u)
    add("chunk_upto", j <= u)
    add("chunk_in", np.broadcast_to(np.arange(NP) % C != 0, (P, NP)))
    add("half0", (i % 2 == 0)[:, None]); add("half1", (i % 2 == 1)[:, None])
    return at, np.concatenate(parts, 1)


AT, TABLE = constants()


@contextmanager
def stage(nc, signals):
    with nc.Block() as block:
        yield block
    nc.gpsimd.sem_clear(range(signals[0].num, signals[-1].num + 1))
    nc.all_engine_barrier()


class Steps:

    def __init__(self, engine, sem):
        self.engine, self.sem, self.n = engine, sem, 0

    def __call__(self, instruction):
        self.n += 1
        instruction.then_inc(self.sem, 1)
        return self.n

    def wait(self):
        self.engine.wait_ge(self.sem, self.n)

    def then(self, instruction):
        self(instruction)
        self.wait()


class Loads:

    def __init__(self, engine, sem):
        self.engine, self.sem, self.n = engine, sem, 0

    def __call__(self, out, in_):
        self.n += 16
        self.engine.dma_start(out, in_).then_inc(self.sem, 16)

    def wait(self):
        self.engine.wait_ge(self.sem, self.n)


def inverse_root(act, logged, x, scale=1.0, at=0):
    act.activation(x, x, ACT.Ln, scale=scale).then_inc(logged, 1)
    act.wait_ge(logged, at + 1)
    return act.activation(x, x, ACT.Exp, scale=-0.5)


class Core:

    def __init__(self, tensors):
        self.consts = tensors["consts"]
        self.x_prompt = tensors["x_prompt"]
        self.x_sample = tensors["x_sample"]
        self.cache_sb_kv = tensors["cache_sb_kv"]
        self.cache_dsa = tensors["cache_dsa"]
        self.state_ret = tensors["state_ret"]
        self.state_wkv = tensors["state_wkv"]
        self.state_shift = tensors["state_shift"]
        self.page_table = tensors["page_table"]
        self.norm_g = tensors["norm_g"]
        self.w_in = tensors["w_in"]
        self.shift_mu = tensors["shift_mu"]
        self.rw_w0 = tensors["rw_w0"]
        self.rw_w2 = tensors["rw_w2"]
        self.rw_a0 = tensors["rw_a0"]
        self.rw_a2 = tensors["rw_a2"]
        self.rw_kk = tensors["rw_kk"]
        self.rw_ka = tensors["rw_ka"]
        self.rw_rk = tensors["rw_rk"]
        self.rw_lnx_w = tensors["rw_lnx_w"]
        self.rw_lnx_b = tensors["rw_lnx_b"]
        self.w_out = tensors["w_out"]
        self.final_g = tensors["final_g"]
        self.y_prompt = tensors["y_prompt"]
        self.y_sample = tensors["y_sample"]
        self.p_sb = tensors["p_sb"]
        self.p_dsa = tensors["p_dsa"]
        self.p_ret = tensors["p_ret"]
        self.p_wkv = tensors["p_wkv"]
        self.p_shift = tensors["p_shift"]
        self.s_sb = tensors["s_sb"]
        self.s_dsa = tensors["s_dsa"]
        self.s_ret = tensors["s_ret"]
        self.s_wkv = tensors["s_wkv"]
        self.s_shift = tensors["s_shift"]


def scope(nc, ctx):
    def sb(name, shape, dt=F32):
        return ctx.enter_context(nc.sbuf_tensor(name, shape, dt))

    def ps(name, shape):
        return ctx.enter_context(nc.psum_tensor(name, shape, F32))

    return sb, ps


def turn(nc, k, name, jobs):
    turned, kept_v, kept_s = k.signals[:3]
    R = 4
    with ExitStack() as ctx:
        _, ps = scope(nc, ctx)
        banks = ps(f"{name}_banks", [P, R, 512])
        with stage(nc, k.signals) as block:
            @block.tensor
            def _(pe):
                for n, (pieces, _) in enumerate(jobs):
                    if n >= R:
                        before = n - R
                        pe.wait_ge(kept_v if before % 2 == 0 else kept_s, before // 2 + 1)
                    at = 0
                    for piece in pieces:
                        rows, cols = piece.shape
                        last = pe.transpose(banks[0:cols, n % R, at:at + rows], piece, k.c("ident")[0:rows, 0:rows])
                        at += rows
                    last.then_inc(turned, 1)

            def copies(engine, copy, kept, odd):
                for n, (_, outs) in enumerate(jobs):
                    if n % 2 != odd:
                        continue
                    engine.wait_ge(turned, n + 1)
                    for m, (view, dst) in enumerate(outs):
                        last = copy(dst, view(banks[:, n % R, :]))
                    last.then_inc(kept, 1)

            @block.vector
            def _(dve):
                copies(dve, dve.tensor_copy, kept_v, 0)

            @block.scalar
            def _(act):
                copies(act, act.copy, kept_s, 1)


HALF_K = KT // 2
HALF_N = NT // 2


def split_pair(sb, name):
    return sb(f"{name}_hi", [P, KT, NT], F32R), sb(f"{name}_lo", [P, KT, NT], F32R)


def weight_buffers(k, name, sb):
    k.raw = sb(f"{name}_w_raw", [P, 4, HALF_K, P])
    k.w_hi = sb(f"{name}_w_hi", [P, 3, HALF_K, P], F32R)
    k.w_lo = sb(f"{name}_w_lo", [P, 3, HALF_K, P], F32R)


def project(nc, k, l, name, weights, tiles, source, keep, gates=()):
    product_ready, kept_a, kept_v, rounded, parted, used, opened, stepped = k.signals[:8]
    loaded = k.signals[8:12]
    w_l = weights[bass.ds(l, 1)].rearrange("a (k p) c -> p (a k) c", p=P)
    s_hi, s_lo = source
    pieces = 2 * len(tiles)
    with ExitStack() as ctx:
        _, ps = scope(nc, ctx)
        psum = ps(f"{name}_psum", [P, 2, 2, 512])
        with stage(nc, k.signals) as block:
            @block.sync
            def _(sp):
                for u in range(pieces):
                    col, width, twice = tiles[u // 2]
                    half = slice(HALF_K * (u % 2), HALF_K * (u % 2) + HALF_K)
                    if u >= 4:
                        sp.wait_ge(parted, u - 3)
                    dst = k.raw[:, u % 4, :, :]
                    if twice:
                        sp.dma_start(dst[:, :, 0:width], w_l[:, half, col:col + width]).then_inc(loaded[u % 4], 16)
                        sp.dma_start(dst[:, :, width:P], w_l[:, half, col:col + width]).then_inc(loaded[u % 4], 16)
                    else:
                        sp.dma_start(dst, w_l[:, half, col:col + P]).then_inc(loaded[u % 4], 16)

            arrived, count = [], [0] * 4
            for u in range(pieces):
                count[u % 4] += 32 if tiles[u // 2][2] else 16
                arrived.append(count[u % 4])

            @block.tensor
            def _(pe):
                for i in range(len(tiles)):
                    if i >= 2:
                        pe.wait_ge(kept_a, i - 1)
                        pe.wait_ge(kept_v, i - 1)
                    for u in (2 * i, 2 * i + 1):
                        pe.wait_ge(parted, u + 1)
                        for t in range(HALF_K):
                            f = HALF_K * (u % 2) + t
                            first, last_k = f == 0, f == KT - 1
                            for w, parts in ((k.w_hi, (s_hi, s_lo)), (k.w_lo, (s_hi,))):
                                for part in parts:
                                    for c in range(2):
                                        last = pe.matmul(psum[:, i % 2, c, 0:HALF_N], w[:, u % 3, t, :], part[:, f, HALF_N * c:HALF_N * c + HALF_N],
                                                         start=first and w is k.w_hi and part is s_hi, stop=last_k and w is k.w_lo)
                        last.then_inc(used if u % 2 == 0 else product_ready, 1)

            def piece_free(engine, u):
                if u >= 3:
                    v = u - 3
                    engine.wait_ge(used if v % 2 == 0 else product_ready, v // 2 + 1)

            @block.scalar
            def _(act):
                def round_piece(u):
                    act.wait_ge(loaded[u % 4], arrived[u])
                    piece_free(act, u)
                    act.copy(k.w_hi[:, u % 3, :, :], k.raw[:, u % 4, :, :]).then_inc(rounded, 1)

                for u in range(3):
                    round_piece(u)
                for i in range(len(tiles)):
                    for u in (2 * i + 3, 2 * i + 4):
                        if u == 2 * i + 4:
                            act.wait_ge(product_ready, i + 1)
                            if keep is not None:
                                act.copy(keep[:, i, 0:HALF_N], psum[:, i % 2, 0, 0:HALF_N]).then_inc(kept_a, 1)
                        if u < pieces:
                            round_piece(u)
                    if i in gates:
                        act.wait_ge(kept_v, i + 1)
                        act.wait_ge(kept_a, i + 1)
                        if gates.index(i) >= 2:
                            act.wait_ge(stepped, 3 * (gates.index(i) - 1))
                        act.activation(k.scratch[:, i % 2, :], keep[:, i, :], ACT.Exp, scale=-1.0).then_inc(opened, 1)

            @block.vector
            def _(dve):
                step = Steps(dve, stepped)

                def part_piece(u):
                    dve.wait_ge(rounded, u + 1)
                    piece_free(dve, u)
                    dve.tensor_tensor(k.w_lo[:, u % 3, :, :], k.raw[:, u % 4, :, :], k.w_hi[:, u % 3, :, :], ALU.subtract).then_inc(parted, 1)

                def silu(i):
                    e = k.scratch[:, i % 2, :]
                    dve.wait_ge(opened, gates.index(i) + 1)
                    step.then(dve.tensor_scalar(e, e, 1.0, None, ALU.add))
                    step.then(dve.reciprocal(e, e))
                    step(dve.tensor_tensor(keep[:, i, :], keep[:, i, :], e, ALU.mult))

                for u in range(3):
                    part_piece(u)
                for i in range(len(tiles)):
                    for u in (2 * i + 3, 2 * i + 4):
                        if u == 2 * i + 4:
                            dve.wait_ge(product_ready, i + 1)
                            if keep is not None:
                                dve.tensor_copy(keep[:, i, HALF_N:NT], psum[:, i % 2, 1, 0:HALF_N]).then_inc(kept_v, 1)
                            else:
                                for c, kept in ((0, kept_a), (1, kept_v)):
                                    x = k.xT[:, i, HALF_N * c:HALF_N * c + HALF_N]
                                    dve.tensor_tensor(x, x, psum[:, i % 2, c, 0:HALF_N], ALU.add).then_inc(kept, 1)
                        if u < pieces:
                            part_piece(u)
                        if u == 2 * i + 4 and i - 1 in gates:
                            silu(i - 1)
                if len(tiles) - 1 in gates:
                    silu(len(tiles) - 1)


def project_group(nc, k, l, name, tiles, gates):
    project(nc, k, l, name, k.w_in, [(*t, t == (4864, 64)) for t in tiles], k.h, k.ft, gates)


def project_out(nc, k, l):
    with ExitStack() as ctx:
        sb, _ = scope(nc, ctx)
        hi, lo = split_pair(sb, "mix")
        rounded, = k.signals[:1]
        with stage(nc, k.signals) as block:
            @block.scalar
            def _(act):
                for t in range(KT):
                    act.copy(hi[:, t, :], k.mixT[:, t, :]).then_inc(rounded, 1)

            @block.vector
            def _(dve):
                for t in range(KT):
                    dve.wait_ge(rounded, t + 1)
                    dve.tensor_tensor(lo[:, t, :], k.mixT[:, t, :], hi[:, t, :], ALU.subtract)
        weight_buffers(k, "out", sb)
        project(nc, k, l, "out", k.w_out, [(P * i, P, False) for i in range(KT)], (hi, lo), None)


def load_x(nc, k):
    with ExitStack() as ctx:
        sb, _ = scope(nc, ctx)
        rows = sb("x_rows", [P, 2, D])
        for a in range(TT):
            n = P if a < QB else NS
            arrived, = k.signals[:1]
            with stage(nc, k.signals) as block:
                @block.sync
                def _(sp):
                    src = k.x_prompt.rearrange("b t d -> (b t) d")[a * P:a * P + n] if a < QB else k.x_sample.rearrange("b t d -> (b t) d")
                    sp.dma_start(rows[0:n, a % 2, :], src).then_inc(arrived, 16)
                    sp.wait_ge(arrived, 16)
            turn(nc, k, f"xin{a}", [([rows[0:n, a % 2, P * (4 * q + i):P * (4 * q + i + 1)] for i in range(4)],
                 [(lambda b, n=n: b[:, 0:4 * n].rearrange("p (i t) -> p i t", t=n), k.xT[:, 4 * q:4 * q + 4, a * P:a * P + n])]) for q in range(4)])


def norm(nc, k, name, gains, out):
    squared, summed, scaled, powered, logged, normed, rounded, parted = k.signals[:8]
    with ExitStack() as ctx:
        sb, ps = scope(nc, ctx)
        sq = sb(f"{name}_sq", [P, 2, NT])
        rs = sb(f"{name}_rs", [P, NT])
        sums = ps(f"{name}_sums", [P, 2, 512])
        pair = isinstance(out, tuple)
        with stage(nc, k.signals) as block:
            @block.scalar
            def _(act):
                for t in range(KT):
                    if t >= 2:
                        act.wait_ge(summed, t - 1)
                    act.activation(sq[:, t % 2, :], k.xT[:, t, :], ACT.Square).then_inc(squared, 1)
                act.wait_ge(scaled, 2)
                inverse_root(act, logged, rs[:, :]).then_inc(powered, 1)
                for t in range(KT if pair else 0):
                    act.wait_ge(normed, t + 1)
                    act.copy(out[0][:, t, :], sq[:, t % 2, :]).then_inc(rounded, 1)

            @block.tensor
            def _(pe):
                for t in range(KT):
                    pe.wait_ge(squared, t + 1)
                    pe.matmul(sums[:, 0, :], k.c("ones"), sq[:, t % 2, 0:NP], start=(t == 0), stop=(t == KT - 1))
                    pe.matmul(sums[:, 1, 0:NS], k.c("ones"), sq[:, t % 2, NP:NT], start=(t == 0), stop=(t == KT - 1)).then_inc(summed, 1)

            @block.vector
            def _(dve):
                dve.wait_ge(summed, KT)
                dve.tensor_scalar(rs[:, 0:NP], sums[:, 0, :], 1.0 / D, EPS, ALU.mult, ALU.add).then_inc(scaled, 1)
                dve.tensor_scalar(rs[:, NP:NT], sums[:, 1, 0:NS], 1.0 / D, EPS, ALU.mult, ALU.add).then_inc(scaled, 1)
                dve.wait_ge(powered, 1)
                for t in range(KT + 1):
                    if t < KT:
                        if pair and t >= 2:
                            dve.wait_ge(parted, t - 1)
                        y = sq[:, t % 2, :] if pair else out[:, t, :]
                        dve.scalar_tensor_tensor(y, k.xT[:, t, :], gains[:, t:t + 1], rs[:, :], ALU.mult, ALU.mult).then_inc(normed, 1)
                    if pair and t >= 1:
                        dve.wait_ge(rounded, t)
                        dve.tensor_tensor(out[1][:, t - 1, :], sq[:, (t - 1) % 2, :], out[0][:, t - 1, :], ALU.subtract).then_inc(parted, 1)


def load_parameters(nc, k, l):
    with ExitStack() as ctx:
        sb, _ = scope(nc, ctx)
        rows = sb("prm_rows", [PRM_ROWS, P])
        loaded, cleared = k.signals[:2]
        with stage(nc, k.signals) as block:
            @block.vector
            def _(dve):
                dve.memset(rows[:, :], 0.0).then_inc(cleared, 1)

            @block.sync
            def _(sp):
                sp.wait_ge(cleared, 1)
                load = Loads(sp, loaded)

                def full(row, ap, n):
                    load(rows[row:row + n, :], ap[bass.ds(l, 1)].rearrange("a (n p) -> (a n) p", p=P))

                full(ROW_G, k.norm_g, KT)
                for row, ap in ((ROW_W0, k.rw_w0), (ROW_A0, k.rw_a0), (ROW_KK, k.rw_kk), (ROW_KA, k.rw_ka),
                                (ROW_LNW, k.rw_lnx_w), (ROW_LNB, k.rw_lnx_b)):
                    full(row, ap, 4)
                load(rows[ROW_RK:ROW_RK + 4, :], k.rw_rk[bass.ds(l, 1)].rearrange("a (j h) d -> (a j) (h d)", h=2))
                mu = k.shift_mu[bass.ds(l, 1)]
                for first, col, n in ((0, 0, 4), (5, 608, 8)):
                    load(rows[ROW_MU + first:ROW_MU + first + n, :], mu[:, col:col + P * n].rearrange("a (n p) -> (a n) p", p=P))
                for slot, col in ((4, 512), (13, 1632)):
                    load(rows[ROW_MU + slot:ROW_MU + slot + 1, 0:LORA], mu[:, col:col + LORA])
                load.wait()
        turn(nc, k, "prm", [([rows[:, :]], [(lambda b: b[:, 0:PRM_ROWS], k.prm[:, :])])])


def spill_x(nc, k, back):
    moved, = k.signals[:1]
    with stage(nc, k.signals) as block:
        @block.sync
        def _(sp):
            a, b = k.x_spill.rearrange("p (k t) -> p k t", t=NT), k.xT[:, :, :]
            (sp.dma_start(b, a) if back else sp.dma_start(a, b)).then_inc(moved, 16)
            sp.wait_ge(moved, 16)


def store_y(nc, k):
    with ExitStack() as ctx:
        sb, _ = scope(nc, ctx)
        rows = sb("fg_rows", [KT, P])
        fg = sb("fg", [P, KT])
        yT = sb("yT", [P, KT, NT])
        y = sb("y", [P, D])
        moved, = k.signals[:1]
        with stage(nc, k.signals) as block:
            @block.sync
            def _(sp):
                sp.dma_start(rows[:, :], k.final_g.rearrange("(n p) -> n p", p=P)).then_inc(moved, 16)
                sp.wait_ge(moved, 16)
        turn(nc, k, "fgt", [([rows[:, :]], [(lambda b: b[:, 0:KT], fg[:, :])])])
        norm(nc, k, "final", fg, yT)
        for a in range(TT):
            n = P if a < QB else NS
            turn(nc, k, f"yout{a}", [([yT[:, 4 * q + i, a * P:a * P + n] for i in range(4)],
                 [(lambda b, n=n: b[0:n, :], y[0:n, 512 * q:512 * q + 512])]) for q in range(4)])
            with stage(nc, k.signals) as block:
                @block.sync
                def _(sp):
                    dst = k.y_prompt.rearrange("b t d -> (b t) d")[a * P:a * P + n] if a < QB else k.y_sample.rearrange("b t d -> (b t) d")
                    sp.dma_start(dst, y[0:n, :]).then_inc(moved, 16)
                    sp.wait_ge(moved, 16)


def gate(nc, k, first, g):
    with stage(nc, k.signals) as block:
        @block.vector
        def _(dve):
            for i in range(3):
                dve.tensor_tensor(k.mixT[:, first + i, :], k.mixT[:, first + i, :], k.ft[:, g + i, :], ALU.mult)

        @block.gpsimd
        def _(pool):
            pool.tensor_tensor(k.mixT[:, first + 3, :], k.mixT[:, first + 3, :], k.ft[:, g + 3, :], ALU.mult)


def tokens(a):
    return (P, slice(a * P, a * P + P)) if a < QB else (NS, slice(NP, NT))


def side_by_side(n, width):
    return lambda b: b[:, 0:width * n].rearrange("p (i t) -> p i t", t=n)


def retention(nc, k, l):
    ft = k.ft
    with ExitStack() as ctx:
        sb, ps = scope(nc, ctx)
        qk = sb("ret_qk", [P, TT, 512])
        v = sb("ret_v", [P, TT, 512])
        rot = sb("ret_rot", [P, TT, 512])
        tmp = sb("ret_tmp", [P, TT, 4, 32])
        state = sb("ret_state", [P, 2, 2 * P])
        state_s = sb("ret_state_s", [P, NB, 2, P])
        qdz = sb("ret_qdz", [P, 2, 2, NS])
        qT, qdT, kz = ft[:, 0:2, :], ft[:, 2:4, :], ft[:, 4:8, :]
        jobs = []
        for a in range(TT):
            n, cols = tokens(a)
            jobs.append(([ft[:, s, cols] for s in range(4)], [(lambda b, n=n: b[0:n, :], qk[0:n, a, :])]))
            jobs.append(([ft[:, s, cols] for s in range(4, 8)], [(lambda b, n=n: b[0:n, :], v[0:n, a, :])]))
        turn(nc, k, "ret_in", jobs)

        turned, loaded = k.signals[:2]
        with stage(nc, k.signals) as block:
            @block.sync
            def _(sp):
                load = Loads(sp, loaded)
                for s in range(NB):
                    for par in range(2):
                        load(state_s[64 * par:64 * par + 64, s, :, :],
                             k.state_ret[bass.ds(l, 1), s].rearrange("a (j b) d e -> a b d j e", b=2)[0, par])
                load.wait()

            @block.vector
            def _(dve):
                step = Steps(dve, turned)
                dve.memset(state[:, :, :], 0.0)
                dve.memset(qdz[:, :, :, :], 0.0)
                dve.memset(kz[64:128, 0:2, :], 0.0)
                dve.memset(kz[0:64, 2:4, :], 0.0)
                for r0, (n, a0, a1) in enumerate(((P, 0, QB), (NS, QB, TT))):
                    w = a1 - a0
                    for part, (cos, sin) in enumerate((("cos", "sin"), ("cosk", "sink"))):
                        def halves(t):
                            h = t[0:n, a0:a1, 256 * part:256 * part + 256].rearrange("p a (h u d) -> p a h u d", h=4, u=2)
                            return h[:, :, :, 0, :], h[:, :, :, 1, :]

                        def table(name):
                            return k.c(name).rearrange("p (a d) -> p a d", d=32)[0:n, a0:a1].unsqueeze(2).to_broadcast([n, w, 4, 32])

                        def each(op, out, a, b, y):
                            for i in range(w):
                                last = dve.tensor_tensor(out[:, i], a[:, i], b[:, i], y)
                            op(last)

                        (x1, x2), (y1, y2) = halves(qk), halves(rot)
                        z = tmp[0:n, a0:a1]
                        each(step, y1, x1, table(cos), ALU.mult)
                        each(step.then, z, x2, table(sin), ALU.mult)
                        each(step, y2, x1, table(sin), ALU.mult)
                        each(step.then, y1, y1, z, ALU.subtract)
                        each(step.then, z, x2, table(cos), ALU.mult)
                        each(step.then, y2, y2, z, ALU.add)
                        dec = k.c("kdec" if part else "qdec").rearrange("p (r h) -> p r h", r=2)
                        for h in range(4):
                            col = slice(256 * part + 64 * h, 256 * part + 64 * h + 64)
                            step(dve.tensor_scalar(qk[0:n, a0:a1, col], rot[0:n, a0:a1, col], dec[0:n, r0, h:h + 1], None, ALU.mult))
        jobs = []
        for a in range(TT):
            n, cols = tokens(a)
            outs = [(side_by_side(n, 4), ft[:, 0:4, cols])]
            if a == QB:
                outs += [(lambda b, r=r: b[64 * r:64 * r + 64, 2 * NS:4 * NS].rearrange("p (i t) -> p i t", t=NS),
                          qdz[64 * r:64 * r + 64, r, :, :]) for r in range(2)]
            jobs.append(([t[0:n, a, P * i:P * i + P] for t in (rot, qk) for i in range(2)], outs))
            jobs.append(([rot[0:n, a, 256 + P * i:384 + P * i] for i in range(2)],
                         [(lambda b, n=n, r=r: b[64 * r:64 * r + 64, 0:2 * n].rearrange("p (i t) -> p i t", t=n),
                           kz[64 * r:64 * r + 64, 2 * r:2 * r + 2, cols]) for r in range(2)]))
        turn(nc, k, "ret_qk_T", jobs)

        scored, masked, made, kept, grown, carried, stored = k.signals[:7]
        with ExitStack() as inner:
            sb2, ps2 = scope(nc, inner)
            att = sb2("ret_att", [P, 2, 512])
            p_att, p_out, p_state = (ps2(f"ret_p_{x}", [P, 2, 512]) for x in ("att", "out", "state"))
            with stage(nc, k.signals) as block:
                @block.tensor
                def _(pe):
                    for c in range(QB):
                        tok = slice(c * P, c * P + P)
                        if c >= 2:
                            pe.wait_ge(masked, c - 1)
                            pe.wait_ge(carried, c - 1)
                            pe.wait_ge(kept, c - 1)
                        for h in range(4):
                            last = pe.matmul(p_att[:, c % 2, P * h:P * h + P], kz[:, 2 * (h % 2) + h // 2, tok],
                                             qT[:, h // 2, tok], start=True, stop=True)
                        last.then_inc(scored, 1)
                        for j in range(2):
                            last = pe.matmul(p_state[:, c % 2, 256 * j:256 * j + 256], qk[:, c, 256 + P * j:384 + P * j],
                                             v[:, c, 256 * j:256 * j + 256], start=True, stop=True)
                        last.then_inc(grown, 1)
                        pe.wait_ge(masked, c + 1)
                        if c >= 1:
                            pe.wait_ge(carried, c)
                        for h in range(4):
                            out = p_out[:, c % 2, P * h:P * h + P]
                            last = pe.matmul(out, v[:, c, P * h:P * h + P], att[:, c % 2, P * h:P * h + P], start=True, stop=(c == 0))
                            if c:
                                last = pe.matmul(out, state[:, h // 2, P * (h % 2):P * (h % 2) + P], qdT[:, h // 2, tok], start=False, stop=True)
                        last.then_inc(made, 1)

                @block.scalar
                def _(act):
                    for c in range(QB):
                        act.wait_ge(made, c + 1)
                        act.copy(k.mixT[:, 0:4, c * P:c * P + P], p_out[:, c % 2, :].rearrange("p (h t) -> p h t", h=4)).then_inc(kept, 1)

                @block.vector
                def _(dve):
                    for c in range(QB):
                        dve.wait_ge(scored, c + 1)
                        if c >= 2:
                            dve.wait_ge(made, c - 1)
                        dve.tensor_tensor(att[:, c % 2, :], p_att[:, c % 2, :], k.c("ret_mask"), ALU.mult).then_inc(masked, 1)
                        dve.wait_ge(grown, c + 1)
                        dve.wait_ge(made, c + 1)
                        for h in range(4):
                            r, j = h % 2, h // 2
                            s = state[64 * r:64 * r + 64, j, P * r:P * r + P]
                            g = p_state[64 * r:64 * r + 64, c % 2, 256 * j + P * r:256 * j + P * r + P]
                            last = dve.scalar_tensor_tensor(s, s, float(np.exp(P * LOG_G[h])), g, ALU.mult, ALU.add)
                        last.then_inc(carried, 1)

                @block.sync
                def _(sp):
                    store = Loads(sp, stored)
                    sp.wait_ge(carried, QB)
                    for h in range(4):
                        r, j = h % 2, h // 2
                        store(k.p_ret[bass.ds(l, 1), 0, h].rearrange("a d e -> (a d) e"), state[64 * r:64 * r + 64, j, P * r:P * r + P])
                    store.wait()

        scored, masked, made, grown, spread, advanced, copied, stored = k.signals[:8]
        with ExitStack() as inner:
            sb2, ps2 = scope(nc, inner)
            att = sb2("ret_att_s", [NS, 4, NS])
            vx = [rot[0:NS, 2 * i:2 * i + 2, :].rearrange("p a (s e) -> p (a s) e", e=P) for i in range(2)]
            p_att = ps2("ret_ps_att", [NS, 512])
            p_out = ps2("ret_ps_out", [P, 512])
            p_state = ps2("ret_ps_state", [P, 2, 2, 512])
            with stage(nc, k.signals) as block:
                @block.tensor
                def _(pe):
                    for h in range(4):
                        last = pe.matmul(p_att[:, NS * h:NS * h + NS], kz[:, 2 * (h % 2) + h // 2, NP:NT], qT[:, h // 2, NP:NT], start=True, stop=True)
                    last.then_inc(scored, 1)
                    pe.wait_ge(masked, 1)
                    for h in range(4):
                        pe.matmul(p_out[:, NS * h:NS * h + NS], v[0:NS, QB, P * h:P * h + P], att[:, h, :], start=True, stop=False, skip_group_check=True)
                        for s in range(NB):
                            last = pe.matmul(p_out[:, NS * h + DS * s:NS * h + DS * s + DS], state_s[:, s, h // 2, :],
                                             qdz[:, h % 2, h // 2, DS * s:DS * s + DS], start=False, stop=(s == NB - 1), skip_group_check=True)
                    last.then_inc(made, 1)
                    for h in range(4):
                        pe.wait_ge(spread, h + 1)
                        if h >= 2:
                            pe.wait_ge(advanced, h - 1)
                        for q in range(2):
                            last = pe.matmul(p_state[:, h % 2, q, :], qk[0:NS, QB, 256 + P * (h // 2):384 + P * (h // 2)],
                                             vx[h % 2][:, 4 * q:4 * q + 4, :], start=True, stop=True)
                        last.then_inc(grown, 1)

                @block.scalar
                def _(act):
                    act.wait_ge(made, 1)
                    act.copy(k.mixT[:, 0:4, NP:NT], p_out[:, 0:4 * NS].rearrange("p (h t) -> p h t", h=4)).then_inc(copied, 1)

                @block.vector
                def _(dve):
                    dve.wait_ge(scored, 1)
                    dve.tensor_tensor(att[:, :, :], p_att[:, 0:4 * NS].rearrange("p (h t) -> p h t", h=4),
                                      k.c("ret_mask_s")[0:NS].rearrange("p (h t) -> p h t", h=4), ALU.mult).then_inc(masked, 1)
                    for h in range(5):
                        if h < 4:
                            if h >= 2:
                                dve.wait_ge(grown, h - 1)
                            dve.tensor_tensor(vx[h % 2], v[0:NS, QB, P * h:P * h + P].unsqueeze(1).to_broadcast([NS, NB, P]),
                                              k.c("seq_of")[0:NS].unsqueeze(2).to_broadcast([NS, NB, P]), ALU.mult).then_inc(spread, 1)
                        if h == 0:
                            dve.wait_ge(made, 1)
                            continue
                        g, r = h - 1, (h - 1) % 2
                        dve.wait_ge(grown, g + 1)
                        for q in range(2):
                            s = state_s[64 * r:64 * r + 64, 4 * q:4 * q + 4, g // 2, :]
                            last = dve.scalar_tensor_tensor(s, s, float(np.exp(DS * LOG_G[g])),
                                                            p_state[64 * r:64 * r + 64, g % 2, q, :].rearrange("p (s e) -> p s e", e=P), ALU.mult, ALU.add)
                        last.then_inc(advanced, 1)

                @block.sync
                def _(sp):
                    store = Loads(sp, stored)
                    sp.wait_ge(advanced, 4)
                    for s in range(NB):
                        for par in range(2):
                            store(k.s_ret[bass.ds(l, 1), s].rearrange("a (j b) d e -> a b d j e", b=2)[0, par], state_s[64 * par:64 * par + 64, s, :, :])
                    store.wait()

        head_norm(nc, k)
    gate(nc, k, 0, 8)


def head_norm(nc, k):
    squared, summed, scaled, powered, normed, logged = k.signals[:6]
    with ExitStack() as ctx:
        _, ps = scope(nc, ctx)
        sums = ps("hn_sums", [P, 2, 2, 512])
        with stage(nc, k.signals) as block:
            @block.scalar
            def _(act):
                for i in range(5):
                    if i >= 1:
                        act.wait_ge(scaled, 2 * i)
                        inverse_root(act, logged, k.scratch[:, (i - 1) % 2, :], at=i - 1).then_inc(powered, 1)
                    if i < 4:
                        if i >= 2:
                            act.wait_ge(normed, i - 1)
                        act.activation(k.scratch[:, i % 2, :], k.mixT[:, i, :], ACT.Square).then_inc(squared, 1)

            @block.tensor
            def _(pe):
                for i in range(4):
                    pe.wait_ge(squared, i + 1)
                    pe.matmul(sums[:, i % 2, 0, :], k.c("ones"), k.scratch[:, i % 2, 0:NP], start=True, stop=True)
                    pe.matmul(sums[:, i % 2, 1, 0:NS], k.c("ones"), k.scratch[:, i % 2, NP:NT], start=True, stop=True).then_inc(summed, 1)

            @block.vector
            def _(dve):
                for i in range(4):
                    r = k.scratch[:, i % 2, :]
                    dve.wait_ge(summed, i + 1)
                    dve.tensor_scalar(r[:, 0:NP], sums[:, i % 2, 0, :], 1.0 / P, EPS, ALU.mult, ALU.add).then_inc(scaled, 1)
                    dve.tensor_scalar(r[:, NP:NT], sums[:, i % 2, 1, 0:NS], 1.0 / P, EPS, ALU.mult, ALU.add).then_inc(scaled, 1)
                    dve.wait_ge(powered, i + 1)
                    dve.tensor_tensor(k.mixT[:, i, :], k.mixT[:, i, :], r, ALU.mult).then_inc(normed, 1)


def stick_breaking(nc, k, l):
    ft = k.ft
    with ExitStack() as ctx:
        sb, ps = scope(nc, ctx)
        kv = sb("sb_kv", [P, TT, 1024])
        jobs = []
        for a in range(TT):
            n, cols = tokens(a)
            for u in range(2):
                jobs.append(([ft[:, 4 + 4 * u + s, cols] for s in range(4)], [(lambda b, n=n: b[0:n, :], kv[0:n, a, 512 * u:512 * u + 512])]))
        turn(nc, k, "sb_in", jobs)

        scored, split, shrunk, logged, summed_up, weighted, exped, applied, kept, stored, own, stepped = k.signals[:12]
        units = [(h, b) for h in range(4) for b in range(QB)]
        starts = [sum(NP - P * c for c in range(b)) for b in range(QB + 1)]
        AREA = starts[QB]

        def blk(t, h, b, lo=0, hi=None):
            return t[:, h % 2, starts[b] + lo:(starts[b + 1] if hi is None else starts[b] + hi)]

        with ExitStack() as inner:
            sb2, ps2 = scope(nc, inner)
            mag = k.scratch
            low = sb2("sb_low", [P, 2, 512])
            logs = sb2("sb_logs", [P, 2, AREA])
            miss = sb2("sb_miss", [P, 2, AREA])
            p_z = ps2("sb_p_z", [P, 3, 512])
            p_after = ps2("sb_p_after", [P, 2, 512])
            p_out = ps2("sb_p_out", [P, 2, 512])
            with stage(nc, k.signals) as block:
                @block.sync
                def _(sp):
                    store = Loads(sp, stored)
                    for a in range(QB):
                        store(k.p_sb[bass.ds(l, 1), 0, a * P:a * P + P].rearrange("a t u h d -> (a t) (u h d)"), kv[:, a, :])
                    store(k.s_sb[bass.ds(l, 1)].rearrange("a n t u h d -> (a n t) (u h d)"), kv[0:NS, QB, :])
                    store.wait()

                @block.tensor
                def _(pe):
                    def scores(h):
                        for b in range(QB):
                            u = QB * h + b
                            if u >= 3:
                                pe.wait_ge(split, u - 2)
                            pe.matmul(p_z[:, u % 3, 0:NP - P * b], ft[:, 4 + h, P * b:P * b + P], ft[:, h, P * b:NP], start=True, stop=True).then_inc(scored, 1)

                    def after(h):
                        for b in range(QB):
                            u = QB * h + b
                            if b == 0:
                                pe.wait_ge(logged, QB * (h + 1))
                            if u >= 2:
                                pe.wait_ge(summed_up, u - 1)
                            out = p_after[:, u % 2, :]
                            last = pe.matmul(out[:, 0:NP - P * b], k.c("later"), blk(miss, h, b), start=True, stop=(b == QB - 1))
                            for c in range(b + 1, QB):
                                last = pe.matmul(out[:, P * (c - b):NP - P * b], k.c("ones"), blk(miss, h, c), start=False, stop=(c == QB - 1))
                            last.then_inc(weighted, 1)

                    def apply(h):
                        if h >= 2:
                            pe.wait_ge(kept, h - 1)
                        pe.wait_ge(exped, QB * (h + 1))
                        pe.wait_ge(own, h + 1)
                        for b in range(QB):
                            last = pe.matmul(p_out[:, h % 2, P * b:NP], kv[:, b, 512 + P * h:640 + P * h], blk(logs, h, b), start=(b == 0), stop=(b == QB - 1))
                        last.then_inc(applied, 1)

                    for h in range(4):
                        scores(h)
                        after(h)
                        if h >= 1:
                            apply(h - 1)
                    apply(3)

                @block.scalar
                def _(act):
                    def shrink(u):
                        h, b = units[u]
                        m = mag[:, u % 2, 0:NP - P * b]
                        act.wait_ge(split, u + 1)
                        act.activation(m, m, ACT.Exp, scale=-1.0).then_inc(shrunk, 1)
                        act.wait_ge(shrunk, 2 * u + 1)
                        act.activation(m, m, ACT.Ln, bias=1.0).then_inc(shrunk, 1)

                    def weights(u):
                        h, b = units[u]
                        w = blk(logs, h, b)
                        act.wait_ge(summed_up, u + 1)
                        act.activation(w, w, ACT.Exp).then_inc(exped, 1)

                    for h in range(4):
                        for b in range(QB):
                            shrink(QB * h + b)
                        for b in range(QB):
                            weights(QB * h + b)
                        if h >= 1:
                            act.wait_ge(applied, h)
                            act.copy(k.mixT[:, 4 + h - 1, 0:NP], p_out[:, (h - 1) % 2, :]).then_inc(kept, 1)
                    act.wait_ge(applied, 4)
                    act.copy(k.mixT[:, 7, 0:NP], p_out[:, 1, :]).then_inc(kept, 1)

                @block.gpsimd
                def _(pool):
                    for h in range(4):
                        pool.wait_ge(exped, QB * (h + 1))
                        for b in range(QB):
                            w = blk(logs, h, b, 0, P)
                            last = pool.tensor_tensor(w, w, k.c("before"), ALU.mult)
                        last.then_inc(own, 1)

                @block.vector
                def _(dve):
                    steps = Steps(dve, stepped)
                    for h in range(4):
                        for b in range(QB + 1):
                            if b < QB:
                                u, n = QB * h + b, NP - P * b
                                z = p_z[:, u % 3, 0:n]
                                if b == 0 and h >= 2:
                                    dve.wait_ge(applied, h - 1)
                                dve.wait_ge(scored, u + 1)
                                steps.then(dve.tensor_scalar(low[:, u % 2, 0:n], z, SB_SCALE, None, ALU.mult))
                                dve.scalar_tensor_tensor(mag[:, u % 2, 0:n], low[:, u % 2, 0:n], -1.0, low[:, u % 2, 0:n], ALU.mult, ALU.max).then_inc(split, 1)
                            if b >= 1:
                                u, n = QB * h + b - 1, NP - P * (b - 1)
                                x, g = blk(logs, h, b - 1), blk(miss, h, b - 1)
                                dve.wait_ge(shrunk, 2 * u + 2)
                                steps.then(dve.scalar_tensor_tensor(x, low[:, u % 2, 0:n], 0.0, mag[:, u % 2, 0:n], ALU.min, ALU.subtract))
                                steps.then(dve.tensor_tensor(g, x, low[:, u % 2, 0:n], ALU.subtract))
                                dve.tensor_tensor(g[:, 0:P], g[:, 0:P], k.c("before"), ALU.mult).then_inc(logged, 1)
                        for b in range(QB):
                            u, n = QB * h + b, NP - P * b
                            x = blk(logs, h, b)
                            dve.wait_ge(weighted, u + 1)
                            dve.tensor_tensor(x, x, p_after[:, u % 2, 0:n], ALU.add).then_inc(summed_up, 1)
        stick_samples(nc, k, l, kv)
    gate(nc, k, 4, 12)


def stick_samples(nc, k, l, kv):
    ft = k.ft
    COLS = 4 * NS
    cache = k.cache_sb_kv.rearrange("l n t u h d -> (l n) t u (h d)")
    with ExitStack() as ctx:
        sb, ps = scope(nc, ctx)
        pages = kv[:, 0:QB, :].rearrange("p (s u) (w x) -> p s (u w) x", s=2, w=2)
        keys = sb("sbs_keys", [P, 3, 4, P])
        low = sb("sbs_low", [P, 5, COLS])
        mag = sb("sbs_mag", [P, 5, COLS])
        logs = sb("sbs_logs", [P, 5, COLS])
        miss = sb("sbs_miss", [P, 5, COLS])
        p_keys = ps("sbs_p_keys", [P, 3, 512])
        p_z = ps("sbs_p_z", [P, 2, 512])
        p_after = ps("sbs_p_after", [P, 2, 512])
        p_out = ps("sbs_p_out", [P, 512])
        loaded, turned, copied_s, copied_v, scored = k.signals[0:2], *k.signals[2:6]

        def load_pages(sp, which, used, each):
            loads = [Loads(sp, s) for s in loaded]
            for s in range(NB):
                if s >= 2:
                    sp.wait_ge(used, each * (s - 1))
                for p in range(PAGES):
                    page = sp.value_load(k.pages[0:1, PAGES * s + p:PAGES * s + p + 1], min_val=0, max_val=POOL - 1)
                    loads[s % 2](pages[:, s % 2, p, :], cache[bass.ds(l * POOL + page, 1), :, which].rearrange("a t x -> (a t) x"))

        with stage(nc, k.signals) as block:
            @block.sync
            def _(sp):
                load_pages(sp, 0, turned, PAGES)

            @block.tensor
            def _(pe):
                units = [(s, p) for s in range(NB) for p in range(PAGES)]
                for h in range(4):
                    pe.matmul(p_z[0:NS, 1, NS * h:NS * h + NS], ft[:, 4 + h, NP:NT], ft[:, h, NP:NT], start=True, stop=True)
                for u in range(len(units) + 1):
                    if u < len(units):
                        s, p = units[u]
                        if p == 0:
                            pe.wait_ge(loaded[s % 2], 16 * PAGES * (s // 2 + 1))
                        if u >= 3:
                            before = u - 3
                            pe.wait_ge(copied_v if before % 2 == 0 else copied_s, before // 2 + 1)
                        for h in range(4):
                            last = pe.transpose(p_keys[:, u % 3, P * h:P * h + P], pages[:, s % 2, p, P * h:P * h + P], k.c("ident"))
                        last.then_inc(turned, 1)
                    if u >= 1:
                        b = u - 1
                        s, p = units[b]
                        pe.wait_ge(copied_v if b % 2 == 0 else copied_s, b // 2 + 1)
                        for h in range(4):
                            col = COLS * p + NS * h + DS * s
                            last = pe.matmul(p_z[:, 0, col:col + DS], keys[:, b % 3, h, :], ft[:, h, NP + DS * s:NP + DS * s + DS], start=True, stop=True)
                        last.then_inc(scored, 1)

            def copies(engine, copy, copied, odd):
                for u in range(odd, NB * PAGES, 2):
                    engine.wait_ge(turned, u + 1)
                    if u >= 3:
                        engine.wait_ge(scored, u - 2)
                    copy(keys[:, u % 3, :, :], p_keys[:, u % 3, :].rearrange("p (h t) -> p h t", h=4)).then_inc(copied, 1)

            @block.vector
            def _(dve):
                copies(dve, dve.tensor_copy, copied_v, 0)

            @block.scalar
            def _(act):
                copies(act, act.copy, copied_s, 1)

        scaled, shrunk, missed, summed, weighted, done = k.signals[:6]
        paged = lambda t: t[:, 0:4, :]
        new = lambda t: t[0:NS, 4, :]
        z = (p_z[:, 0, :].rearrange("p (g c) -> p g c", g=4), p_z[0:NS, 1, 0:COLS])
        both = (paged, new)
        with stage(nc, k.signals) as block:
            @block.vector
            def _(dve):
                step = Steps(dve, done)
                for i, part in enumerate(both):
                    step.then(dve.tensor_scalar(part(low), z[i], SB_SCALE, None, ALU.mult))
                    dve.scalar_tensor_tensor(part(mag), part(low), -1.0, part(low), ALU.mult, ALU.max).then_inc(scaled, 1)
                for i, part in enumerate(both):
                    dve.wait_ge(shrunk, 2 * i + 2)
                    step.then(dve.scalar_tensor_tensor(part(logs), part(low), 0.0, part(mag), ALU.min, ALU.subtract))
                    last = dve.tensor_tensor(part(miss), part(logs), part(low), ALU.subtract)
                    if i == 0:
                        last.then_inc(missed, 1)
                    else:
                        step.then(last)
                m = k.c("before_s")[0:NS].unsqueeze(1).to_broadcast([NS, 4, NS])
                g = new(miss).rearrange("p (h q) -> p h q", h=4)
                dve.tensor_tensor(g, g, m, ALU.mult).then_inc(missed, 1)
                dve.wait_ge(summed, 1)
                dve.tensor_tensor(paged(logs), paged(logs), p_after[:, 0, :].rearrange("p (g c) -> p g c", g=4), ALU.add).then_inc(weighted, 1)
                dve.tensor_tensor(new(logs), new(logs), p_after[0:NS, 1, 0:COLS], ALU.add).then_inc(weighted, 1)
                dve.wait_ge(shrunk, 6)
                g = new(logs).rearrange("p (h q) -> p h q", h=4)
                dve.tensor_tensor(g, g, m, ALU.mult)

            @block.scalar
            def _(act):
                for i, part in enumerate(both):
                    act.wait_ge(scaled, i + 1)
                    act.activation(part(mag), part(mag), ACT.Exp, scale=-1.0).then_inc(shrunk, 1)
                    act.wait_ge(shrunk, 2 * i + 1)
                    act.activation(part(mag), part(mag), ACT.Ln, bias=1.0).then_inc(shrunk, 1)
                for i, part in enumerate(both):
                    act.wait_ge(weighted, i + 1)
                    act.activation(part(logs), part(logs), ACT.Exp).then_inc(shrunk, 1)

            @block.tensor
            def _(pe):
                pe.wait_ge(missed, 2)
                for p in range(PAGES):
                    out = p_after[:, 0, COLS * p:COLS * p + COLS]
                    pe.matmul(out, k.c("later"), miss[:, p, :], start=True, stop=False)
                    for q in range(p + 1, PAGES):
                        pe.matmul(out, k.c("ones"), miss[:, q, :], start=False, stop=False)
                    pe.matmul(out, k.c("ones")[0:NS], new(miss), start=False, stop=True)
                pe.matmul(p_after[0:NS, 1, 0:COLS], k.c("later")[0:NS, 0:NS], new(miss), start=True, stop=True).then_inc(summed, 1)

        applied, kept = k.signals[2:4]
        with stage(nc, k.signals) as block:
            @block.sync
            def _(sp):
                load_pages(sp, 1, applied, 1)

            @block.tensor
            def _(pe):
                for h in range(4):
                    pe.matmul(p_out[:, NS * h:NS * h + NS], kv[0:NS, QB, 512 + P * h:640 + P * h], new(logs)[:, NS * h:NS * h + NS],
                              start=(h == 0), stop=False, skip_group_check=True)
                for s in range(NB):
                    pe.wait_ge(loaded[s % 2], 16 * PAGES * (s // 2 + 1))
                    for p in range(PAGES):
                        for h in range(4):
                            col = slice(NS * h + DS * s, NS * h + DS * s + DS)
                            last = pe.matmul(p_out[:, col], pages[:, s % 2, p, P * h:P * h + P], logs[:, p, col], start=False, stop=(p == PAGES - 1), skip_group_check=True)
                    last.then_inc(applied, 1)

            @block.scalar
            def _(act):
                act.wait_ge(applied, NB)
                act.copy(k.mixT[:, 4:8, NP:NT], p_out[:, 0:COLS].rearrange("p (h t) -> p h t", h=4))


def take_top(dve, step, rounds, top, score, work):
    for r in range(rounds):
        src = score if r == 0 else work
        step.then(dve.max(top, src))
        step.then(dve.match_replace(work, top, src, NEG))


def sparse_attention(nc, k, l):
    ft = k.ft
    with ExitStack() as ctx:
        sb, ps = scope(nc, ctx)
        tm = sb("dsa_tm", [P, TT, DSA_W + 8])
        ikz = sb("dsa_ikz", [P, 2, NP])
        jobs = []
        for a in range(TT):
            n, cols = tokens(a)
            jobs.append(([ft[:, 4, cols], ft[:, 5, cols]], [(lambda b, n=n: b[0:n, 0:256], tm[0:n, a, 0:256])]))
            jobs.append(([ft[0:64, 6, cols], ft[0:8, 11, cols]], [(lambda b, n=n: b[0:n, 0:72], tm[0:n, a, 256:328])]))
        turn(nc, k, "dsa_in", jobs)

        stored, cleared, weighed = k.signals[:3]
        with stage(nc, k.signals) as block:
            @block.sync
            def _(sp):
                store = Loads(sp, stored)
                store(k.p_dsa[bass.ds(l, 1), 0].rearrange("a (n p) w -> p (a n) w", p=P), tm[:, 0:QB, 0:DSA_W])
                store(k.s_dsa[bass.ds(l, 1)].rearrange("a n t w -> (a n t) w"), tm[0:NS, QB, 0:DSA_W])
                store.wait()

            @block.gpsimd
            def _(pool):
                pool.memset(ikz[64:128, 0, :], 0.0)
                pool.memset(ikz[0:64, 1, :], 0.0)

            @block.vector
            def _(dve):
                for r in range(2):
                    dve.tensor_copy(ikz[64 * r:64 * r + 64, r, :], ft[64 * r:64 * r + 64, 6, 0:NP])
                dve.tensor_scalar(tm[:, 0:QB, 320:328], tm[:, 0:QB, 320:328], 8 ** -0.5, None, ALU.mult)
                dve.tensor_scalar(tm[0:NS, QB, 320:328], tm[0:NS, QB, 320:328], 8 ** -0.5, None, ALU.mult)

        sparse_prompt(nc, k, tm, ikz)
        sparse_samples(nc, k, l, tm)
    gate(nc, k, 8, 12)


def sparse_prompt(nc, k, tm, ikz):
    ft = k.ft
    with ExitStack() as ctx:
        sb, ps = scope(nc, ctx)
        rel = sb("dsa_rel", [P, 2, 512])
        score = sb("dsa_score", [P, 512])
        work = sb("dsa_work", [P, 512])
        top = sb("dsa_top", [P, 8])
        neg = sb("dsa_neg_row", [P, 2, 512])
        prob = sb("dsa_prob", [P, 2, 512])
        probT = sb("dsa_probT", [P, 2, 512])
        small = sb("dsa_small", [P, 2, 4])
        p_rel = ps("dsa_p_rel", [P, 2, 512])
        p_log = ps("dsa_p_log", [P, 2, 512])
        p_T = ps("dsa_p_T", [P, 2, 512])
        p_out = ps("dsa_p_out", [P, 2, 512])
        multiplied, rectified, added, looked, biased, exped, normed, turned, copied, applied, kept, own = k.signals[:12]
        with stage(nc, k.signals) as block:
            @block.tensor
            def _(pe):
                def index(q):
                    for h in range(8):
                        u = 8 * q + h
                        if u >= 2:
                            pe.wait_ge(rectified, u - 1)
                        pe.matmul(p_rel[:, u % 2, 0:P * (q + 1)], ft[:, 7 + h // 2, P * q:P * q + P], ikz[:, h % 2, 0:P * (q + 1)],
                                  start=True, stop=True).then_inc(multiplied, 1)

                for q in range(QB):
                    index(q)
                    for h in range(5):
                        u = 4 * q + h
                        if h < 4:
                            if u >= 2:
                                pe.wait_ge(biased, u - 1)
                            pe.matmul(p_log[:, u % 2, 0:P * (q + 1)], ft[:, h, P * q:P * q + P], ft[:, 4, 0:P * (q + 1)],
                                      start=True, stop=True).then_inc(looked, 1)
                        if h >= 1:
                            v = u - 1
                            pe.wait_ge(normed, v + 1)
                            if v >= 2:
                                pe.wait_ge(copied, v - 1)
                            for b in range(q + 1):
                                last = pe.transpose(p_T[:, v % 2, P * b:P * b + P], prob[:, v % 2, P * b:P * b + P], k.c("ident"))
                            last.then_inc(turned, 1)
                            pe.wait_ge(copied, v + 1)
                            if v >= 2:
                                pe.wait_ge(kept, v - 1)
                            for b in range(q + 1):
                                last = pe.matmul(p_out[:, v % 2, 0:P], tm[:, b, P:2 * P], probT[:, v % 2, P * b:P * b + P], start=(b == 0), stop=(b == q))
                            last.then_inc(applied, 1)

            @block.scalar
            def _(act):
                def rectify(q):
                    for h in range(8):
                        u = 8 * q + h
                        act.wait_ge(multiplied, u + 1)
                        if u >= 2:
                            act.wait_ge(added, u - 1)
                        act.activation(rel[:, u % 2, 0:P * (q + 1)], p_rel[:, u % 2, 0:P * (q + 1)], ACT.Relu, scale=0.125).then_inc(rectified, 1)

                for q in range(QB):
                    w = P * (q + 1)
                    rectify(q)
                    for h in range(5):
                        u = 4 * q + h
                        if h < 4:
                            act.wait_ge(biased, u + 1)
                            act.activation(prob[:, u % 2, 0:w], prob[:, u % 2, 0:w], ACT.Exp, bias=small[:, u % 2, 0:1],
                                           accum_out=small[:, u % 2, 1:2]).then_inc(exped, 1)
                        if h >= 1:
                            v = u - 1
                            act.wait_ge(turned, v + 1)
                            if v >= 2:
                                act.wait_ge(applied, v - 1)
                            act.copy(probT[:, v % 2, 0:w], p_T[:, v % 2, 0:w]).then_inc(copied, 1)
                            act.wait_ge(applied, v + 1)
                            act.copy(k.mixT[:, 8 + h - 1, P * q:P * q + P], p_out[:, v % 2, 0:P]).then_inc(kept, 1)

            @block.vector
            def _(dve):
                step = Steps(dve, own)
                for q in range(QB):
                    w = P * (q + 1)
                    s = score[:, 0:w]
                    for h in range(8):
                        u = 8 * q + h
                        dve.wait_ge(rectified, u + 1)
                        g = tm[:, q, 320 + h:321 + h]
                        if h == 0:
                            last = dve.tensor_scalar(s, rel[:, u % 2, 0:w], g, None, ALU.mult)
                        else:
                            last = dve.scalar_tensor_tensor(s, rel[:, u % 2, 0:w], g, s, ALU.mult, ALU.add)
                        last.then_inc(added, 1)
                        dve.wait_ge(added, u + 1)
                    d = score[:, P * q:w]
                    n = neg[:, q % 2, 0:w]
                    if q == 0:
                        step.then(dve.tensor_copy(n, k.c("dsa_neg")))
                    else:
                        step.then(dve.tensor_tensor(d, d, k.c("dsa_neg"), ALU.add))
                        take_top(dve, step, TOPK // 8, top[:, :], s, work[:, 0:w])
                        step.then(dve.tensor_tensor(n, work[:, 0:w], s, ALU.is_equal))
                        step.then(dve.tensor_scalar(n, n, NEG, None, ALU.mult))
                    for h in range(5):
                        u = 4 * q + h
                        if h < 4:
                            p, m = prob[:, u % 2, 0:w], small[:, u % 2, 0:1]
                            dve.wait_ge(looked, u + 1)
                            if u >= 2:
                                dve.wait_ge(turned, u - 1)
                            step.then(dve.scalar_tensor_tensor(p, p_log[:, u % 2, 0:w], SB_SCALE, n, ALU.mult, ALU.add))
                            dve.tensor_reduce(m, p, AX.X, ALU.max, negate=True).then_inc(biased, 1)
                        if h >= 1:
                            v = u - 1
                            dve.wait_ge(exped, v + 1)
                            step.then(dve.reciprocal(small[:, v % 2, 2:3], small[:, v % 2, 1:2]))
                            dve.tensor_scalar(prob[:, v % 2, 0:w], prob[:, v % 2, 0:w], small[:, v % 2, 2:3], None, ALU.mult).then_inc(normed, 1)


def sparse_samples(nc, k, l, tm):
    ft = k.ft
    WIDE = PAST + NS
    cache = k.cache_dsa.rearrange("l n t w -> (l n) t w")
    with ExitStack() as ctx:
        sb, ps = scope(nc, ctx)
        iq = sb("dss_iq", [P, NB, 2, 4, DS])
        qs = sb("dss_q", [P, NB, 4, NS])
        wv = sb("dss_wv", [NS, NB])
        wx = sb("dss_wx", [NS, NB, P])
        stored, loaded, own, zeroed = k.signals[:4]
        with stage(nc, k.signals) as block:
            @block.sync
            def _(sp):
                sp.dma_start(k.sample_w, tm[0:NS, QB, 320:328]).then_inc(stored, 16)
                sp.wait_ge(stored, 16)
                load = Loads(sp, loaded)
                for r in range(2):
                    for j in range(4):
                        load(wv[16 * r + 4 * j:16 * r + 4 * j + 4, :], k.sample_w.rearrange("(s t) h -> h t s", t=DS)[2 * j + r])

            @block.gpsimd
            def _(pool):
                pool.memset(iq[:, :, :, :, :], 0.0)
                pool.memset(qs[:, :, :, :], 0.0).then_inc(zeroed, 1)

            @block.vector
            def _(dve):
                dve.wait_ge(zeroed, 1)
                for s in range(NB):
                    tok = slice(NP + DS * s, NP + DS * s + DS)
                    for r in range(2):
                        dve.tensor_copy(iq[64 * r:64 * r + 64, s, r, :, :], ft[64 * r:64 * r + 64, 7:11, tok])
                    dve.tensor_copy(qs[:, s, :, DS * s:DS * s + DS], ft[:, 0:4, tok])
                dve.wait_ge(loaded, 16 * 8)
                dve.tensor_tensor(wx[:, :, :], k.c("spread")[0:NS].rearrange("p (s c) -> p s c", s=NB),
                                  wv[:, :].unsqueeze(2).to_broadcast([NS, NB, P]), ALU.mult)

        with ExitStack() as inner:
            sb2, ps2 = scope(nc, inner)
            score = sb2("dss_score", [P, WIDE])
            logit = sb2("dss_logit", [P, WIDE])
            with ExitStack() as first:
                sb3, ps3 = scope(nc, first)
                pages = sb3("dss_pages", [P, 2, PAGES, DSA_W + 64])
                keys = sb3("dss_keys", [P, 2, PAST])
                ikeys = sb3("dss_ikeys", [P, 2, PAST])
                rel = k.scratch[0:NS]
                p_keys, p_ikeys, p_rel, p_reln, p_score, p_scoren, p_log = (ps3(f"dss_p{i}", [P, 512]) for i in range(7))
                loaded0, loaded1, turned, copied_v, copied_s, related, rectified, summed, looked, out = k.signals[:10]
                with stage(nc, k.signals) as block:
                    @block.sync
                    def _(sp):
                        loads = [Loads(sp, loaded0), Loads(sp, loaded1)]
                        for s in range(NB):
                            if s >= 2:
                                sp.wait_ge(turned, s - 1)
                            for p in range(PAGES):
                                page = sp.value_load(k.pages[0:1, PAGES * s + p:PAGES * s + p + 1], min_val=0, max_val=POOL - 1)
                                row = cache[bass.ds(l * POOL + page, 1)].rearrange("a t w -> (a t) w")
                                loads[s % 2](pages[:, s % 2, p, 0:DSA_W], row)
                                loads[s % 2](pages[:, s % 2, p, DSA_W:DSA_W + 64], row[:, 256:DSA_W])

                    @block.tensor
                    def _(pe):
                        for s in range(NB):
                            pe.wait_ge((loaded0, loaded1)[s % 2], 16 * 2 * PAGES * (s // 2 + 1))
                            if s >= 1:
                                pe.wait_ge(copied_v, s)
                                pe.wait_ge(copied_s, s)
                            for p in range(PAGES):
                                pe.transpose(p_keys[:, P * p:P * p + P], pages[:, s % 2, p, 0:P], k.c("ident"))
                                last = pe.transpose(p_ikeys[:, P * p:P * p + P], pages[:, s % 2, p, 256:384], k.c("ident"))
                            last.then_inc(turned, 1)
                            pe.wait_ge(copied_v, s + 1)
                            pe.wait_ge(copied_s, s + 1)
                            if s >= 1:
                                pe.wait_ge(rectified, 2 * s)
                            mine = iq[:, s].rearrange("p r j t -> p (r j t)")
                            pe.matmul(p_rel[0:NS, :], mine, ikeys[:, s % 2, :], start=True, stop=True)
                            pe.matmul(p_reln[0:NS, 0:NS], mine, ft[:, 6, NP:NT], start=True, stop=True).then_inc(related, 1)
                            pe.matmul(p_log[:, :], qs[:, s].rearrange("p h c -> p (h c)"), keys[:, s % 2, :], start=(s == 0), stop=(s == NB - 1)).then_inc(looked, 1)
                            pe.wait_ge(rectified, 2 * s + 2)
                            pe.matmul(p_score[:, :], wx[:, s, :], rel[:, s % 2, 0:PAST], start=(s == 0), stop=(s == NB - 1))
                            pe.matmul(p_scoren[:, 0:NS], wx[:, s, :], rel[:, s % 2, PAST:WIDE], start=(s == 0), stop=(s == NB - 1)).then_inc(summed, 1)
                        for s in range(NB):
                            last = pe.matmul(p_reln[:, 0:NS], qs[:, s].rearrange("p h c -> p (h c)"), ft[:, 4, NP:NT], start=(s == 0), stop=(s == NB - 1))
                        last.then_inc(summed, 1)

                    @block.vector
                    def _(dve):
                        for s in range(NB):
                            dve.wait_ge(turned, s + 1)
                            if s >= 2:
                                dve.wait_ge(looked, s - 1)
                            dve.tensor_copy(keys[:, s % 2, :], p_keys[:, :]).then_inc(copied_v, 1)
                        dve.wait_ge(summed, NB + 1)
                        dve.tensor_copy(score[:, 0:PAST], p_score[:, :])
                        dve.tensor_tensor(score[:, PAST:WIDE], p_scoren[:, 0:NS], k.c("dsa_neg_s"), ALU.add)
                        dve.tensor_scalar(logit[:, PAST:WIDE], p_reln[:, 0:NS], SB_SCALE, None, ALU.mult)

                    @block.scalar
                    def _(act):
                        for s in range(NB):
                            act.wait_ge(turned, s + 1)
                            if s >= 2:
                                act.wait_ge(related, s - 1)
                            act.copy(ikeys[:, s % 2, :], p_ikeys[:, :]).then_inc(copied_s, 1)
                            act.wait_ge(related, s + 1)
                            if s >= 2:
                                act.wait_ge(summed, s - 1)
                            act.activation(rel[:, s % 2, 0:PAST], p_rel[0:NS, :], ACT.Relu, scale=0.125).then_inc(rectified, 1)
                            act.activation(rel[:, s % 2, PAST:WIDE], p_reln[0:NS, 0:NS], ACT.Relu, scale=0.125).then_inc(rectified, 1)
                        act.wait_ge(looked, NB)
                        act.activation(logit[:, 0:PAST], p_log[:, :], ACT.Copy, scale=SB_SCALE)

            PAD = 7
            work = sb2("dss_work", [P, WIDE + PAD])
            top = sb2("dss_top", [P, 2, 8])
            small = sb2("dss_small", [P, 4])
            probT = sb2("dss_probT", [P, 5, P])
            vals = sb2("dss_vals", [P, 2, PAGES, P])
            p_T = ps2("dss_p_T", [P, 512])
            p_Tn = ps2("dss_p_Tn", [P, 512])
            p_out = ps2("dss_p_out", [P, 512])
            own, biased, exped, normed, turned, copied, loaded0, loaded1, applied = k.signals[:9]
            with stage(nc, k.signals) as block:
                @block.sync
                def _(sp):
                    loads = [Loads(sp, loaded0), Loads(sp, loaded1)]
                    for s in range(NB):
                        if s >= 2:
                            sp.wait_ge(applied, s - 1)
                        for p in range(PAGES):
                            page = sp.value_load(k.pages[0:1, PAGES * s + p:PAGES * s + p + 1], min_val=0, max_val=POOL - 1)
                            loads[s % 2](vals[:, s % 2, p, :], cache[bass.ds(l * POOL + page, 1)].rearrange("a t w -> (a t) w")[:, P:2 * P])

                @block.vector
                def _(dve):
                    step = Steps(dve, own)
                    take_top(dve, step, TOPK_S // 8, top[:, 0, :], score[:, :], work[:, 0:WIDE])
                    step.then(dve.max(top[:, 0, :], work[:, 0:WIDE]))
                    dve.memset(top[:, 1, 0:PAD], -NEG)
                    step(dve.memset(work[:, WIDE:WIDE + PAD], -NEG))
                    step.then(dve.tensor_copy(top[:, 1, PAD:8], top[:, 0, 0:1]))
                    step.then(dve.match_replace(work[:, :], top[:, 1, :], work[:, :], NEG))
                    step.then(dve.tensor_tensor(work[:, 0:WIDE], work[:, 0:WIDE], score[:, :], ALU.is_equal))
                    step.then(dve.scalar_tensor_tensor(logit[:, :], work[:, 0:WIDE], NEG, logit[:, :], ALU.mult, ALU.add))
                    dve.tensor_reduce(small[:, 0:1], logit[:, :], AX.X, ALU.max, negate=True).then_inc(biased, 1)
                    dve.wait_ge(exped, 1)
                    step.then(dve.reciprocal(small[:, 2:3], small[:, 1:2]))
                    dve.tensor_scalar(logit[:, :], logit[:, :], small[:, 2:3], None, ALU.mult).then_inc(normed, 1)
                    dve.wait_ge(turned, 1)
                    dve.tensor_copy(probT[:, 0:4, :], p_T[:, :].rearrange("p (g c) -> p g c", g=4)).then_inc(copied, 1)
                    dve.tensor_copy(probT[0:NS, 4, :], p_Tn[0:NS, 0:P]).then_inc(copied, 1)

                @block.scalar
                def _(act):
                    act.wait_ge(biased, 1)
                    act.activation(logit[:, :], logit[:, :], ACT.Exp, bias=small[:, 0:1], accum_out=small[:, 1:2]).then_inc(exped, 1)
                    act.wait_ge(applied, NB)
                    act.copy(k.mixT[:, 8:12, NP:NT], p_out[:, 0:P].rearrange("p (h t) -> p h t", h=4))

                @block.tensor
                def _(pe):
                    pe.wait_ge(normed, 1)
                    for g in range(4):
                        pe.transpose(p_T[:, P * g:P * g + P], logit[:, P * g:P * g + P], k.c("ident"))
                    pe.transpose(p_Tn[0:NS, 0:P], logit[:, PAST:WIDE], k.c("ident")).then_inc(turned, 1)
                    pe.wait_ge(copied, 2)
                    pe.matmul(p_out[:, 0:P], tm[0:NS, QB, P:2 * P], probT[0:NS, 4, :], start=True, stop=False, skip_group_check=True)
                    for s in range(NB):
                        pe.wait_ge((loaded0, loaded1)[s % 2], 16 * PAGES * (s // 2 + 1))
                        for p in range(PAGES):
                            def mine(t):
                                return t.rearrange("p (h c) -> p h c", h=4)[:, :, DS * s:DS * s + DS]
                            last = pe.matmul(mine(p_out[:, 0:P]), vals[:, s % 2, p, :], mine(probT[:, p, :]), start=False, stop=(p == PAGES - 1), skip_group_check=True)
                        last.then_inc(applied, 1)


R_SLOT, WL_SLOT, K_SLOT, V_SLOT, AL_SLOT, RG_SLOT = 0, 4, 5, 9, 13, 14
SHIFT_RUNS = ((0, 4, P, 0), (4, 1, LORA, 512), (5, 4, P, 608), (9, 4, P, 1120), (13, 1, LORA, 1632))
HALF = 32
KK_SCALE = 2.0 ** 20


def rwkv(nc, k, l):
    with ExitStack() as ctx:
        sb, _ = scope(nc, ctx)
        k.bonus = sb("rw_bonus", [P, 4, NT])
        k.kr = sb("rw_kr", [P, 4, NC, 2, C])
        k.bk = sb("rw_bk", [P, 4, NC, 2, C])
        k.ends = sb("rw_ends", [P, 4, NC])
        token_shift(nc, k, l)
        with ExitStack() as inner:
            rwkv_vectors(nc, k, l, inner)
            store_sample_rows(nc, k)
        rwkv_chunks(nc, k, l)
        rwkv_out(nc, k)
    gate(nc, k, 12, RG_SLOT)


def token_shift(nc, k, l):
    ft = k.ft
    with ExitStack() as ctx:
        sb, _ = scope(nc, ctx)
        rows = sb("ts_rows", [NB, SHIFT_W])
        last_p = sb("ts_last_p", [1, SHIFT_W])
        last_s = sb("ts_last_s", [NB, SHIFT_W])
        first = sb("ts_first", [P, 14, NB])
        diff = sb("ts_diff", [P, 4, NT])
        loaded, stepped = k.signals[:2]
        with stage(nc, k.signals) as block:
            @block.sync
            def _(sp):
                sp.dma_start(rows[:, :], k.state_shift[bass.ds(l, 1)].rearrange("a n w -> (a n) w")).then_inc(loaded, 16)
                sp.wait_ge(loaded, 16)
        jobs = []
        for slot, count, w, col in SHIFT_RUNS:
            jobs.append(([rows[:, col + w * i:col + w * i + w] for i in range(count)],
                         [(lambda b, w=w, n=count: b[0:w, 0:NB * n].rearrange("p (i s) -> p i s", s=NB), first[0:w, slot:slot + count, :])]))
        width = {s: (LORA if s in (WL_SLOT, AL_SLOT) else P) for s in range(14)}
        at = 0
        for slots in (range(0, 4), range(4, 8), range(8, 12), range(12, 14)):
            w = sum(width[s] for s in slots)
            jobs.append(([ft[0:width[s], s, NP - 1:NP] for s in slots], [(lambda b, w=w: b[0:1, 0:w], last_p[:, at:at + w])]))
            jobs.append(([ft[0:width[s], s, NP + DS - 1:NT:DS] for s in slots], [(lambda b, w=w: b[0:NB, 0:w], last_s[:, at:at + w])]))
            at += w
        turn(nc, k, "ts", jobs)
        with stage(nc, k.signals) as block:
            @block.sync
            def _(sp):
                store = Loads(sp, loaded)
                store(k.p_shift[bass.ds(l, 1)].rearrange("a n w -> (a n) w"), last_p[:, :])
                store(k.s_shift[bass.ds(l, 1)].rearrange("a n w -> (a n) w"), last_s[:, :])
                store.wait()

            @block.vector
            def _(dve):
                step = Steps(dve, stepped)
                for slot, n, w, col in SHIFT_RUNS:
                    x, d = ft[0:w, slot:slot + n, :], diff[0:w, 0:n, :]
                    seqs = lambda t, i: t[:, i, NP:NT].rearrange("p (s t) -> p s t", t=DS)
                    dve.tensor_tensor(d[:, :, 1:NP], x[:, :, 0:NP - 1], x[:, :, 1:NP], ALU.subtract)
                    dve.tensor_scalar(d[:, :, 0:1], x[:, :, 0:1], -1.0, None, ALU.mult)
                    for i in range(n):
                        dve.tensor_tensor(seqs(d, i)[:, :, 1:DS], seqs(x, i)[:, :, 0:DS - 1], seqs(x, i)[:, :, 1:DS], ALU.subtract)
                        last = dve.tensor_tensor(seqs(d, i)[:, :, 0], first[0:w, slot + i, :], seqs(x, i)[:, :, 0], ALU.subtract)
                    step.then(last)
                    for i in range(n):
                        last = dve.scalar_tensor_tensor(x[:, i, :], d[:, i, :], k.prm[0:w, ROW_MU + slot + i:ROW_MU + slot + i + 1], x[:, i, :], ALU.mult, ALU.add)
                    step.then(last)


def rwkv_vectors(nc, k, l, outer):
    ft = k.ft
    sb, _ = scope(nc, outer)
    logw = sb("rv_logw", [P, 4, NT])
    beta = sb("rv_beta", [P, 4, NT])
    kap = sb("rv_kap", [P, 4, NT])
    lora = sb("rv_lora", [LORA, 2, GW])
    minus = sb("rv_minus", [P, 8])
    with ExitStack() as ctx:
        sb2, ps = scope(nc, ctx)
        tmp = sb2("rv_tmp", [P, 2, NT])
        prod = ps("rv_prod", [P, 2, 2, 512])
        loaded, negated, doubled, stepped, opened, multiplied, halved = k.signals[:7]
        th = ft[0:LORA, WL_SLOT, :]
        with stage(nc, k.signals) as block:
            @block.sync
            def _(sp):
                load = Loads(sp, loaded)
                load(lora[:, 0, :], k.rw_w2[bass.ds(l, 1)].rearrange("a r c -> (a r) c"))
                load(lora[:, 1, :], k.rw_a2[bass.ds(l, 1)].rearrange("a r c -> (a r) c"))

            @block.scalar
            def _(act):
                act.activation(th, th, ACT.Exp, scale=2.0).then_inc(doubled, 1)
                act.wait_ge(negated, 2)
                for u in range(8):
                    act.wait_ge(multiplied, u + 1)
                    out, i = (logw, beta)[u % 2], u // 2
                    bias = minus[:, 4 * (u % 2) + i:4 * (u % 2) + i + 1]
                    act.activation(out[:, i, 0:NP], prod[:, u % 2, 0, :], ACT.Exp, scale=-1.0, bias=bias).then_inc(opened, 1)
                    act.activation(out[:, i, NP:NT], prod[:, u % 2, 1, 0:NS], ACT.Exp, scale=-1.0, bias=bias).then_inc(opened, 1)

            @block.tensor
            def _(pe):
                pe.wait_ge(loaded, 32)
                pe.wait_ge(halved, 1)
                for u in range(8):
                    if u >= 2:
                        pe.wait_ge(opened, 2 * (u - 1))
                    x = ft[0:LORA, (WL_SLOT, AL_SLOT)[u % 2], :]
                    w = lora[:, u % 2, P * (u // 2):P * (u // 2) + P]
                    pe.matmul(prod[:, u % 2, 0, :], w, x[:, 0:NP], start=True, stop=True)
                    pe.matmul(prod[:, u % 2, 1, 0:NS], w, x[:, NP:NT], start=True, stop=True).then_inc(multiplied, 1)

            @block.vector
            def _(dve):
                step = Steps(dve, stepped)
                dve.tensor_scalar(minus[:, 0:4], k.prm[:, ROW_W0:ROW_W0 + 4], -1.0, None, ALU.mult).then_inc(negated, 1)
                dve.tensor_scalar(minus[:, 4:8], k.prm[:, ROW_A0:ROW_A0 + 4], -1.0, None, ALU.mult).then_inc(negated, 1)
                dve.wait_ge(doubled, 1)
                step.then(dve.tensor_scalar(th, th, 1.0, None, ALU.add))
                step.then(dve.reciprocal(th, th))
                dve.tensor_scalar(th, th, -2.0, 1.0, ALU.mult, ALU.add).then_inc(halved, 1)
                for u in range(8):
                    x = (logw, beta)[u % 2][:, u // 2, :]
                    dve.wait_ge(opened, 2 * u + 2)
                    step.then(dve.tensor_scalar(x, x, 1.0, None, ALU.add))
                    step.then(dve.reciprocal(x, x))
                    if u % 2 == 0:
                        step.then(dve.tensor_scalar(x, x, -float(np.exp(-0.5)), None, ALU.mult))

        def col(row, i):
            return k.prm[:, row + i:row + i + 1]

        squared, summed, bounded, inverted, stepped, logged = k.signals[:6]
        with stage(nc, k.signals) as block:
            @block.vector
            def _(dve):
                step = Steps(dve, stepped)
                for i in range(4):
                    kx, t, z = ft[:, K_SLOT + i, :], tmp[:, 0, :], tmp[:, 1, :]
                    step.then(dve.tensor_scalar(kap[:, i, :], kx, col(ROW_KK, i), None, ALU.mult))
                    dve.tensor_tensor(t, kap[:, i, :], kap[:, i, :], ALU.mult).then_inc(squared, 1)
                    step.then(dve.tensor_scalar(z, beta[:, i, :], -1.0, col(ROW_KA, i), ALU.add, ALU.mult))
                    step.then(dve.scalar_tensor_tensor(kx, z, 1.0, kx, ALU.add, ALU.mult))
                    step.then(dve.scalar_tensor_tensor(z, ft[:, R_SLOT + i, :], col(ROW_RK, i), kx, ALU.mult, ALU.mult))
                    dve.wait_ge(summed, 2 * i + 1)
                    for a, b, part in ((0, NP, 0), (NP, NT, 1)):
                        dve.tensor_scalar(t[:, a:b], prod[:, 0, part, 0:b - a], 1e-24, None, ALU.max).then_inc(bounded, 1)
                    dve.wait_ge(inverted, i + 1)
                    step.then(dve.scalar_tensor_tensor(kap[:, i, :], kap[:, i, :], -KK_SCALE ** 0.5, t, ALU.mult, ALU.mult))
                    step.then(dve.scalar_tensor_tensor(beta[:, i, :], kap[:, i, :], -1.0, beta[:, i, :], ALU.mult, ALU.mult))
                    dve.wait_ge(summed, 2 * i + 2)
                    for a, b, part in ((0, NP, 0), (NP, NT, 1)):
                        last = dve.tensor_tensor(k.bonus[:, i, a:b], prod[:, 1, part, 0:b - a], ft[:, V_SLOT + i, a:b], ALU.mult)
                    step.then(last)

            @block.tensor
            def _(pe):
                for i in range(4):
                    for u in range(2):
                        if u == 0:
                            pe.wait_ge(squared, i + 1)
                        else:
                            pe.wait_ge(stepped, 7 * i + 4)
                        pe.matmul(prod[:, u, 0, :], k.c("head_ones"), tmp[:, u, 0:NP], start=True, stop=True)
                        pe.matmul(prod[:, u, 1, 0:NS], k.c("head_ones"), tmp[:, u, NP:NT], start=True, stop=True).then_inc(summed, 1)

            @block.scalar
            def _(act):
                for i in range(4):
                    act.wait_ge(bounded, 2 * i + 2)
                    inverse_root(act, logged, tmp[:, 0, :], scale=KK_SCALE, at=i).then_inc(inverted, 1)

        lam = sb2("rv_lam", [P, 2, NP])
        exps = sb2("rv_exps", [P, 2, 3, NP])
        summed, shifted, exped, used, ended = k.signals[:5]
        with stage(nc, k.signals) as block:
            @block.vector
            def _(dve):
                for i in range(5):
                    if i < 4:
                        w = logw[:, i, 0:NP]
                        if i >= 2:
                            dve.wait_ge(exped, 3 * (i - 1))
                        dve.tensor_tensor_scan(lam[:, i % 2, :], k.c("chunk_in"), w, 0.0, ALU.mult, ALU.add).then_inc(summed, 1)
                        dve.wait_ge(summed, i + 1)
                        dve.tensor_tensor(tmp[:, i % 2, 0:NP], lam[:, i % 2, :], w, ALU.subtract).then_inc(shifted, 1)
                    if i >= 1:
                        j = i - 1
                        up, down, before = (exps[:, j % 2, x, :].rearrange("p (c t) -> p c t", t=C) for x in range(3))
                        tok = lambda t: t[:, 0:NP].rearrange("p (c t) -> p c t", t=C)
                        dve.wait_ge(exped, 3 * j + 3)
                        dve.tensor_tensor(k.kr[:, j, :, 0, :], tok(kap[:, j, :]), before, ALU.mult)
                        dve.tensor_tensor(k.kr[:, j, :, 1, :], tok(ft[:, R_SLOT + j, :]), up, ALU.mult)
                        dve.tensor_tensor(k.bk[:, j, :, 0, :], tok(beta[:, j, :]), down, ALU.mult)
                        dve.tensor_tensor(k.bk[:, j, :, 1, :], tok(ft[:, K_SLOT + j, :]), down, ALU.mult)
                        dve.tensor_copy(k.ends[:, j, :], up[:, :, C - 1]).then_inc(used, 1)

            @block.scalar
            def _(act):
                for i in range(4):
                    if i >= 2:
                        act.wait_ge(used, i - 1)
                    act.wait_ge(summed, i + 1)
                    act.activation(exps[:, i % 2, 0, :], lam[:, i % 2, :], ACT.Exp).then_inc(exped, 1)
                    act.activation(exps[:, i % 2, 1, :], lam[:, i % 2, :], ACT.Exp, scale=-1.0).then_inc(exped, 1)
                    act.wait_ge(shifted, i + 1)
                    act.activation(exps[:, i % 2, 2, :], tmp[:, i % 2, 0:NP], ACT.Exp).then_inc(exped, 1)
                act.activation(logw[:, :, NP:NT], logw[:, :, NP:NT], ACT.Exp).then_inc(ended, 1)
    k.sample_sources = (ft[:, R_SLOT:R_SLOT + 4], logw, ft[:, K_SLOT:K_SLOT + 4], ft[:, V_SLOT:V_SLOT + 4], kap, beta)


def store_sample_rows(nc, k):
    with ExitStack() as ctx:
        sb, _ = scope(nc, ctx)
        rows = sb("rs_rows", [NS, 6, GW])
        turn(nc, k, "rs", [([t[:, i, NP:NT] for i in range(4)], [(lambda b: b[0:NS, :], rows[:, n, :])])
                           for n, t in enumerate(k.sample_sources)])
        with stage(nc, k.signals) as block:
            @block.sync
            def _(sp):
                sp.dma_start(k.sample_rows, rows[:, :, :].rearrange("p v c -> p (v c)")).then_inc(k.signals[0], 16)
                sp.wait_ge(k.signals[0], 16)


class Samples:

    def __init__(self, nc, k, l, sb):
        self.k, self.l = k, l
        self.vec = sb("rs_vec", [P, DS, 6, C])
        self.state = k.mixT[:, 12:16, :].rearrange("p k t -> p (k t)")[:, 0:HALF * C].rearrange("p (i j) -> p i j", j=C)
        self.tmp = sb("rs_tmp", [P, HALF, C])
        self.mine = sb("rs_mine", [P, DS, HALF])
        self.other = sb("rs_other", [P, DS, HALF])
        self.sa = sb("rs_sa", [P, HALF])
        self.y = sb("rs_y", [P, DS, HALF])

    def load(self, load):
        k = self.k
        load(self.state, k.state_wkv[bass.ds(self.l, 1)].rearrange("a s h (b i) j -> (a s h b) i j", b=2))
        for s in range(NB):
            for half in range(2):
                load(self.vec[16 * s + half:16 * s + 16:2], k.sample_rows.rearrange("(s t) (v h d) -> s h t v d", t=DS, v=6, h=H8)[s])
        load.wait()

    def choose(self, dve, step):
        step.then(dve.tensor_scalar(self.mine[:, :, :], self.vec[:, :, 3, 0:HALF], self.k.c("half0"), None, ALU.mult))
        step.then(dve.tensor_scalar(self.other[:, :, :], self.vec[:, :, 3, HALF:C], self.k.c("half1"), None, ALU.mult))
        dve.tensor_tensor(self.mine[:, :, :], self.mine[:, :, :], self.other[:, :, :], ALU.add)

    def advance(self, pool, step, reduced, t):
        S, Z = self.state, self.tmp[:, :, :]
        over_i = lambda n: self.vec[:, t, n, :].unsqueeze(1).to_broadcast([P, HALF, C])
        over_j = lambda v: v.unsqueeze(2).to_broadcast([P, HALF, C])
        step.then(pool.tensor_tensor(Z, S, over_i(4), ALU.mult))
        step(pool.tensor_tensor(S, S, over_i(1), ALU.mult))
        pool.wait_ge(reduced, 1)
        step.then(pool.tensor_tensor(Z, over_j(self.sa[:, :]), over_i(5), ALU.mult))
        step.then(pool.tensor_tensor(S, S, Z, ALU.add))
        step.then(pool.tensor_tensor(Z, over_j(self.mine[:, t, :]), over_i(2), ALU.mult))
        step.then(pool.tensor_tensor(S, S, Z, ALU.add))
        step.then(pool.tensor_tensor(Z, S, over_i(0), ALU.mult))

    def store(self, store, back, row):
        k = self.k
        store(k.s_wkv[bass.ds(self.l, 1)].rearrange("a s h (b i) j -> (a s h b) i j", b=2), self.state)
        for s in range(NB):
            store(k.sample_y.rearrange("(s t) (g i) -> s g t i", t=DS, i=HALF)[s], self.y[16 * s:16 * s + 16])
        store.wait()
        back(row, k.sample_y)
        back.wait()


def rwkv_chunks(nc, k, l):
    ft = k.ft
    with ExitStack() as ctx:
        sb, ps = scope(nc, ctx)
        state = sb("rc_state", [P, 2, 4, P])
        x_mat, u_mat = sb("rc_x", [P, 4, P]), sb("rc_u", [P, 4, P])
        own = {n: sb(f"rc_{n}", [P, 2, 4, P]) for n in "a b c e f g k_kappa v_rows beta_rows k_rows".split()}
        samples = Samples(nc, k, l, sb)
        zeroed = [own[n][:] for n in ("a", "b", "c", "e", "f", "k_kappa")]
        spare = ft[:, WL_SLOT:V_SLOT, :].rearrange("p s t -> p (s t)")
        spare = [spare[:, 8 * P * i:8 * P * (i + 1)].rearrange("p (q j t) -> p q j t", q=2, j=4) for i in range(2)]
        zeroed += spare
        held = dict(beta="a", n4="a", rT="a", k="b", n4T="b", dT="b", v="c", inv="c",
                    blockT="e", n2="e", n8T="e", r1="e", block="f", n2T="f", r="f", d="g", total="g")
        mats = {n: own[b] for n, b in held.items()} | {n: own[n] for n in ("k_kappa", "v_rows", "beta_rows", "k_rows")}
        mats.update(kappa=spare[0], restT=spare[1], r2T=spare[1])
        beta_r, k_r = sb("rc_beta_r", [P, 2, 4, C]), sb("rc_k_r", [P, 2, 4, C])
        banks = ExitStack()
        _, ps = scope(nc, banks)
        bank = [[ps(f"rc_p{q}{n}", [P, 512]) for n in "wxyz"] for q in range(2)]
        pairs = lambda t: t[:, :].rearrange("p (j f) -> p j f", j=4)
        mask = lambda name: k.c(name).unsqueeze(1).to_broadcast([P, 4, C])
        eye = k.c("ident").unsqueeze(1).to_broadcast([P, 4, P])
        LOW, UP = slice(0, C), slice(C, P)
        loaded, chosen = k.signals[:2]
        with stage(nc, k.signals) as block:
            @block.sync
            def _(sp):
                samples.load(Loads(sp, loaded))

            @block.vector
            def _(dve):
                dve.memset(state[:], 0.0)
                for t in zeroed[0::2]:
                    dve.memset(t, 0.0)
                dve.wait_ge(loaded, 16 * (1 + 2 * NB))
                samples.choose(dve, Steps(dve, chosen))

            @block.gpsimd
            def _(pool):
                for t in zeroed[1::2]:
                    pool.memset(t, 0.0)

        made, by_v, by_s, by_p = (k.signals[2 * i:2 * i + 2] for i in range(4))
        advanced, advanced_v, advanced_s, stepped, reduced = k.signals[8:13]

        def spread(copy, dst, src):
            for rows in (LOW, UP):
                last = copy(dst[rows, :, rows], src[rows])
            return last

        for c in range(0, NC, 2):
            with stage(nc, k.signals) as block:
                @block.tensor
                def _(pe):
                    done = [Steps(pe, s) for s in made]
                    moved = Steps(pe, advanced)

                    def products(q, n, left, right):
                        pe_in, pe_by = mats[left], mats[right]
                        for j in range(4):
                            last = pe.matmul(bank[q][n][:, P * j:P * j + P], pe_in[:, q, j, :], pe_by[:, q, j, :], start=True, stop=True)
                        done[q](last)

                    def turned(q, n, name):
                        for j in range(4):
                            last = pe.transpose(bank[q][n][:, P * j:P * j + P], mats[name][:, q, j, :], k.c("ident"))
                        done[q](last)

                    def against(q, n, name):
                        for j in range(4):
                            last = pe.matmul(bank[q][n][:, P * j:P * j + P], mats[name][:, q, j, :],
                                             k.kr[:, j, c + q].rearrange("p x t -> p (x t)"), start=True, stop=True)
                        done[q](last)

                    def summed(out, width, terms):
                        for j in range(4):
                            for i, (left, right) in enumerate(terms):
                                last = pe.matmul(out[:, width * j:width * j + width], left[:, j, :], right(j), start=(i == 0), stop=(i == len(terms) - 1))
                        moved(last)

                    def full(t):
                        return lambda j: t[:, j, :]

                    def x_products(q):
                        summed(bank[q][1], P, ((mats["kappa"][:, q], full(state[:, q])), (mats["k_kappa"][:, q], full(mats["v_rows"][:, q]))))

                    for q in range(2):
                        pe.wait_ge(by_v[q], 1)
                        against(q, 0, "beta")
                    for q in range(2):
                        pe.wait_ge(by_s[q], 1)
                        against(q, 1, "k")
                    for q in range(2):
                        pe.wait_ge(by_s[q], 2)
                        turned(q, 2, "v")
                    for q in range(2):
                        pe.wait_ge(by_v[q], 2)
                        turned(q, 3, "blockT")
                    for q in range(2):
                        pe.wait_ge(by_v[q], 3)
                        pe.wait_ge(by_s[q], 3)
                        products(q, 2, "blockT", "block")
                        pe.wait_ge(by_v[q], 4)
                        products(q, 3, "block", "blockT")
                    for q in range(2):
                        pe.wait_ge(by_v[q], 7)
                        pe.wait_ge(by_s[q], 4)
                        products(q, 2, "n2T", "n2")
                        products(q, 3, "n2", "n2T")
                        turned(q, 0, "beta")
                        pe.wait_ge(by_v[q], 9)
                        turned(q, 1, "k")
                    for q in range(2):
                        pe.wait_ge(by_s[q], 6)
                        products(q, 0, "n2T", "d")
                        pe.wait_ge(by_v[q], 10)
                        products(q, 2, "n4", "n4T")
                    for q in range(2):
                        pe.wait_ge(by_v[q], 11)
                        products(q, 3, "n4T", "d")
                    for q in range(2):
                        pe.wait_ge(by_v[q], 12)
                        pe.wait_ge(by_s[q], 8)
                        products(q, 0, "n8T", "d")
                    for q in range(2):
                        pe.wait_ge(by_v[q], 13)
                        products(q, 2, "restT", "d")
                        products(q, 3, "d", "restT")
                        turned(q, 0, "d")
                    for q in range(2):
                        pe.wait_ge(by_s[q], 9)
                        pe.wait_ge(by_v[q], 14)
                        products(q, 2, "r", "rT")
                    pe.wait_ge(by_p[0], 1)
                    x_products(0)
                    for q in range(2):
                        pe.wait_ge(by_v[q], 16)
                        products(q, 3, "r2T", "r1")
                    for q in range(2):
                        pe.wait_ge(by_v[q], 17)
                        pe.wait_ge(by_s[q], 10)
                        products(q, 0, "total", "dT")
                    for q in range(2):
                        if q == 1:
                            pe.wait_ge(advanced_v, 3)
                            pe.wait_ge(by_p[1], 1)
                            x_products(1)
                        pe.wait_ge(by_s[q], 11)
                        pe.wait_ge(advanced_s, 2 * q + 1)
                        summed(bank[q][2], P, ((mats["inv"][:, q], full(x_mat)),))
                        pe.wait_ge(advanced_v, 3 * q + 1)
                        summed(bank[q][3], P, ((mats["beta_rows"][:, q], full(u_mat)), (mats["k_rows"][:, q], full(mats["v_rows"][:, q]))))
                        summed(bank[q][0], C, ((state[:, q], lambda j: k.kr[:, j, c + q, 1, :]), (u_mat, lambda j: beta_r[:, q, j, :]),
                                               (mats["v_rows"][:, q], lambda j: k_r[:, q, j, :])))

                @block.gpsimd
                def _(pool):
                    done = [Steps(pool, s) for s in by_p]
                    for q in range(2):
                        done[q](spread(pool.tensor_copy, mats["kappa"][:, q], k.kr[:, :, c + q, 0, :]))
                    for q in range(2):
                        done[q].wait()
                    samples.advance(pool, Steps(pool, stepped), reduced, c // 2)

                @block.scalar
                def _(act):
                    done = [Steps(act, s) for s in by_s]
                    moved = Steps(act, advanced_s)

                    def keep(q, after, name, n):
                        act.wait_ge(made[q], after)
                        done[q](act.copy(mats[name][:, q], pairs(bank[q][n])))

                    for q in range(2):
                        done[q](spread(act.copy, mats["k"][:, q], k.bk[:, :, c + q, 1, :]))
                    for q in range(2):
                        done[q](spread(act.copy, mats["v"][:, q], ft[:, V_SLOT:V_SLOT + 4, C * (c + q):C * (c + q + 1)]))
                    for q in range(2):
                        keep(q, 3, "v_rows", 2)
                    for q in range(2):
                        keep(q, 6, "n2T", 3)
                    for q in range(2):
                        keep(q, 9, "n4", 2)
                        keep(q, 9, "beta_rows", 0)
                    for q in range(2):
                        keep(q, 10, "k_rows", 1)
                    for q in range(2):
                        keep(q, 12, "n8T", 2)
                    for q in range(2):
                        keep(q, 15, "r", 2)
                    for q in range(2):
                        keep(q, 17, "dT", 0)
                    act.wait_ge(advanced, 1)
                    moved(act.copy(x_mat[:], pairs(bank[0][1])))
                    for q in range(2):
                        keep(q, 20, "inv", 0)
                    for q in range(2):
                        if q == 1:
                            act.wait_ge(advanced, 5)
                            moved(act.copy(x_mat[:], pairs(bank[1][1])))
                        act.wait_ge(advanced, 4 * q + 4)
                        moved(act.copy(ft[:, R_SLOT:R_SLOT + 4, C * (c + q):C * (c + q + 1)], bank[q][0][:, 0:4 * C].rearrange("p (j t) -> p j t", j=4)))

                @block.vector
                def _(dve):
                    done = [Steps(dve, s) for s in by_v]
                    moved = Steps(dve, advanced_v)
                    kappas, rs = (lambda t: pairs(t)[:, :, 0:C]), (lambda t: pairs(t)[:, :, C:P])

                    def masked(q, name, src, m):
                        for rows in (LOW, UP):
                            last = dve.tensor_tensor(mats[name][rows, q, :, rows], kappas(src)[rows], mask(m)[rows], ALU.mult)
                        done[q](last)

                    def keep(q, after, name, n):
                        dve.wait_ge(made[q], after)
                        done[q](dve.tensor_copy(mats[name][:, q], pairs(bank[q][n])))

                    def add(q, after, name, n, other):
                        dve.wait_ge(made[q], after)
                        done[q](dve.tensor_tensor(mats[name][:, q], pairs(bank[q][n]), other, ALU.add))

                    for q in range(2):
                        done[q](spread(dve.tensor_copy, mats["beta"][:, q], k.bk[:, :, c + q, 0, :]))
                    for q in range(2):
                        dve.wait_ge(made[q], 1)
                        masked(q, "blockT", bank[q][0], "block_before")
                    for q in range(2):
                        keep(q, 4, "block", 3)
                        add(q, 4, "d", 3, eye)
                    for q in range(2):
                        masked(q, "restT", bank[q][0], "block_earlier")
                        done[q](dve.tensor_tensor(beta_r[:, q], rs(bank[q][0]), mask("chunk_upto"), ALU.mult))
                        keep(q, 6, "n2", 2)
                    for q in range(2):
                        masked(q, "k_kappa", bank[q][1], "chunk_before")
                        done[q](dve.tensor_tensor(k_r[:, q], rs(bank[q][1]), mask("chunk_upto"), ALU.mult))
                    dve.wait_ge(stepped, 1)
                    dve.tensor_reduce(samples.sa[:, :], samples.tmp[:, :, :], AX.X, ALU.add).then_inc(reduced, 1)
                    for q in range(2):
                        keep(q, 10, "n4T", 3)
                    for q in range(2):
                        add(q, 11, "d", 0, mats["d"][:, q])
                    for q in range(2):
                        add(q, 13, "d", 3, mats["d"][:, q])
                    for q in range(2):
                        add(q, 14, "d", 0, mats["d"][:, q])
                    for q in range(2):
                        keep(q, 16, "rT", 3)
                    for q in range(2):
                        dve.wait_ge(by_s[q], 9)
                        done[q](dve.tensor_tensor(mats["r1"][:, q], mats["r"][:, q], eye, ALU.add))
                    for q in range(2):
                        keep(q, 18, "r2T", 2)
                    for q in range(2):
                        add(q, 19, "total", 3, mats["r1"][:, q])
                    for q in range(2):
                        if q == 1:
                            dve.wait_ge(stepped, 7)
                            dve.tensor_reduce(samples.y[:, c // 2, :], samples.tmp[:, :, :], AX.X, ALU.add)
                        dve.wait_ge(advanced, 4 * q + 2)
                        moved(dve.tensor_copy(u_mat[:], pairs(bank[q][2])))
                        dve.wait_ge(advanced, 4 * q + 3)
                        new = state[:, 1 - q]
                        moved.then(dve.tensor_tensor(new, state[:, q], pairs(bank[q][3]), ALU.add))
                        moved(dve.tensor_tensor(new, new, k.ends[:, :, c + q].unsqueeze(2).to_broadcast([P, 4, P]), ALU.mult))
        banks.close()
        outT = x_mat
        row = own["a"][0:NS].rearrange("p q j f -> p (q j f)")[:, 0:GW]
        turn(nc, k, "rc_state", [([state[:, 0, j, :] for j in range(4)], [(lambda b: b[:, :].rearrange("p (j f) -> p j f", j=4), outT[:, :, :])])])
        with stage(nc, k.signals) as block:
            @block.sync
            def _(sp):
                store = Loads(sp, k.signals[0])
                for h in range(H8):
                    r = h % 2
                    store(k.p_wkv[bass.ds(l, 1), 0, h].rearrange("a i j -> (a i) j"), outT[C * r:C * r + C, h // 2, C * r:C * r + C])
                samples.store(store, Loads(sp, k.signals[1]), row)
        turn(nc, k, "rsy", [([row[:, P * i:P * i + P] for i in range(4)], [(side_by_side(NS, 4), ft[:, R_SLOT:R_SLOT + 4, NP:NT])])])


def rwkv_out(nc, k):
    ft = k.ft
    with ExitStack() as ctx:
        sb, ps = scope(nc, ctx)
        sq = sb("ro_sq", [P, NT])
        sums = ps("ro_sums", [P, 2, 2, 512])
        summed, centered, squared, scaled, powered, stepped, logged = k.signals[:7]
        halves = ((0, NP, 0), (NP, NT, 1))
        with stage(nc, k.signals) as block:
            @block.tensor
            def _(pe):
                for i in range(4):
                    if i >= 1:
                        pe.wait_ge(scaled, 2 * i)
                    for a, b, part in halves:
                        last = pe.matmul(sums[:, 0, part, 0:b - a], k.c("head_ones"), ft[:, R_SLOT + i, a:b], start=True, stop=True)
                    last.then_inc(summed, 1)
                    pe.wait_ge(squared, i + 1)
                    for a, b, part in halves:
                        last = pe.matmul(sums[:, 1, part, 0:b - a], k.c("head_ones"), sq[:, a:b], start=True, stop=True)
                    last.then_inc(summed, 1)

            @block.scalar
            def _(act):
                for i in range(4):
                    act.wait_ge(scaled, 2 * i + 2)
                    inverse_root(act, logged, sq[:, :], at=i).then_inc(powered, 1)

            @block.vector
            def _(dve):
                step = Steps(dve, stepped)
                for i in range(4):
                    y, out = ft[:, R_SLOT + i, :], k.mixT[:, 12 + i, :]
                    dve.wait_ge(summed, 2 * i + 1)
                    for a, b, part in halves:
                        last = dve.scalar_tensor_tensor(y[:, a:b], sums[:, 0, part, 0:b - a], -1.0 / C, y[:, a:b], ALU.mult, ALU.add)
                    step.then(last)
                    dve.tensor_tensor(sq[:, :], y, y, ALU.mult).then_inc(squared, 1)
                    dve.wait_ge(summed, 2 * i + 2)
                    for a, b, part in halves:
                        dve.tensor_scalar(sq[:, a:b], sums[:, 1, part, 0:b - a], 1.0 / C, LN_EPS, ALU.mult, ALU.add).then_inc(scaled, 1)
                    dve.wait_ge(powered, i + 1)
                    step.then(dve.scalar_tensor_tensor(y, y, k.prm[:, ROW_LNW + i:ROW_LNW + i + 1], sq[:, :], ALU.mult, ALU.mult))
                    step.then(dve.scalar_tensor_tensor(out, y, k.prm[:, ROW_LNB + i:ROW_LNB + i + 1], k.bonus[:, i, :], ALU.add, ALU.add))


INPUTS = ["x_prompt", "x_sample", "cache_sb_kv", "cache_dsa", "state_ret", "state_wkv", "state_shift", "page_table",
          "norm_g", "w_in", "shift_mu", "rw_w0", "rw_w2", "rw_a0", "rw_a2", "rw_kk", "rw_ka", "rw_rk",
          "rw_lnx_w", "rw_lnx_b", "w_out", "final_g"]
OUTPUTS = [("y_prompt", (1, NP, D)), ("y_sample", (NB, DS, D)),
           ("p_sb", (DEPTH, 1, NP, 2, 4, P)), ("p_dsa", (DEPTH, 1, NP, DSA_W)), ("p_ret", (DEPTH, 1, 4, 64, P)),
           ("p_wkv", (DEPTH, 1, H8, 64, 64)), ("p_shift", (DEPTH, 1, SHIFT_W)),
           ("s_sb", (DEPTH, NB, DS, 2, 4, P)), ("s_dsa", (DEPTH, NB, DS, DSA_W)), ("s_ret", (DEPTH, NB, 4, 64, P)),
           ("s_wkv", (DEPTH, NB, H8, 64, 64)), ("s_shift", (DEPTH, NB, SHIFT_W))]


def build(nc, tensors, groups="ABCD", probe=None):
    k = Core(tensors)
    with ExitStack() as ctx, nc.allow_non_contiguous_dma(reason="rows of a few values"):
        sb, _ = scope(nc, ctx)
        k.signals = [ctx.enter_context(nc.semaphore(f"signal_{i}")) for i in range(24)]
        k.table = sb("table", [P, TABLE.shape[1]])
        k.c = lambda name: k.table[:, AT[name][0]:AT[name][0] + AT[name][1]]
        k.prm = sb("prm", [P, PRM_ROWS])
        k.pages = sb("pages", [1, NB * PAGES], I32)
        k.scratch = sb("scratch", [P, 2, NT])
        k.mixT = sb("mixT", [P, KT, NT])
        k.x_spill = nc.dram_tensor("x_spill", (P, KT * NT), F32, kind="Internal").ap()
        k.sample_rows = nc.dram_tensor("sample_rows", (NS, 6 * GW), F32, kind="Internal").ap()
        k.sample_y = nc.dram_tensor("sample_y", (NS, GW), F32, kind="Internal").ap()
        k.sample_w = nc.dram_tensor("sample_w", (NS, 8), F32, kind="Internal").ap()
        arrived, = k.signals[:1]
        with stage(nc, k.signals) as block:
            @block.sync
            def _(sp):
                load = Loads(sp, arrived)
                load(k.table[:, :], k.consts)
                load(k.pages[:, :], k.page_table.rearrange("a b -> (a b)").unsqueeze(0))
                load.wait()

            @block.vector
            def _(dve):
                dve.memset(k.mixT[:, :, :], 0.0)

        with ExitStack() as own:
            k.xT = scope(nc, own)[0]("xT_in", [P, KT, NT])
            load_x(nc, k)
            spill_x(nc, k, back=False)

        with nc.Fori(0, DEPTH) as l:
            with ExitStack() as layer:
                sb2, _ = scope(nc, layer)
                k.ft = sb2("ft", [P, SLOTS, NT])
                with ExitStack() as most:
                    sb3, _ = scope(nc, most)
                    k.h = split_pair(sb3, "h")
                    with ExitStack() as own:
                        k.xT = scope(nc, own)[0]("xT_norm", [P, KT, NT])
                        spill_x(nc, k, back=True)
                        load_parameters(nc, k, l)
                        norm(nc, k, "norm", k.prm[:, ROW_G:ROW_G + KT], k.h)
                    for letter, name, tiles, mixer in (("A", "ret", RET_TILES, retention), ("B", "sb", SB_TILES, stick_breaking),
                                                       ("C", "dsa", DSA_TILES, sparse_attention)):
                        if letter in groups:
                            with ExitStack() as own:
                                weight_buffers(k, name, scope(nc, own)[0])
                                project_group(nc, k, l, name, tiles, list(range(len(tiles) - 4, len(tiles))))
                            mixer(nc, k, l)
                    if "D" in groups:
                        weight_buffers(k, "rw", sb3)
                        project_group(nc, k, l, "rw", RW_TILES, list(range(RG_SLOT, RG_SLOT + 4)))
                if "D" in groups:
                    rwkv(nc, k, l)
                if probe is not None:
                    moved, = k.signals[:1]
                    with stage(nc, k.signals) as block:
                        @block.sync
                        def _(sp):
                            sp.dma_start(probe[bass.ds(l, 1)].rearrange("a p n -> (a p) n"), k.mixT[:, :, :].rearrange("p k t -> p (k t)")).then_inc(moved, 16)
                            sp.wait_ge(moved, 16)
            with ExitStack() as own:
                k.xT = scope(nc, own)[0]("xT_out", [P, KT, NT])
                spill_x(nc, k, back=True)
                project_out(nc, k, l)
                spill_x(nc, k, back=False)
        with ExitStack() as own:
            k.xT = scope(nc, own)[0]("xT_last", [P, KT, NT])
            spill_x(nc, k, back=True)
            store_y(nc, k)


def kernel(**inputs):
    import numpy as _np
    import concourse.bacc as _bacc
    from concourse.bass_utils import run_bass_kernel_spmd as _run

    nc = _bacc.Bacc("TRN2", target_bir_lowering=False, num_devices=1)
    arrays, tensors = {"in_consts": TABLE}, {}
    for name in INPUTS:
        arrays["in_" + name] = _np.ascontiguousarray(inputs[name])
    for name, a in arrays.items():
        tensors[name[3:]] = nc.dram_tensor(name, a.shape, mybir.dt.from_np(a.dtype), kind="ExternalInput").ap()
    for name, shape in OUTPUTS:
        tensors[name] = nc.dram_tensor("out_" + name, shape, F32, kind="ExternalOutput").ap()
    build(nc, tensors)
    r = _run(nc, [arrays], core_ids=[0])
    return tuple(r.results[0]["out_" + name] for name, _ in OUTPUTS)
```

```python
from contextlib import ExitStack, contextmanager

import numpy as np

import concourse.bass as bass
from concourse import mybir

F32 = mybir.dt.float32
F32R = mybir.dt.float32r
I32 = mybir.dt.int32
ALU = mybir.AluOpType
ACT = mybir.ActivationFunctionType
AX = mybir.AxisListType

P = 128
D = 2048
KT = D // P
DEPTH = 2
NP = 512
NB = 8
DS = 4
NS = NB * DS
NT = NP + NS
QB = NP // P
TT = QB + 1
PAST = 512
PAGES = PAST // P
POOL = 40
GW = 512
DSA_W = 320
SHIFT_W = 1728
LORA = 96
TOPK = 128
TOPK_S = (PAST + DS) // 4
C = 64
NC = NP // C
H8 = 8
EPS = 1e-6
LN_EPS = 64e-5
NEG = -1e30
SB_SCALE = 128 ** -0.5
LOG_G = np.log1p(-np.exp2(-5.0 - np.arange(4)))

def _tiles(col, n):
    return [(col + P * i, P) for i in range(n)]

RET_TILES = _tiles(0, 12)
SB_TILES = _tiles(1536, 16)
DSA_TILES = _tiles(3584, 6) + [(4864, 64)] + _tiles(4352, 4) + [(4928, 8)] + _tiles(4936, 4)
RW_TILES = (_tiles(5448, 4) + [(5960, LORA)] + _tiles(6056, 8) + [(7080, LORA)] + _tiles(7176, 4))
SLOTS = 18

ROW_G, ROW_W0, ROW_A0, ROW_KK, ROW_KA, ROW_RK, ROW_LNW, ROW_LNB, ROW_MU = 0, 16, 20, 24, 28, 32, 36, 40, 44
PRM_ROWS = ROW_MU + 14


def constants():
    f = np.float32
    at, parts = {}, []

    def add(name, a):
        a = np.asarray(a, f).reshape(len(a), -1)
        full = np.zeros((P, a.shape[1]), f)
        full[: len(a)] = a
        at[name] = (sum(x.shape[1] for x in parts), a.shape[1])
        parts.append(full)

    i = np.arange(P)
    add("ident", np.eye(P))
    add("ones", np.ones((P, P)))
    add("head_ones", (i[:, None] // 64 == i[None] // 64))
    add("later", i[:, None] > i[None])
    add("before", i[:, None] < i[None])
    diff = i[None, :] - i[:, None]
    add("ret_mask", np.stack([np.where(diff >= 0, np.exp(np.maximum(diff, 0) * g), 0) for g in LOG_G], 1))
    t = np.arange(NS)
    same = t[:, None] // DS == t[None] // DS
    dt = t[None] - t[:, None]
    add("ret_mask_s", np.stack([np.where(same & (dt >= 0), np.exp(np.maximum(dt, 0) * g), 0) for g in LOG_G], 1))
    qdec = np.zeros((P, 2, 4)); kdec = np.zeros((P, 2, 4))
    qdec[:, 0] = np.exp((i[:, None] + 1) * LOG_G); kdec[:, 0] = np.exp((P - 1 - i[:, None]) * LOG_G)
    qdec[:NS, 1] = np.exp((t[:, None] % DS + 1) * LOG_G); kdec[:NS, 1] = np.exp((DS - 1 - t[:, None] % DS) * LOG_G)
    add("qdec", qdec); add("kdec", kdec)
    pos = np.zeros((P, TT), f)
    for a in range(QB):
        pos[:, a] = a * P + i
    pos[:NS, QB] = PAST + t % DS
    inv = (1.0 / (10000.0 ** (np.arange(32, dtype=f) / f(32)))).astype(f)
    ang = (pos[:, :, None] * inv).astype(f).astype(np.float64)
    add("cos", np.cos(ang)); add("sin", np.sin(ang))
    add("cosk", np.cos(ang) * 0.125); add("sink", np.sin(ang) * 0.125)
    add("seq_of", (t[:, None] // DS == np.arange(NB)[None]))
    add("before_s", same & (t[:, None] < t[None]))
    add("dsa_neg", np.where(i[None] <= i[:, None], 0, NEG))
    row = np.arange(P) % NS
    add("dsa_neg_s", np.where((row[:, None] // DS == t[None] // DS) & (t[None] <= row[:, None]), 0, NEG))
    rt = np.arange(NS) % DS
    add("spread", (rt[:, None, None] == row[None, None] % DS) & (np.arange(NB)[None, :, None] == row[None, None] // DS))
    j, u = i[:, None] % C, np.arange(C)[None]
    add("block_before", (j < u) & (j // 16 == u // 16))
    add("block_earlier", j // 16 < u // 16)
    add("chunk_before", j < u)
    add("chunk_upto", j <= u)
    add("chunk_in", np.broadcast_to(np.arange(NP) % C != 0, (P, NP)))
    add("half0", (i % 2 == 0)[:, None]); add("half1", (i % 2 == 1)[:, None])
    return at, np.concatenate(parts, 1)


AT, TABLE = constants()


@contextmanager
def stage(nc, signals):
    with nc.Block() as block:
        yield block
    nc.gpsimd.sem_clear(range(signals[0].num, signals[-1].num + 1))
    nc.all_engine_barrier()


class Steps:

    def __init__(self, engine, sem):
        self.engine, self.sem, self.n = engine, sem, 0

    def __call__(self, instruction):
        self.n += 1
        instruction.then_inc(self.sem, 1)
        return self.n

    def wait(self):
        self.engine.wait_ge(self.sem, self.n)

    def then(self, instruction):
        self(instruction)
        self.wait()


class Loads:

    def __init__(self, engine, sem):
        self.engine, self.sem, self.n = engine, sem, 0

    def __call__(self, out, in_):
        self.n += 16
        self.engine.dma_start(out, in_).then_inc(self.sem, 16)

    def wait(self):
        self.engine.wait_ge(self.sem, self.n)


def inverse_root(act, logged, x, scale=1.0, at=0):
    act.activation(x, x, ACT.Ln, scale=scale).then_inc(logged, 1)
    act.wait_ge(logged, at + 1)
    return act.activation(x, x, ACT.Exp, scale=-0.5)


def inverse_roots(act, scaled, logged, powered, x, scale=1.0):
    for i in range(4):
        act.wait_ge(scaled, 2 * i + 2)
        act.activation(x[:, i, :], x[:, i, :], ACT.Ln, scale=scale).then_inc(logged, 1)
    for i in range(4):
        act.wait_ge(logged, i + 1)
        act.activation(x[:, i, :], x[:, i, :], ACT.Exp, scale=-0.5).then_inc(powered, 1)


class Core:

    def __init__(self, tensors):
        self.consts = tensors["consts"]
        self.x_prompt = tensors["x_prompt"]
        self.x_sample = tensors["x_sample"]
        self.cache_sb_kv = tensors["cache_sb_kv"]
        self.cache_dsa = tensors["cache_dsa"]
        self.state_ret = tensors["state_ret"]
        self.state_wkv = tensors["state_wkv"]
        self.state_shift = tensors["state_shift"]
        self.page_table = tensors["page_table"]
        self.norm_g = tensors["norm_g"]
        self.w_in = tensors["w_in"]
        self.shift_mu = tensors["shift_mu"]
        self.rw_w0 = tensors["rw_w0"]
        self.rw_w2 = tensors["rw_w2"]
        self.rw_a0 = tensors["rw_a0"]
        self.rw_a2 = tensors["rw_a2"]
        self.rw_kk = tensors["rw_kk"]
        self.rw_ka = tensors["rw_ka"]
        self.rw_rk = tensors["rw_rk"]
        self.rw_lnx_w = tensors["rw_lnx_w"]
        self.rw_lnx_b = tensors["rw_lnx_b"]
        self.w_out = tensors["w_out"]
        self.final_g = tensors["final_g"]
        self.y_prompt = tensors["y_prompt"]
        self.y_sample = tensors["y_sample"]
        self.p_sb = tensors["p_sb"]
        self.p_dsa = tensors["p_dsa"]
        self.p_ret = tensors["p_ret"]
        self.p_wkv = tensors["p_wkv"]
        self.p_shift = tensors["p_shift"]
        self.s_sb = tensors["s_sb"]
        self.s_dsa = tensors["s_dsa"]
        self.s_ret = tensors["s_ret"]
        self.s_wkv = tensors["s_wkv"]
        self.s_shift = tensors["s_shift"]


def scope(nc, ctx):
    def sb(name, shape, dt=F32):
        return ctx.enter_context(nc.sbuf_tensor(name, shape, dt))

    def ps(name, shape):
        return ctx.enter_context(nc.psum_tensor(name, shape, F32))

    return sb, ps


def turn(nc, k, name, jobs):
    turned, kept_v, kept_s = k.signals[:3]
    R = 4
    with ExitStack() as ctx:
        _, ps = scope(nc, ctx)
        banks = ps(f"{name}_banks", [P, R, 512])
        with stage(nc, k.signals) as block:
            @block.tensor
            def _(pe):
                for n, (pieces, _) in enumerate(jobs):
                    if n >= R:
                        before = n - R
                        pe.wait_ge(kept_v if before % 2 == 0 else kept_s, before // 2 + 1)
                    at = 0
                    for piece in pieces:
                        rows, cols = piece.shape
                        last = pe.transpose(banks[0:cols, n % R, at:at + rows], piece, k.c("ident")[0:rows, 0:rows])
                        at += rows
                    last.then_inc(turned, 1)

            def copies(engine, copy, kept, odd):
                for n, (_, outs) in enumerate(jobs):
                    if n % 2 != odd:
                        continue
                    engine.wait_ge(turned, n + 1)
                    for m, (view, dst) in enumerate(outs):
                        last = copy(dst, view(banks[:, n % R, :]))
                    last.then_inc(kept, 1)

            @block.vector
            def _(dve):
                copies(dve, dve.tensor_copy, kept_v, 0)

            @block.scalar
            def _(act):
                copies(act, act.copy, kept_s, 1)


HALF_K = KT // 2
HALF_N = NT // 2


def split_pair(sb, name):
    return sb(f"{name}_hi", [P, KT, NT], F32R), sb(f"{name}_lo", [P, KT, NT], F32R)


def weight_buffers(k, name, sb):
    k.raw = sb(f"{name}_w_raw", [P, 4, HALF_K, P])
    k.w_hi = sb(f"{name}_w_hi", [P, 3, HALF_K, P], F32R)
    k.w_lo = sb(f"{name}_w_lo", [P, 3, HALF_K, P], F32R)


def project(nc, k, l, name, weights, tiles, source, keep, gates=(), due=None):
    product_ready, kept_a, kept_v, rounded, parted, used, opened, stepped = k.signals[:8]
    loaded = k.signals[8:12]
    stored, gated = k.signals[12:14]
    x_arrived = k.signals[14:18]
    w_l = weights[bass.ds(l, 1)].rearrange("a (k p) c -> p (a k) c", p=P)
    s_hi, s_lo = source
    pieces = 2 * len(tiles)
    slots = [*gates, *(i for i in range(len(tiles)) if i not in gates)]
    tiles = [tiles[i] for i in slots]
    with ExitStack() as ctx:
        _, ps = scope(nc, ctx)
        psum = ps(f"{name}_psum", [P, 2, 2, 512])
        with stage(nc, k.signals) as block:
            @block.sync
            def _(sp):
                store = Loads(sp, stored)

                def store_tile(i):
                    sp.wait_ge(kept_v, i + 1)
                    store(x_rows(k)[:, i, :], k.xT[:, i, :])

                for u in range(pieces):
                    if keep is None and u % 2 == 0 and u >= 8:
                        store_tile(u // 2 - 4)
                    if keep is None and u % 8 == 3:
                        part = slice(u // 8 * KT // 4, (u // 8 + 1) * KT // 4)
                        sp.dma_start(k.xT[:, part, :], x_rows(k)[:, part, :]).then_inc(x_arrived[u // 8], 16)
                    col, width, twice = tiles[u // 2]
                    half = slice(HALF_K * (u % 2), HALF_K * (u % 2) + HALF_K)
                    if u >= 4:
                        sp.wait_ge(parted, u - 3)
                    dst = k.raw[:, u % 4, :, :]
                    if twice:
                        sp.dma_start(dst[:, :, 0:width], w_l[:, half, col:col + width]).then_inc(loaded[u % 4], 16)
                        sp.dma_start(dst[:, :, width:P], w_l[:, half, col:col + width]).then_inc(loaded[u % 4], 16)
                    else:
                        sp.dma_start(dst, w_l[:, half, col:col + P]).then_inc(loaded[u % 4], 16)
                if keep is None:
                    for i in range(len(tiles) - 4, len(tiles)):
                        store_tile(i)
                    store.wait()

            arrived, count = [], [0] * 4
            for u in range(pieces):
                count[u % 4] += 32 if tiles[u // 2][2] else 16
                arrived.append(count[u % 4])

            @block.tensor
            def _(pe):
                for i in range(len(tiles)):
                    if i >= 2:
                        pe.wait_ge(kept_a, i - 1)
                        pe.wait_ge(kept_v, i - 1)
                    for u in (2 * i, 2 * i + 1):
                        pe.wait_ge(parted, u + 1)
                        for t in range(HALF_K):
                            f = HALF_K * (u % 2) + t
                            first, last_k = f == 0, f == KT - 1
                            for w, parts in ((k.w_hi, (s_hi, s_lo)), (k.w_lo, (s_hi,))):
                                for part in parts:
                                    for c in range(2):
                                        last = pe.matmul(psum[:, i % 2, c, 0:HALF_N], w[:, u % 3, t, :], part[:, f, HALF_N * c:HALF_N * c + HALF_N],
                                                         start=first and w is k.w_hi and part is s_hi, stop=last_k and w is k.w_lo)
                        last.then_inc(used if u % 2 == 0 else product_ready, 1)

            if due is not None:
                @block.gpsimd
                def _(pool):
                    for i in range(4):
                        mix = k.mixT[:, due[0] + i, :]
                        pool.tensor_tensor(mix, mix, k.ft[:, due[1] + i, :], ALU.mult).then_inc(gated, 1)

            def slots_free(engine, i):
                if due is not None and i == 0:
                    engine.wait_ge(gated, 4)

            def piece_free(engine, u):
                if u >= 3:
                    v = u - 3
                    engine.wait_ge(used if v % 2 == 0 else product_ready, v // 2 + 1)

            @block.scalar
            def _(act):
                def round_piece(u):
                    act.wait_ge(loaded[u % 4], arrived[u])
                    piece_free(act, u)
                    act.copy(k.w_hi[:, u % 3, :, :], k.raw[:, u % 4, :, :]).then_inc(rounded, 1)

                for u in range(3):
                    round_piece(u)
                for i in range(len(tiles)):
                    for u in (2 * i + 3, 2 * i + 4):
                        if u == 2 * i + 4:
                            act.wait_ge(product_ready, i + 1)
                            if keep is not None:
                                slots_free(act, i)
                                act.copy(keep[:, slots[i], 0:HALF_N], psum[:, i % 2, 0, 0:HALF_N]).then_inc(kept_a, 1)
                        if u < pieces:
                            round_piece(u)
                    if i < len(gates):
                        act.wait_ge(kept_v, i + 1)
                        act.wait_ge(kept_a, i + 1)
                        if i >= 2:
                            act.wait_ge(stepped, 3 * (i - 1))
                        act.activation(k.scratch[:, i % 2, :], keep[:, slots[i], :], ACT.Exp, scale=-1.0).then_inc(opened, 1)

            @block.vector
            def _(dve):
                step = Steps(dve, stepped)

                def part_piece(u):
                    dve.wait_ge(rounded, u + 1)
                    piece_free(dve, u)
                    dve.tensor_tensor(k.w_lo[:, u % 3, :, :], k.raw[:, u % 4, :, :], k.w_hi[:, u % 3, :, :], ALU.subtract).then_inc(parted, 1)

                def silu(i):
                    e = k.scratch[:, i % 2, :]
                    dve.wait_ge(opened, i + 1)
                    step.then(dve.tensor_scalar(e, e, 1.0, None, ALU.add))
                    step.then(dve.reciprocal(e, e))
                    step(dve.tensor_tensor(keep[:, slots[i], :], keep[:, slots[i], :], e, ALU.mult))

                for u in range(3):
                    part_piece(u)
                for i in range(len(tiles)):
                    for u in (2 * i + 3, 2 * i + 4):
                        if u == 2 * i + 4:
                            dve.wait_ge(product_ready, i + 1)
                            if keep is not None:
                                slots_free(dve, i)
                                dve.tensor_copy(keep[:, slots[i], HALF_N:NT], psum[:, i % 2, 1, 0:HALF_N]).then_inc(kept_v, 1)
                            else:
                                if i % (KT // 4) == 0:
                                    dve.wait_ge(x_arrived[i // (KT // 4)], 16)
                                for c, kept in ((0, kept_a), (1, kept_v)):
                                    x = k.xT[:, i, HALF_N * c:HALF_N * c + HALF_N]
                                    dve.tensor_tensor(x, x, psum[:, i % 2, c, 0:HALF_N], ALU.add).then_inc(kept, 1)
                        if u < pieces:
                            part_piece(u)
                        if u == 2 * i + 4 and 0 <= i - 1 < len(gates):
                            silu(i - 1)


def project_group(nc, k, l, name, tiles, gates, due):
    project(nc, k, l, name, k.w_in, [(*t, t == (4864, 64)) for t in tiles], k.h, k.ft, gates, due)


def project_out(nc, k, l):
    with ExitStack() as ctx:
        sb, _ = scope(nc, ctx)
        hi, lo = split_pair(sb, "mix")
        rounded, = k.signals[:1]
        with stage(nc, k.signals) as block:
            @block.scalar
            def _(act):
                for t in range(KT):
                    act.copy(hi[:, t, :], k.mixT[:, t, :]).then_inc(rounded, 1)

            def rest(engine, tiles):
                for t in tiles:
                    engine.wait_ge(rounded, t + 1)
                    engine.tensor_tensor(lo[:, t, :], k.mixT[:, t, :], hi[:, t, :], ALU.subtract)

            @block.vector
            def _(dve):
                rest(dve, [t for t in range(KT) if t % 3 != 1])

            @block.gpsimd
            def _(pool):
                rest(pool, range(1, KT, 3))
        weight_buffers(k, "out", sb)
        project(nc, k, l, "out", k.w_out, [(P * i, P, False) for i in range(KT)], (hi, lo), None)


def turn_x(nc, k, rows):
    jobs = []
    for a in range(TT):
        n = P if a < QB else NS
        for q in range(4):
            jobs.append(([rows[0:n, a, P * (4 * q + i):P * (4 * q + i + 1)] for i in range(4)],
                         [(lambda b, n=n: b[:, 0:4 * n].rearrange("p (i t) -> p i t", t=n), k.xT[:, 4 * q:4 * q + 4, a * P:a * P + n])]))
    turn(nc, k, "xin", jobs)


def norm(nc, k, name, gains, out):
    squared, summed, scaled, powered, logged, normed, rounded = k.signals[:7]
    arrived = k.signals[8:12]
    with ExitStack() as ctx:
        sb, ps = scope(nc, ctx)
        sq = sb(f"{name}_sq", [P, 2, NT])
        rs = sb(f"{name}_rs", [P, NT])
        sums = ps(f"{name}_sums", [P, 2, 512])
        pair = isinstance(out, tuple)
        with stage(nc, k.signals) as block:
            @block.sync
            def _(sp):
                for i in range(4):
                    part = slice(i * KT // 4, (i + 1) * KT // 4)
                    sp.dma_start(k.xT[:, part, :], x_rows(k)[:, part, :]).then_inc(arrived[i], 16)

            @block.scalar
            def _(act):
                for t in range(KT):
                    if t % (KT // 4) == 0:
                        act.wait_ge(arrived[t // (KT // 4)], 16)
                    if t >= 2:
                        act.wait_ge(summed, t - 1)
                    act.activation(sq[:, t % 2, :], k.xT[:, t, :], ACT.Square).then_inc(squared, 1)
                act.wait_ge(scaled, 2)
                inverse_root(act, logged, rs[:, :]).then_inc(powered, 1)
                for t in range(KT if pair else 0):
                    act.wait_ge(normed, t + 1)
                    act.copy(out[0][:, t, :], k.xT[:, t, :]).then_inc(rounded, 1)

            @block.tensor
            def _(pe):
                for t in range(KT):
                    pe.wait_ge(squared, t + 1)
                    pe.matmul(sums[:, 0, :], k.c("ones"), sq[:, t % 2, 0:NP], start=(t == 0), stop=(t == KT - 1))
                    pe.matmul(sums[:, 1, 0:NS], k.c("ones"), sq[:, t % 2, NP:NT], start=(t == 0), stop=(t == KT - 1)).then_inc(summed, 1)

            def rest(engine, t):
                engine.wait_ge(rounded, t + 1)
                engine.tensor_tensor(out[1][:, t, :], k.xT[:, t, :], out[0][:, t, :], ALU.subtract)

            if pair:
                @block.gpsimd
                def _(pool):
                    for t in range(KT):
                        if t % 3:
                            rest(pool, t)

            @block.vector
            def _(dve):
                dve.wait_ge(summed, KT)
                dve.tensor_scalar(rs[:, 0:NP], sums[:, 0, :], 1.0 / D, EPS, ALU.mult, ALU.add).then_inc(scaled, 1)
                dve.tensor_scalar(rs[:, NP:NT], sums[:, 1, 0:NS], 1.0 / D, EPS, ALU.mult, ALU.add).then_inc(scaled, 1)
                dve.wait_ge(powered, 1)
                for t in range(KT + 2):
                    if t < KT:
                        y = k.xT[:, t, :] if pair else out[:, t, :]
                        dve.scalar_tensor_tensor(y, k.xT[:, t, :], gains[:, t:t + 1], rs[:, :], ALU.mult, ALU.mult).then_inc(normed, 1)
                    if pair and t >= 2 and (t - 2) % 3 == 0:
                        rest(dve, t - 2)


def load_parameters(nc, k, l):
    with ExitStack() as ctx:
        sb, _ = scope(nc, ctx)
        rows = sb("prm_rows", [PRM_ROWS, P])
        loaded, cleared = k.signals[:2]
        with stage(nc, k.signals) as block:
            @block.vector
            def _(dve):
                dve.memset(rows[:, :], 0.0).then_inc(cleared, 1)

            @block.sync
            def _(sp):
                sp.wait_ge(cleared, 1)
                load = Loads(sp, loaded)

                def full(row, ap, n):
                    load(rows[row:row + n, :], ap[bass.ds(l, 1)].rearrange("a (n p) -> (a n) p", p=P))

                full(ROW_G, k.norm_g, KT)
                for row, ap in ((ROW_W0, k.rw_w0), (ROW_A0, k.rw_a0), (ROW_KK, k.rw_kk), (ROW_KA, k.rw_ka),
                                (ROW_LNW, k.rw_lnx_w), (ROW_LNB, k.rw_lnx_b)):
                    full(row, ap, 4)
                load(rows[ROW_RK:ROW_RK + 4, :], k.rw_rk[bass.ds(l, 1)].rearrange("a (j h) d -> (a j) (h d)", h=2))
                mu = k.shift_mu[bass.ds(l, 1)]
                for first, col, n in ((0, 0, 4), (5, 608, 8)):
                    load(rows[ROW_MU + first:ROW_MU + first + n, :], mu[:, col:col + P * n].rearrange("a (n p) -> (a n) p", p=P))
                for slot, col in ((4, 512), (13, 1632)):
                    load(rows[ROW_MU + slot:ROW_MU + slot + 1, 0:LORA], mu[:, col:col + LORA])
                load.wait()
        turn(nc, k, "prm", [([rows[:, :]], [(lambda b: b[:, 0:PRM_ROWS], k.prm[:, :])])])


def x_rows(k):
    return k.x_spill.rearrange("p (k t) -> p k t", t=NT)


def store_x(nc, k):
    stored, = k.signals[:1]
    with stage(nc, k.signals) as block:
        @block.sync
        def _(sp):
            store = Loads(sp, stored)
            store(x_rows(k), k.xT[:, :, :])
            store.wait()


def store_y(nc, k):
    with ExitStack() as ctx:
        sb, _ = scope(nc, ctx)
        rows = sb("fg_rows", [KT, P])
        fg = sb("fg", [P, KT])
        yT = sb("yT", [P, KT, NT])
        y = sb("y", [P, TT, D])
        moved, = k.signals[:1]
        with stage(nc, k.signals) as block:
            @block.sync
            def _(sp):
                sp.dma_start(rows[:, :], k.final_g.rearrange("(n p) -> n p", p=P)).then_inc(moved, 16)
                sp.wait_ge(moved, 16)
        turn(nc, k, "fgt", [([rows[:, :]], [(lambda b: b[:, 0:KT], fg[:, :])])])
        norm(nc, k, "final", fg, yT)
        jobs = []
        for a in range(TT):
            n = P if a < QB else NS
            for q in range(4):
                jobs.append(([yT[:, 4 * q + i, a * P:a * P + n] for i in range(4)], [(lambda b, n=n: b[0:n, :], y[0:n, a, 512 * q:512 * q + 512])]))
        turn(nc, k, "yout", jobs)
        with stage(nc, k.signals) as block:
            @block.sync
            def _(sp):
                store = Loads(sp, moved)
                store(k.y_prompt.rearrange("b (a p) d -> p (b a) d", p=P), y[:, 0:QB, :])
                store(k.y_sample.rearrange("b t d -> (b t) d"), y[0:NS, QB, :])
                store.wait()


def gate(nc, k, first, g):
    with stage(nc, k.signals) as block:
        @block.vector
        def _(dve):
            for i in range(3):
                dve.tensor_tensor(k.mixT[:, first + i, :], k.mixT[:, first + i, :], k.ft[:, g + i, :], ALU.mult)

        @block.gpsimd
        def _(pool):
            pool.tensor_tensor(k.mixT[:, first + 3, :], k.mixT[:, first + 3, :], k.ft[:, g + 3, :], ALU.mult)


def tokens(a):
    return (P, slice(a * P, a * P + P)) if a < QB else (NS, slice(NP, NT))


def side_by_side(n, width):
    return lambda b: b[:, 0:width * n].rearrange("p (i t) -> p i t", t=n)


def retention(nc, k, l):
    ft = k.ft
    with ExitStack() as ctx:
        sb, ps = scope(nc, ctx)
        qk = sb("ret_qk", [P, TT, 512])
        v = sb("ret_v", [P, TT, 512])
        rot = sb("ret_rot", [P, TT, 512])
        tmp = sb("ret_tmp", [P, TT, 4, 32])
        state = sb("ret_state", [P, 2, 2 * P])
        state_s = sb("ret_state_s", [P, NB, 2, P])
        qdz = sb("ret_qdz", [P, 2, 2, NS])
        qT, qdT, kz = ft[:, 0:2, :], ft[:, 2:4, :], ft[:, 4:8, :]
        jobs = []
        for a in range(TT):
            n, cols = tokens(a)
            jobs.append(([ft[:, s, cols] for s in range(4)], [(lambda b, n=n: b[0:n, :], qk[0:n, a, :])]))
            jobs.append(([ft[:, s, cols] for s in range(4, 8)], [(lambda b, n=n: b[0:n, :], v[0:n, a, :])]))
        turn(nc, k, "ret_in", jobs)

        turned, loaded = k.signals[:2]
        with stage(nc, k.signals) as block:
            @block.sync
            def _(sp):
                load = Loads(sp, loaded)
                for s in range(NB):
                    for par in range(2):
                        load(state_s[64 * par:64 * par + 64, s, :, :],
                             k.state_ret[bass.ds(l, 1), s].rearrange("a (j b) d e -> a b d j e", b=2)[0, par])
                load.wait()

            @block.gpsimd
            def _(pool):
                pool.memset(state[:, :, :], 0.0)
                pool.memset(qdz[:, :, :, :], 0.0)

            @block.vector
            def _(dve):
                step = Steps(dve, turned)
                dve.memset(kz[64:128, 0:2, :], 0.0)
                dve.memset(kz[0:64, 2:4, :], 0.0)
                for r0, (n, a0, a1) in enumerate(((P, 0, QB), (NS, QB, TT))):
                    w = a1 - a0
                    for part, (cos, sin) in enumerate((("cos", "sin"), ("cosk", "sink"))):
                        def halves(t):
                            h = t[0:n, a0:a1, 256 * part:256 * part + 256].rearrange("p a (h u d) -> p a h u d", h=4, u=2)
                            return h[:, :, :, 0, :], h[:, :, :, 1, :]

                        def table(name):
                            return k.c(name).rearrange("p (a d) -> p a d", d=32)[0:n, a0:a1].unsqueeze(2).to_broadcast([n, w, 4, 32])

                        def each(op, out, a, b, y):
                            for i in range(w):
                                last = dve.tensor_tensor(out[:, i], a[:, i], b[:, i], y)
                            op(last)

                        (x1, x2), (y1, y2) = halves(qk), halves(rot)
                        z = tmp[0:n, a0:a1]
                        each(step, y1, x1, table(cos), ALU.mult)
                        each(step.then, z, x2, table(sin), ALU.mult)
                        each(step, y2, x1, table(sin), ALU.mult)
                        each(step.then, y1, y1, z, ALU.subtract)
                        each(step.then, z, x2, table(cos), ALU.mult)
                        each(step.then, y2, y2, z, ALU.add)
                        dec = k.c("kdec" if part else "qdec").rearrange("p (r h) -> p r h", r=2)
                        for h in range(4):
                            col = slice(256 * part + 64 * h, 256 * part + 64 * h + 64)
                            step(dve.tensor_scalar(qk[0:n, a0:a1, col], rot[0:n, a0:a1, col], dec[0:n, r0, h:h + 1], None, ALU.mult))
        jobs = []
        for a in range(TT):
            n, cols = tokens(a)
            outs = [(side_by_side(n, 4), ft[:, 0:4, cols])]
            if a == QB:
                outs += [(lambda b, r=r: b[64 * r:64 * r + 64, 2 * NS:4 * NS].rearrange("p (i t) -> p i t", t=NS),
                          qdz[64 * r:64 * r + 64, r, :, :]) for r in range(2)]
            jobs.append(([t[0:n, a, P * i:P * i + P] for t in (rot, qk) for i in range(2)], outs))
            jobs.append(([rot[0:n, a, 256 + P * i:384 + P * i] for i in range(2)],
                         [(lambda b, n=n, r=r: b[64 * r:64 * r + 64, 0:2 * n].rearrange("p (i t) -> p i t", t=n),
                           kz[64 * r:64 * r + 64, 2 * r:2 * r + 2, cols]) for r in range(2)]))
        turn(nc, k, "ret_qk_T", jobs)

        scored, masked, made, kept, grown, carried, stored = k.signals[:7]
        with ExitStack() as inner:
            sb2, ps2 = scope(nc, inner)
            att = sb2("ret_att", [P, 2, 512])
            p_att, p_out, p_state = (ps2(f"ret_p_{x}", [P, 2, 512]) for x in ("att", "out", "state"))
            with stage(nc, k.signals) as block:
                @block.tensor
                def _(pe):
                    for c in range(QB):
                        tok = slice(c * P, c * P + P)
                        if c >= 2:
                            pe.wait_ge(masked, c - 1)
                            pe.wait_ge(carried, c - 1)
                            pe.wait_ge(kept, c - 1)
                        for h in range(4):
                            last = pe.matmul(p_att[:, c % 2, P * h:P * h + P], kz[:, 2 * (h % 2) + h // 2, tok],
                                             qT[:, h // 2, tok], start=True, stop=True)
                        last.then_inc(scored, 1)
                        for j in range(2):
                            last = pe.matmul(p_state[:, c % 2, 256 * j:256 * j + 256], qk[:, c, 256 + P * j:384 + P * j],
                                             v[:, c, 256 * j:256 * j + 256], start=True, stop=True)
                        last.then_inc(grown, 1)
                        pe.wait_ge(masked, c + 1)
                        if c >= 1:
                            pe.wait_ge(carried, c)
                        for h in range(4):
                            out = p_out[:, c % 2, P * h:P * h + P]
                            last = pe.matmul(out, v[:, c, P * h:P * h + P], att[:, c % 2, P * h:P * h + P], start=True, stop=(c == 0))
                            if c:
                                last = pe.matmul(out, state[:, h // 2, P * (h % 2):P * (h % 2) + P], qdT[:, h // 2, tok], start=False, stop=True)
                        last.then_inc(made, 1)

                @block.scalar
                def _(act):
                    for c in range(QB):
                        act.wait_ge(made, c + 1)
                        act.copy(k.mixT[:, 0:4, c * P:c * P + P], p_out[:, c % 2, :].rearrange("p (h t) -> p h t", h=4)).then_inc(kept, 1)

                @block.vector
                def _(dve):
                    for c in range(QB):
                        dve.wait_ge(scored, c + 1)
                        if c >= 2:
                            dve.wait_ge(made, c - 1)
                        dve.tensor_tensor(att[:, c % 2, :], p_att[:, c % 2, :], k.c("ret_mask"), ALU.mult).then_inc(masked, 1)
                        dve.wait_ge(grown, c + 1)
                        dve.wait_ge(made, c + 1)
                        for h in range(4):
                            r, j = h % 2, h // 2
                            s = state[64 * r:64 * r + 64, j, P * r:P * r + P]
                            g = p_state[64 * r:64 * r + 64, c % 2, 256 * j + P * r:256 * j + P * r + P]
                            last = dve.scalar_tensor_tensor(s, s, float(np.exp(P * LOG_G[h])), g, ALU.mult, ALU.add)
                        last.then_inc(carried, 1)

                @block.sync
                def _(sp):
                    store = Loads(sp, stored)
                    sp.wait_ge(carried, QB)
                    for h in range(4):
                        r, j = h % 2, h // 2
                        store(k.p_ret[bass.ds(l, 1), 0, h].rearrange("a d e -> (a d) e"), state[64 * r:64 * r + 64, j, P * r:P * r + P])
                    store.wait()

        scored, masked, made, grown, spread, advanced, copied, stored = k.signals[:8]
        with ExitStack() as inner:
            sb2, ps2 = scope(nc, inner)
            att = sb2("ret_att_s", [NS, 4, NS])
            vx = [rot[0:NS, 2 * i:2 * i + 2, :].rearrange("p a (s e) -> p (a s) e", e=P) for i in range(2)]
            p_att = ps2("ret_ps_att", [NS, 512])
            p_out = ps2("ret_ps_out", [P, 512])
            p_state = ps2("ret_ps_state", [P, 2, 2, 512])
            with stage(nc, k.signals) as block:
                @block.tensor
                def _(pe):
                    for h in range(4):
                        last = pe.matmul(p_att[:, NS * h:NS * h + NS], kz[:, 2 * (h % 2) + h // 2, NP:NT], qT[:, h // 2, NP:NT], start=True, stop=True)
                    last.then_inc(scored, 1)
                    pe.wait_ge(masked, 1)
                    for h in range(4):
                        pe.matmul(p_out[:, NS * h:NS * h + NS], v[0:NS, QB, P * h:P * h + P], att[:, h, :], start=True, stop=False, skip_group_check=True)
                        for s in range(NB):
                            last = pe.matmul(p_out[:, NS * h + DS * s:NS * h + DS * s + DS], state_s[:, s, h // 2, :],
                                             qdz[:, h % 2, h // 2, DS * s:DS * s + DS], start=False, stop=(s == NB - 1), skip_group_check=True)
                    last.then_inc(made, 1)
                    for h in range(4):
                        pe.wait_ge(spread, h + 1)
                        if h >= 2:
                            pe.wait_ge(advanced, h - 1)
                        for q in range(2):
                            last = pe.matmul(p_state[:, h % 2, q, :], qk[0:NS, QB, 256 + P * (h // 2):384 + P * (h // 2)],
                                             vx[h % 2][:, 4 * q:4 * q + 4, :], start=True, stop=True)
                        last.then_inc(grown, 1)

                @block.scalar
                def _(act):
                    act.wait_ge(made, 1)
                    act.copy(k.mixT[:, 0:4, NP:NT], p_out[:, 0:4 * NS].rearrange("p (h t) -> p h t", h=4)).then_inc(copied, 1)

                @block.vector
                def _(dve):
                    dve.wait_ge(scored, 1)
                    dve.tensor_tensor(att[:, :, :], p_att[:, 0:4 * NS].rearrange("p (h t) -> p h t", h=4),
                                      k.c("ret_mask_s")[0:NS].rearrange("p (h t) -> p h t", h=4), ALU.mult).then_inc(masked, 1)
                    for h in range(5):
                        if h < 4:
                            if h >= 2:
                                dve.wait_ge(grown, h - 1)
                            dve.tensor_tensor(vx[h % 2], v[0:NS, QB, P * h:P * h + P].unsqueeze(1).to_broadcast([NS, NB, P]),
                                              k.c("seq_of")[0:NS].unsqueeze(2).to_broadcast([NS, NB, P]), ALU.mult).then_inc(spread, 1)
                        if h == 0:
                            dve.wait_ge(made, 1)
                            continue
                        g, r = h - 1, (h - 1) % 2
                        dve.wait_ge(grown, g + 1)
                        for q in range(2):
                            s = state_s[64 * r:64 * r + 64, 4 * q:4 * q + 4, g // 2, :]
                            last = dve.scalar_tensor_tensor(s, s, float(np.exp(DS * LOG_G[g])),
                                                            p_state[64 * r:64 * r + 64, g % 2, q, :].rearrange("p (s e) -> p s e", e=P), ALU.mult, ALU.add)
                        last.then_inc(advanced, 1)

                @block.sync
                def _(sp):
                    store = Loads(sp, stored)
                    sp.wait_ge(advanced, 4)
                    for h in range(4):
                        store(k.s_ret[bass.ds(l, 1), :, h].rearrange("a s d e -> (a d) s e"), state_s[64 * (h % 2):64 * (h % 2) + 64, :, h // 2, :])
                    store.wait()

        head_norm(nc, k, rot[:, :, :].rearrange("p a c -> p (a c)")[:, 0:4 * NT].rearrange("p (i t) -> p i t", t=NT))


def head_norm(nc, k, sq):
    squared, summed, scaled, powered, logged = k.signals[:5]
    with ExitStack() as ctx:
        _, ps = scope(nc, ctx)
        sums = ps("hn_sums", [P, 4, 512])
        sums_s = ps("hn_sums_s", [P, 4, NS])
        with stage(nc, k.signals) as block:
            @block.scalar
            def _(act):
                for i in range(4):
                    act.activation(sq[:, i, :], k.mixT[:, i, :], ACT.Square).then_inc(squared, 1)
                inverse_roots(act, scaled, logged, powered, sq)

            @block.tensor
            def _(pe):
                for i in range(4):
                    pe.wait_ge(squared, i + 1)
                    if i >= 1:
                        pe.wait_ge(scaled, 2 * i)
                    pe.matmul(sums[:, i, :], k.c("ones"), sq[:, i, 0:NP], start=True, stop=True)
                    pe.matmul(sums_s[:, i, :], k.c("ones"), sq[:, i, NP:NT], start=True, stop=True).then_inc(summed, 1)

            @block.vector
            def _(dve):
                for i in range(4):
                    dve.wait_ge(summed, i + 1)
                    dve.tensor_scalar(sq[:, i, 0:NP], sums[:, i, :], 1.0 / P, EPS, ALU.mult, ALU.add).then_inc(scaled, 1)
                    dve.tensor_scalar(sq[:, i, NP:NT], sums_s[:, i, :], 1.0 / P, EPS, ALU.mult, ALU.add).then_inc(scaled, 1)
                for i in range(4):
                    dve.wait_ge(powered, i + 1)
                    dve.tensor_tensor(k.mixT[:, i, :], k.mixT[:, i, :], sq[:, i, :], ALU.mult)


def stick_breaking(nc, k, l):
    ft = k.ft
    with ExitStack() as ctx:
        sb, ps = scope(nc, ctx)
        kv = sb("sb_kv", [P, TT, 1024])
        jobs = []
        for a in range(TT):
            n, cols = tokens(a)
            for u in range(2):
                jobs.append(([ft[:, 4 + 4 * u + s, cols] for s in range(4)], [(lambda b, n=n: b[0:n, :], kv[0:n, a, 512 * u:512 * u + 512])]))
        turn(nc, k, "sb_in", jobs)

        scored, split, shrunk, logged, summed_up, weighted, exped, applied, kept, stored, own, stepped, opened = k.signals[:13]
        starts = [sum(NP - P * c for c in range(b)) for b in range(QB + 1)]
        AREA = starts[QB]

        def blk(t, h, b, lo=0, hi=None):
            return t[:, h % 2, starts[b] + lo:(starts[b + 1] if hi is None else starts[b] + hi)]

        with ExitStack() as inner:
            sb2, ps2 = scope(nc, inner)
            logs = sb2("sb_logs", [P, 2, AREA])
            miss = sb2("sb_miss", [P, 2, AREA])
            p_z = ps2("sb_p_z", [P, 3, 512])
            p_after = ps2("sb_p_after", [P, 2, 512])
            p_out = ps2("sb_p_out", [P, 2, 512])
            with stage(nc, k.signals) as block:
                @block.sync
                def _(sp):
                    store = Loads(sp, stored)
                    for a in range(QB):
                        store(k.p_sb[bass.ds(l, 1), 0, a * P:a * P + P].rearrange("a t u h d -> (a t) (u h d)"), kv[:, a, :])
                    store(k.s_sb[bass.ds(l, 1)].rearrange("a n t u h d -> (a n t) (u h d)"), kv[0:NS, QB, :])
                    store.wait()

                @block.tensor
                def _(pe):
                    def scores(h):
                        for b in range(QB):
                            u = QB * h + b
                            if u >= 3:
                                pe.wait_ge(split, u - 2)
                            pe.matmul(p_z[:, u % 3, 0:NP - P * b], ft[:, 4 + h, P * b:P * b + P], ft[:, h, P * b:NP], start=True, stop=True).then_inc(scored, 1)

                    def after(h):
                        for b in range(QB):
                            u = QB * h + b
                            if b == 0:
                                pe.wait_ge(logged, QB * (h + 1))
                            if u >= 2:
                                pe.wait_ge(summed_up, u - 1)
                            out = p_after[:, u % 2, :]
                            last = pe.matmul(out[:, 0:NP - P * b], k.c("later"), blk(miss, h, b), start=True, stop=(b == QB - 1))
                            for c in range(b + 1, QB):
                                last = pe.matmul(out[:, P * (c - b):NP - P * b], k.c("ones"), blk(miss, h, c), start=False, stop=(c == QB - 1))
                            last.then_inc(weighted, 1)

                    def apply(h):
                        if h >= 2:
                            pe.wait_ge(kept, h - 1)
                        pe.wait_ge(exped, QB * (h + 1))
                        pe.wait_ge(own, h + 1)
                        for b in range(QB):
                            last = pe.matmul(p_out[:, h % 2, P * b:NP], kv[:, b, 512 + P * h:640 + P * h], blk(logs, h, b), start=(b == 0), stop=(b == QB - 1))
                        last.then_inc(applied, 1)

                    scores(0)
                    for h in range(4):
                        if h + 1 < 4:
                            scores(h + 1)
                        after(h)
                        apply(h)

                @block.scalar
                def _(act):
                    def exps(h):
                        for b in range(QB):
                            m = blk(logs, h, b)
                            act.wait_ge(split, QB * h + b + 1)
                            act.activation(m, m, ACT.Exp, scale=-1.0).then_inc(shrunk, 1)

                    exps(0)
                    for h in range(4):
                        for b in range(QB):
                            m = blk(logs, h, b)
                            act.wait_ge(shrunk, QB * h + b + 1)
                            act.activation(m, m, ACT.Ln, bias=1.0).then_inc(opened, 1)
                        if h + 1 < 4:
                            exps(h + 1)
                        for b in range(QB):
                            w = blk(logs, h, b)
                            act.wait_ge(summed_up, QB * h + b + 1)
                            act.activation(w, w, ACT.Exp).then_inc(exped, 1)
                        if h >= 1:
                            act.wait_ge(applied, h)
                            act.copy(k.mixT[:, 4 + h - 1, 0:NP], p_out[:, (h - 1) % 2, :]).then_inc(kept, 1)
                    act.wait_ge(applied, 4)
                    act.copy(k.mixT[:, 7, 0:NP], p_out[:, 1, :]).then_inc(kept, 1)

                @block.gpsimd
                def _(pool):
                    for h in range(4):
                        pool.wait_ge(exped, QB * (h + 1))
                        for b in range(QB):
                            w = blk(logs, h, b, 0, P)
                            last = pool.tensor_tensor(w, w, k.c("before"), ALU.mult)
                        last.then_inc(own, 1)

                @block.vector
                def _(dve):
                    steps = Steps(dve, stepped)

                    def split_scores(h):
                        if h >= 2:
                            dve.wait_ge(applied, h - 1)
                        for b in range(QB):
                            u, z, low = QB * h + b, p_z[:, (QB * h + b) % 3, 0:NP - P * b], blk(miss, h, b)
                            dve.wait_ge(scored, u + 1)
                            steps.then(dve.tensor_scalar(low, z, SB_SCALE, None, ALU.mult))
                            dve.scalar_tensor_tensor(blk(logs, h, b), low, -1.0, low, ALU.mult, ALU.max).then_inc(split, 1)

                    split_scores(0)
                    for h in range(4):
                        for b in range(QB):
                            x, g = blk(logs, h, b), blk(miss, h, b)
                            dve.wait_ge(opened, QB * h + b + 1)
                            steps.then(dve.scalar_tensor_tensor(x, g, 0.0, x, ALU.min, ALU.subtract))
                            steps.then(dve.tensor_tensor(g, x, g, ALU.subtract))
                            dve.tensor_tensor(g[:, 0:P], g[:, 0:P], k.c("before"), ALU.mult).then_inc(logged, 1)
                        if h + 1 < 4:
                            split_scores(h + 1)
                        for b in range(QB):
                            u, n, x = QB * h + b, NP - P * b, blk(logs, h, b)
                            dve.wait_ge(weighted, u + 1)
                            dve.tensor_tensor(x, x, p_after[:, u % 2, 0:n], ALU.add).then_inc(summed_up, 1)
        stick_samples(nc, k, l, kv)


RING = 2 * PAGES


def stick_samples(nc, k, l, kv):
    ft = k.ft
    COLS = 4 * NS
    cache = k.cache_sb_kv.rearrange("l n t u h d -> (l n) t u (h d)")
    with ExitStack() as ctx:
        sb, ps = scope(nc, ctx)
        pages = kv[:, 0:QB, :].rearrange("p a (w x) -> p (a w) x", w=2)
        keys = sb("sbs_keys", [P, 2, 4, PAST])
        qs = k.scratch[:, :, :].rearrange("p a t -> p (a t)")[:, 0:NB * 4 * NS].rearrange("p (s h c) -> p s h c", s=NB, h=4)
        low = sb("sbs_low", [P, 5, COLS])
        mag = sb("sbs_mag", [P, 5, COLS])
        logs = sb("sbs_logs", [P, 5, COLS])
        miss = sb("sbs_miss", [P, 5, COLS])
        p_z = ps("sbs_p_z", [P, 2, 512])
        turned, copied_s, copied_v, scored, zeroed, spread, rows_v, rows_s = k.signals[:8]
        loaded = k.signals[8:8 + RING]

        def load_pages(engine, which, used, first, every):
            for u in range(first, NB * PAGES, every):
                if u >= RING:
                    used(u - RING)
                page = engine.value_load(k.pages[0:1, u:u + 1], min_val=0, max_val=POOL - 1)
                engine.dma_start(pages[:, u % RING, :], cache[bass.ds(l * POOL + page, 1), :, which].rearrange("a t x -> (a t) x")).then_inc(loaded[u % RING], 16)

        with ExitStack() as first:
            _, ps2 = scope(nc, first)
            p_keys = ps2("sbs_p_keys", [P, 2, 512])
            p_rows = ps2("sbs_p_rows", [NS, 4, 512])
            rows = keys[0:NS, 0, :, :]
            with stage(nc, k.signals) as block:
                @block.sync
                def _(sp):
                    load_pages(sp, 0, lambda u: sp.wait_ge(turned, u + 1), 0, 1)

                @block.gpsimd
                def _(pool):
                    pool.memset(qs, 0.0).then_inc(zeroed, 1)

                @block.tensor
                def _(pe):
                    for h in range(4):
                        pe.matmul(p_z[0:NS, 1, NS * h:NS * h + NS], ft[:, 4 + h, NP:NT], ft[:, h, NP:NT], start=True, stop=True)
                    pe.wait_ge(spread, 1)
                    for s in range(NB + 1):
                        if s < NB:
                            for u in range(PAGES * s, PAGES * (s + 1)):
                                pe.wait_ge(loaded[u % RING], 16 * (u // RING + 1))
                                if u >= 2:
                                    pe.wait_ge(copied_v if u % 2 == 0 else copied_s, u // 2)
                                for h in range(4):
                                    last = pe.transpose(p_keys[:, u % 2, P * h:P * h + P], pages[:, u % RING, P * h:P * h + P], k.c("ident"))
                                last.then_inc(turned, 1)
                        if s >= 1:
                            pe.wait_ge(copied_v, 2 * s)
                            pe.wait_ge(copied_s, 2 * s)
                            for h in range(4):
                                last = pe.matmul(p_rows[:, h, :], qs[:, s - 1, h, :], keys[:, (s - 1) % 2, h, :], start=(s == 1), stop=(s == NB))
                            last.then_inc(scored, 1)
                    pe.wait_ge(rows_v, 1)
                    pe.wait_ge(rows_s, 1)
                    for p in range(PAGES):
                        for h in range(4):
                            pe.transpose(p_z[:, 0, COLS * p + NS * h:COLS * p + NS * h + NS], rows[:, h, P * p:P * p + P], k.c("ident")[0:NS, 0:NS])

                def copies(engine, copy, copied, odd, written):
                    for u in range(odd, NB * PAGES, 2):
                        engine.wait_ge(turned, u + 1)
                        s, p = divmod(u, PAGES)
                        if s >= 2:
                            engine.wait_ge(scored, s - 1)
                        copy(keys[:, s % 2, :, P * p:P * p + P], p_keys[:, u % 2, :].rearrange("p (h t) -> p h t", h=4)).then_inc(copied, 1)
                    engine.wait_ge(scored, NB)
                    copy(rows[:, 2 * odd:2 * odd + 2, :], p_rows[:, 2 * odd:2 * odd + 2, :]).then_inc(written, 1)

                @block.vector
                def _(dve):
                    dve.wait_ge(zeroed, 1)
                    for s in range(NB):
                        last = dve.tensor_copy(qs[:, s, :, DS * s:DS * s + DS], ft[:, 0:4, NP + DS * s:NP + DS * s + DS])
                    last.then_inc(spread, 1)
                    copies(dve, dve.tensor_copy, copied_v, 0, rows_v)

                @block.scalar
                def _(act):
                    copies(act, act.copy, copied_s, 1, rows_s)

        p_after = ps("sbs_p_after", [P, 2, 512])
        scaled, shrunk, missed, summed, weighted, done = k.signals[:6]
        paged = lambda t: t[:, 0:4, :]
        new = lambda t: t[0:NS, 4, :]
        z = (p_z[:, 0, :].rearrange("p (g c) -> p g c", g=4), p_z[0:NS, 1, 0:COLS])
        both = (paged, new)
        with stage(nc, k.signals) as block:
            @block.vector
            def _(dve):
                step = Steps(dve, done)
                for i, part in enumerate(both):
                    step.then(dve.tensor_scalar(part(low), z[i], SB_SCALE, None, ALU.mult))
                    dve.scalar_tensor_tensor(part(mag), part(low), -1.0, part(low), ALU.mult, ALU.max).then_inc(scaled, 1)
                for i, part in enumerate(both):
                    dve.wait_ge(shrunk, 2 * i + 2)
                    step.then(dve.scalar_tensor_tensor(part(logs), part(low), 0.0, part(mag), ALU.min, ALU.subtract))
                    last = dve.tensor_tensor(part(miss), part(logs), part(low), ALU.subtract)
                    if i == 0:
                        last.then_inc(missed, 1)
                    else:
                        step.then(last)
                m = k.c("before_s")[0:NS].unsqueeze(1).to_broadcast([NS, 4, NS])
                g = new(miss).rearrange("p (h q) -> p h q", h=4)
                dve.tensor_tensor(g, g, m, ALU.mult).then_inc(missed, 1)
                dve.wait_ge(summed, 1)
                dve.tensor_tensor(paged(logs), paged(logs), p_after[:, 0, :].rearrange("p (g c) -> p g c", g=4), ALU.add).then_inc(weighted, 1)
                dve.tensor_tensor(new(logs), new(logs), p_after[0:NS, 1, 0:COLS], ALU.add).then_inc(weighted, 1)
                dve.wait_ge(shrunk, 6)
                g = new(logs).rearrange("p (h q) -> p h q", h=4)
                dve.tensor_tensor(g, g, m, ALU.mult)

            @block.scalar
            def _(act):
                for i, part in enumerate(both):
                    act.wait_ge(scaled, i + 1)
                    act.activation(part(mag), part(mag), ACT.Exp, scale=-1.0).then_inc(shrunk, 1)
                    act.wait_ge(shrunk, 2 * i + 1)
                    act.activation(part(mag), part(mag), ACT.Ln, bias=1.0).then_inc(shrunk, 1)
                for i, part in enumerate(both):
                    act.wait_ge(weighted, i + 1)
                    act.activation(part(logs), part(logs), ACT.Exp).then_inc(shrunk, 1)

            @block.tensor
            def _(pe):
                pe.wait_ge(missed, 2)
                for p in range(PAGES):
                    out = p_after[:, 0, COLS * p:COLS * p + COLS]
                    pe.matmul(out, k.c("later"), miss[:, p, :], start=True, stop=False)
                    for q in range(p + 1, PAGES):
                        pe.matmul(out, k.c("ones"), miss[:, q, :], start=False, stop=False)
                    pe.matmul(out, k.c("ones")[0:NS], new(miss), start=False, stop=True)
                pe.matmul(p_after[0:NS, 1, 0:COLS], k.c("later")[0:NS, 0:NS], new(miss), start=True, stop=True).then_inc(summed, 1)

        applied, copied, turned, kept, summed, arranged = k.signals[:6]
        p_new = ps("sbs_p_new", [P, 512])
        p_seq = ps("sbs_p_seq", [4 * DS, 2, 512])
        p_out = ps("sbs_p_out", [P, 512])
        seq = keys[0:4 * DS, :, 0, :]
        with stage(nc, k.signals) as block:
            @block.sync
            def _(sp):
                load_pages(sp, 1, lambda u: sp.wait_ge(applied, u + 1), 0, 2)

            @block.scalar
            def _(act):
                load_pages(act, 1, lambda u: act.wait_ge(applied, u + 1), 1, 2)

            @block.tensor
            def _(pe):
                for h in range(4):
                    last = pe.matmul(p_new[:, NS * h:NS * h + NS], kv[0:NS, QB, 512 + P * h:640 + P * h], new(logs)[:, NS * h:NS * h + NS], start=True, stop=True)
                last.then_inc(summed, 1)
                pe.wait_ge(arranged, 1)
                for s in range(NB + 1):
                    if s < NB:
                        if s >= 2:
                            pe.wait_ge(copied, s - 1)
                        for p in range(PAGES):
                            u = PAGES * s + p
                            pe.wait_ge(loaded[u % RING], 16 * (u // RING + 1))
                            pe.matmul(p_seq[:, s % 2, :], miss[:, p, 4 * DS * s:4 * DS * s + 4 * DS], pages[:, u % RING, :], start=(p == 0), stop=(p == PAGES - 1)).then_inc(applied, 1)
                    if s >= 1:
                        pe.wait_ge(copied, s)
                        for h in range(4):
                            col = 4 * DS * (4 * (s - 1) + h)
                            last = pe.transpose(p_out[:, col:col + 4 * DS], seq[:, (s - 1) % 2, P * h:P * h + P], k.c("ident")[0:4 * DS, 0:4 * DS])
                        last.then_inc(turned, 1)

            @block.vector
            def _(dve):
                for p in range(PAGES):
                    last = dve.tensor_copy(miss[:, p, :].rearrange("c (s h t) -> c s h t", s=NB, h=4),
                                           logs[:, p, :].rearrange("c (h s t) -> c s h t", h=4, s=NB))
                last.then_inc(arranged, 1)
                dve.wait_ge(summed, 1)
                dve.tensor_copy(low[:, 0, :], p_new[:, 0:COLS]).then_inc(kept, 1)
                for s in range(NB):
                    dve.wait_ge(applied, PAGES * (s + 1))
                    if s >= 2:
                        dve.wait_ge(turned, s - 1)
                    dve.tensor_copy(seq[:, s % 2, :], p_seq[:, s % 2, :]).then_inc(copied, 1)
                dve.wait_ge(turned, NB)
                dve.wait_ge(kept, 1)
                by_token = lambda t: t.rearrange("p (s t) -> p s t", t=DS)
                for h in range(4):
                    past = p_out[:, :].rearrange("p (s g c) -> p s g c", s=NB, g=4)[:, :, h, DS * h:DS * h + DS]
                    dve.tensor_tensor(by_token(k.mixT[:, 4 + h, NP:NT]), by_token(low[:, 0, NS * h:NS * h + NS]), past, ALU.add)


def take_top(dve, step, rounds, top, score, work, first=0):
    for r in range(first, rounds):
        src = score if r == 0 else work
        step.then(dve.max(top, src))
        step.then(dve.match_replace(work, top, src, NEG))


def sparse_attention(nc, k, l):
    ft = k.ft
    with ExitStack() as ctx:
        sb, ps = scope(nc, ctx)
        tm = sb("dsa_tm", [P, TT, DSA_W + 8])
        ikz = sb("dsa_ikz", [P, 2, NP])
        jobs = []
        for a in range(TT):
            n, cols = tokens(a)
            jobs.append(([ft[:, 4, cols], ft[:, 5, cols]], [(lambda b, n=n: b[0:n, 0:256], tm[0:n, a, 0:256])]))
            jobs.append(([ft[0:64, 6, cols], ft[0:8, 11, cols]], [(lambda b, n=n: b[0:n, 0:72], tm[0:n, a, 256:328])]))
        turn(nc, k, "dsa_in", jobs)

        stored, cleared, weighed = k.signals[:3]
        with stage(nc, k.signals) as block:
            @block.sync
            def _(sp):
                store = Loads(sp, stored)
                store(k.p_dsa[bass.ds(l, 1), 0].rearrange("a (n p) w -> p (a n) w", p=P), tm[:, 0:QB, 0:DSA_W])
                store(k.s_dsa[bass.ds(l, 1)].rearrange("a n t w -> (a n t) w"), tm[0:NS, QB, 0:DSA_W])
                store.wait()

            @block.gpsimd
            def _(pool):
                pool.memset(ikz[64:128, 0, :], 0.0)
                pool.memset(ikz[0:64, 1, :], 0.0)

            @block.vector
            def _(dve):
                for r in range(2):
                    dve.tensor_copy(ikz[64 * r:64 * r + 64, r, :], ft[64 * r:64 * r + 64, 6, 0:NP])
                dve.tensor_scalar(tm[:, 0:QB, 320:328], tm[:, 0:QB, 320:328], 8 ** -0.5, None, ALU.mult)
                dve.tensor_scalar(tm[0:NS, QB, 320:328], tm[0:NS, QB, 320:328], 8 ** -0.5, None, ALU.mult)

        arranged = SampleQueries(sb)
        sparse_prompt(nc, k, tm, ikz, arranged)
        sparse_samples(nc, k, l, tm, arranged)


class SampleQueries:

    def __init__(self, sb):
        self.iq = sb("dss_iq", [P, NB, 2, 4, DS])
        self.qs = sb("dss_q", [P, NB, 4, NS])
        self.wv = sb("dss_wv", [NS, NB])
        self.wx = sb("dss_wx", [NS, NB, P])

    def turn_weights(self, sp, k, tm, stored, loaded):
        sp.dma_start(k.sample_w, tm[0:NS, QB, 320:328]).then_inc(stored, 16)
        sp.wait_ge(stored, 16)
        load = Loads(sp, loaded)
        for r in range(2):
            for j in range(4):
                load(self.wv[16 * r + 4 * j:16 * r + 4 * j + 4, :], k.sample_w.rearrange("(s t) h -> h t s", t=DS)[2 * j + r])

    def arrange(self, pool, k, step, loaded):
        ft = k.ft
        step.then(pool.memset(self.iq[:, :, :, :, :], 0.0))
        step.then(pool.memset(self.qs[:, :, :, :], 0.0))
        for s in range(NB):
            tok = slice(NP + DS * s, NP + DS * s + DS)
            for r in range(2):
                step.then(pool.tensor_copy(self.iq[64 * r:64 * r + 64, s, r, :, :], ft[64 * r:64 * r + 64, 7:11, tok]))
            step.then(pool.tensor_copy(self.qs[:, s, :, DS * s:DS * s + DS], ft[:, 0:4, tok]))
        pool.wait_ge(loaded, 16 * 8)
        pool.tensor_tensor(self.wx[:, :, :], k.c("spread")[0:NS].rearrange("p (s c) -> p s c", s=NB),
                           self.wv[:, :].unsqueeze(2).to_broadcast([NS, NB, P]), ALU.mult)


def sparse_prompt(nc, k, tm, ikz, arranged):
    ft = k.ft
    with ExitStack() as ctx:
        sb, ps = scope(nc, ctx)
        rel = sb("dsa_rel", [P, 2, 512])
        score = sb("dsa_score", [P, 512])
        work = sb("dsa_work", [P, 512])
        top = sb("dsa_top", [P, 8])
        neg = sb("dsa_neg_row", [P, 2, 512])
        prob = sb("dsa_prob", [P, 2, 512])
        probT = sb("dsa_probT", [P, 2, 512])
        small = sb("dsa_small", [P, 2, 4])
        p_rel = ps("dsa_p_rel", [P, 2, 512])
        p_log = ps("dsa_p_log", [P, 2, 512])
        p_T = ps("dsa_p_T", [P, 2, 512])
        p_out = ps("dsa_p_out", [P, 2, 512])
        multiplied, rectified, added, looked, biased, exped, normed, turned, copied, applied, kept, own = k.signals[:12]
        stored, loaded, pool_stepped = k.signals[12:15]
        with stage(nc, k.signals) as block:
            @block.sync
            def _(sp):
                arranged.turn_weights(sp, k, tm, stored, loaded)

            @block.gpsimd
            def _(pool):
                arranged.arrange(pool, k, Steps(pool, pool_stepped), loaded)

            @block.tensor
            def _(pe):
                def index(q):
                    for h in range(8):
                        u = 8 * q + h
                        if u >= 2:
                            pe.wait_ge(rectified, u - 1)
                        pe.matmul(p_rel[:, u % 2, 0:P * (q + 1)], ft[:, 7 + h // 2, P * q:P * q + P], ikz[:, h % 2, 0:P * (q + 1)],
                                  start=True, stop=True).then_inc(multiplied, 1)

                def attend(q, h):
                    u = 4 * q + h
                    if h < 4:
                        if u >= 2:
                            pe.wait_ge(biased, u - 1)
                        pe.matmul(p_log[:, u % 2, 0:P * (q + 1)], ft[:, h, P * q:P * q + P], ft[:, 4, 0:P * (q + 1)],
                                  start=True, stop=True).then_inc(looked, 1)
                    if h >= 2:
                        v = u - 2
                        pe.wait_ge(normed, v + 1)
                        if v >= 2:
                            pe.wait_ge(copied, v - 1)
                        for b in range(q + 1):
                            last = pe.transpose(p_T[:, v % 2, P * b:P * b + P], prob[:, v % 2, P * b:P * b + P], k.c("ident"))
                        last.then_inc(turned, 1)
                        pe.wait_ge(copied, v + 1)
                        if v >= 2:
                            pe.wait_ge(kept, v - 1)
                        for b in range(q + 1):
                            last = pe.matmul(p_out[:, v % 2, 0:P], tm[:, b, P:2 * P], probT[:, v % 2, P * b:P * b + P], start=(b == 0), stop=(b == q))
                        last.then_inc(applied, 1)

                index(0)
                for q in range(1, QB + 1):
                    if q < QB:
                        index(q)
                    for h in range(6):
                        attend(q - 1, h)

            @block.scalar
            def _(act):
                def rectify(q):
                    for h in range(8):
                        u = 8 * q + h
                        act.wait_ge(multiplied, u + 1)
                        if u >= 2:
                            act.wait_ge(added, u - 1)
                        act.activation(rel[:, u % 2, 0:P * (q + 1)], p_rel[:, u % 2, 0:P * (q + 1)], ACT.Relu, scale=0.125).then_inc(rectified, 1)

                def attend(q, h):
                    w, u = P * (q + 1), 4 * q + h
                    if h < 4:
                        act.wait_ge(biased, u + 1)
                        act.activation(prob[:, u % 2, 0:w], prob[:, u % 2, 0:w], ACT.Exp, bias=small[:, u % 2, 0:1],
                                       accum_out=small[:, u % 2, 1:2]).then_inc(exped, 1)
                    if h >= 1:
                        v = u - 1
                        act.wait_ge(turned, v + 1)
                        if v >= 2:
                            act.wait_ge(applied, v - 1)
                        act.copy(probT[:, v % 2, 0:w], p_T[:, v % 2, 0:w]).then_inc(copied, 1)
                        act.wait_ge(applied, v + 1)
                        act.copy(k.mixT[:, 8 + h - 1, P * q:P * q + P], p_out[:, v % 2, 0:P]).then_inc(kept, 1)

                rectify(0)
                for q in range(1, QB + 1):
                    if q < QB:
                        rectify(q)
                    for h in range(5):
                        attend(q - 1, h)

            @block.vector
            def _(dve):
                step = Steps(dve, own)

                def add_scores(q):
                    w = P * (q + 1)
                    s = score[:, 0:w]
                    for h in range(8):
                        u = 8 * q + h
                        dve.wait_ge(rectified, u + 1)
                        g = tm[:, q, 320 + h:321 + h]
                        if h == 0:
                            last = dve.tensor_scalar(s, rel[:, u % 2, 0:w], g, None, ALU.mult)
                        else:
                            last = dve.scalar_tensor_tensor(s, rel[:, u % 2, 0:w], g, s, ALU.mult, ALU.add)
                        last.then_inc(added, 1)
                        dve.wait_ge(added, u + 1)

                def attend(q, h):
                    w = P * (q + 1)
                    n = neg[:, q % 2, 0:w]
                    u = 4 * q + h
                    if h < 4:
                        p, m = prob[:, u % 2, 0:w], small[:, u % 2, 0:1]
                        dve.wait_ge(looked, u + 1)
                        if u >= 2:
                            dve.wait_ge(turned, u - 1)
                        step.then(dve.scalar_tensor_tensor(p, p_log[:, u % 2, 0:w], SB_SCALE, n, ALU.mult, ALU.add))
                        dve.tensor_reduce(m, p, AX.X, ALU.max, negate=True).then_inc(biased, 1)
                    if h >= 1:
                        v = u - 1
                        dve.wait_ge(exped, v + 1)
                        step.then(dve.reciprocal(small[:, v % 2, 2:3], small[:, v % 2, 1:2]))
                        dve.tensor_scalar(prob[:, v % 2, 0:w], prob[:, v % 2, 0:w], small[:, v % 2, 2:3], None, ALU.mult).then_inc(normed, 1)

                add_scores(0)
                step.then(dve.tensor_copy(neg[:, 0, 0:P], k.c("dsa_neg")))
                for q in range(1, QB):
                    w = P * (q + 1)
                    s, d, n = score[:, 0:w], score[:, P * q:w], neg[:, q % 2, 0:w]
                    add_scores(q)
                    step.then(dve.tensor_tensor(d, d, k.c("dsa_neg"), ALU.add))
                    for h in range(5):
                        take_top(dve, step, 3 * h + 3, top[:, :], s, work[:, 0:w], first=3 * h)
                        attend(q - 1, h)
                    take_top(dve, step, TOPK // 8, top[:, :], s, work[:, 0:w], first=15)
                    step.then(dve.tensor_tensor(n, work[:, 0:w], s, ALU.is_equal))
                    step.then(dve.tensor_scalar(n, n, NEG, None, ALU.mult))
                for h in range(5):
                    attend(QB - 1, h)


def sparse_samples(nc, k, l, tm, arranged):
    ft = k.ft
    WIDE = PAST + NS
    cache = k.cache_dsa.rearrange("l n t w -> (l n) t w")
    with ExitStack() as ctx:
        sb, ps = scope(nc, ctx)
        iq, qs, wx = arranged.iq, arranged.qs, arranged.wx
        with ExitStack() as inner:
            sb2, ps2 = scope(nc, inner)
            score = sb2("dss_score", [P, WIDE])
            logit = sb2("dss_logit", [P, WIDE])
            with ExitStack() as first:
                sb3, ps3 = scope(nc, first)
                pages = sb3("dss_pages", [P, 2, PAGES, DSA_W + 64])
                keys = sb3("dss_keys", [P, 2, PAST])
                ikeys = sb3("dss_ikeys", [P, 2, PAST])
                rel = k.scratch[0:NS]
                p_keys, p_ikeys, p_rel, p_reln, p_score, p_scoren, p_log = (ps3(f"dss_p{i}", [P, 512]) for i in range(7))
                loaded0, loaded1, turned, copied_v, copied_s, related, rectified, summed, looked, doubled = k.signals[:10]
                with stage(nc, k.signals) as block:
                    @block.sync
                    def _(sp):
                        loads = [Loads(sp, loaded0), Loads(sp, loaded1)]
                        for s in range(NB):
                            if s >= 2:
                                sp.wait_ge(turned, s - 1)
                            for p in range(PAGES):
                                page = sp.value_load(k.pages[0:1, PAGES * s + p:PAGES * s + p + 1], min_val=0, max_val=POOL - 1)
                                loads[s % 2](pages[:, s % 2, p, 0:DSA_W], cache[bass.ds(l * POOL + page, 1)].rearrange("a t w -> (a t) w"))

                    @block.gpsimd
                    def _(pool):
                        for s in range(NB):
                            pool.wait_ge((loaded0, loaded1)[s % 2], 16 * PAGES * (s // 2 + 1))
                            pool.tensor_copy(pages[:, s % 2, :, DSA_W:DSA_W + 64], pages[:, s % 2, :, 256:DSA_W]).then_inc(doubled, 1)

                    @block.tensor
                    def _(pe):
                        for s in range(NB):
                            pe.wait_ge(doubled, s + 1)
                            if s >= 1:
                                pe.wait_ge(copied_v, s)
                                pe.wait_ge(copied_s, s)
                            for p in range(PAGES):
                                pe.transpose(p_keys[:, P * p:P * p + P], pages[:, s % 2, p, 0:P], k.c("ident"))
                                last = pe.transpose(p_ikeys[:, P * p:P * p + P], pages[:, s % 2, p, 256:384], k.c("ident"))
                            last.then_inc(turned, 1)
                            pe.wait_ge(copied_v, s + 1)
                            pe.wait_ge(copied_s, s + 1)
                            if s >= 1:
                                pe.wait_ge(rectified, 2 * s)
                            mine = iq[:, s].rearrange("p r j t -> p (r j t)")
                            pe.matmul(p_rel[0:NS, :], mine, ikeys[:, s % 2, :], start=True, stop=True)
                            pe.matmul(p_reln[0:NS, 0:NS], mine, ft[:, 6, NP:NT], start=True, stop=True).then_inc(related, 1)
                            pe.matmul(p_log[:, :], qs[:, s].rearrange("p h c -> p (h c)"), keys[:, s % 2, :], start=(s == 0), stop=(s == NB - 1)).then_inc(looked, 1)
                            pe.wait_ge(rectified, 2 * s + 2)
                            pe.matmul(p_score[:, :], wx[:, s, :], rel[:, s % 2, 0:PAST], start=(s == 0), stop=(s == NB - 1))
                            pe.matmul(p_scoren[:, 0:NS], wx[:, s, :], rel[:, s % 2, PAST:WIDE], start=(s == 0), stop=(s == NB - 1)).then_inc(summed, 1)
                        for s in range(NB):
                            last = pe.matmul(p_reln[:, 0:NS], qs[:, s].rearrange("p h c -> p (h c)"), ft[:, 4, NP:NT], start=(s == 0), stop=(s == NB - 1))
                        last.then_inc(summed, 1)

                    @block.vector
                    def _(dve):
                        for s in range(NB):
                            dve.wait_ge(turned, s + 1)
                            if s >= 2:
                                dve.wait_ge(looked, s - 1)
                            dve.tensor_copy(keys[:, s % 2, :], p_keys[:, :]).then_inc(copied_v, 1)
                        dve.wait_ge(summed, NB + 1)
                        dve.tensor_copy(score[:, 0:PAST], p_score[:, :])
                        dve.tensor_tensor(score[:, PAST:WIDE], p_scoren[:, 0:NS], k.c("dsa_neg_s"), ALU.add)
                        dve.tensor_scalar(logit[:, PAST:WIDE], p_reln[:, 0:NS], SB_SCALE, None, ALU.mult)

                    @block.scalar
                    def _(act):
                        for s in range(NB):
                            act.wait_ge(turned, s + 1)
                            if s >= 2:
                                act.wait_ge(related, s - 1)
                            act.copy(ikeys[:, s % 2, :], p_ikeys[:, :]).then_inc(copied_s, 1)
                            act.wait_ge(related, s + 1)
                            if s >= 2:
                                act.wait_ge(summed, s - 1)
                            act.activation(rel[:, s % 2, 0:PAST], p_rel[0:NS, :], ACT.Relu, scale=0.125).then_inc(rectified, 1)
                            act.activation(rel[:, s % 2, PAST:WIDE], p_reln[0:NS, 0:NS], ACT.Relu, scale=0.125).then_inc(rectified, 1)
                        act.wait_ge(looked, NB)
                        act.activation(logit[:, 0:PAST], p_log[:, :], ACT.Copy, scale=SB_SCALE)

            PAD = 7
            work = sb2("dss_work", [P, WIDE + PAD])
            top = sb2("dss_top", [P, 2, 8])
            small = sb2("dss_small", [P, 4])
            probT = sb2("dss_probT", [P, 5, P])
            vals = sb2("dss_vals", [P, NB, PAGES, P])
            p_T = ps2("dss_p_T", [P, 512])
            p_Tn = ps2("dss_p_Tn", [P, 512])
            p_out = ps2("dss_p_out", [P, 512])
            own, biased, exped, normed, turned, copied, loaded, applied = k.signals[:8]
            with stage(nc, k.signals) as block:
                @block.sync
                def _(sp):
                    load = Loads(sp, loaded)
                    for u in range(NB * PAGES):
                        page = sp.value_load(k.pages[0:1, u:u + 1], min_val=0, max_val=POOL - 1)
                        load(vals[:, u // PAGES, u % PAGES, :], cache[bass.ds(l * POOL + page, 1)].rearrange("a t w -> (a t) w")[:, P:2 * P])

                @block.vector
                def _(dve):
                    step = Steps(dve, own)
                    take_top(dve, step, TOPK_S // 8, top[:, 0, :], score[:, :], work[:, 0:WIDE])
                    step.then(dve.max(top[:, 0, :], work[:, 0:WIDE]))
                    dve.memset(top[:, 1, 0:PAD], -NEG)
                    step(dve.memset(work[:, WIDE:WIDE + PAD], -NEG))
                    step.then(dve.tensor_copy(top[:, 1, PAD:8], top[:, 0, 0:1]))
                    step.then(dve.match_replace(work[:, :], top[:, 1, :], work[:, :], NEG))
                    step.then(dve.tensor_tensor(work[:, 0:WIDE], work[:, 0:WIDE], score[:, :], ALU.is_equal))
                    step.then(dve.scalar_tensor_tensor(logit[:, :], work[:, 0:WIDE], NEG, logit[:, :], ALU.mult, ALU.add))
                    dve.tensor_reduce(small[:, 0:1], logit[:, :], AX.X, ALU.max, negate=True).then_inc(biased, 1)
                    dve.wait_ge(exped, 1)
                    step.then(dve.reciprocal(small[:, 2:3], small[:, 1:2]))
                    dve.tensor_scalar(logit[:, :], logit[:, :], small[:, 2:3], None, ALU.mult).then_inc(normed, 1)
                    dve.wait_ge(turned, 1)
                    dve.tensor_copy(probT[:, 0:4, :], p_T[:, :].rearrange("p (g c) -> p g c", g=4)).then_inc(copied, 1)
                    dve.tensor_copy(probT[0:NS, 4, :], p_Tn[0:NS, 0:P]).then_inc(copied, 1)

                @block.scalar
                def _(act):
                    act.wait_ge(biased, 1)
                    act.activation(logit[:, :], logit[:, :], ACT.Exp, bias=small[:, 0:1], accum_out=small[:, 1:2]).then_inc(exped, 1)
                    act.wait_ge(applied, 1)
                    act.copy(k.mixT[:, 8:12, NP:NT], p_out[:, 0:P].rearrange("p (h t) -> p h t", h=4))

                @block.tensor
                def _(pe):
                    pe.wait_ge(normed, 1)
                    for g in range(4):
                        pe.transpose(p_T[:, P * g:P * g + P], logit[:, P * g:P * g + P], k.c("ident"))
                    pe.transpose(p_Tn[0:NS, 0:P], logit[:, PAST:WIDE], k.c("ident")).then_inc(turned, 1)
                    pe.wait_ge(copied, 2)
                    pe.matmul(p_out[:, 0:P], tm[0:NS, QB, P:2 * P], probT[0:NS, 4, :], start=True, stop=False, skip_group_check=True)
                    pe.wait_ge(loaded, 16 * PAGES * NB)
                    for s in range(NB):
                        for p in range(PAGES):
                            def mine(t):
                                return t.rearrange("p (h c) -> p h c", h=4)[:, :, DS * s:DS * s + DS]
                            last = pe.matmul(mine(p_out[:, 0:P]), vals[:, s, p, :], mine(probT[:, p, :]), start=False, stop=(p == PAGES - 1), skip_group_check=True)
                    last.then_inc(applied, 1)


R_SLOT, WL_SLOT, K_SLOT, V_SLOT, AL_SLOT, RG_SLOT = 0, 4, 5, 9, 13, 14
SHIFT_RUNS = ((0, 4, P, 0), (4, 1, LORA, 512), (5, 4, P, 608), (9, 4, P, 1120), (13, 1, LORA, 1632))
HALF = 32
KK_SCALE = 2.0 ** 20


def rwkv(nc, k, l):
    with ExitStack() as ctx:
        sb, _ = scope(nc, ctx)
        k.bonus = sb("rw_bonus", [P, 4, NT])
        k.kr = sb("rw_kr", [P, 4, NC, 2, C])
        k.bk = sb("rw_bk", [P, 4, NC, 2, C])
        k.ends = sb("rw_ends", [P, 4, NC])
        token_shift(nc, k, l)
        with ExitStack() as inner:
            rwkv_vectors(nc, k, l, inner)
            store_sample_rows(nc, k)
        rwkv_chunks(nc, k, l)
        rwkv_out(nc, k)
    gate(nc, k, 12, RG_SLOT)


def token_shift(nc, k, l):
    ft = k.ft
    with ExitStack() as ctx:
        sb, _ = scope(nc, ctx)
        rows = sb("ts_rows", [NB, SHIFT_W])
        last_p = sb("ts_last_p", [1, SHIFT_W])
        last_s = sb("ts_last_s", [NB, SHIFT_W])
        first = sb("ts_first", [P, 14, NB])
        diff = sb("ts_diff", [P, 4, NT])
        loaded, stepped = k.signals[:2]
        with stage(nc, k.signals) as block:
            @block.sync
            def _(sp):
                sp.dma_start(rows[:, :], k.state_shift[bass.ds(l, 1)].rearrange("a n w -> (a n) w")).then_inc(loaded, 16)
                sp.wait_ge(loaded, 16)
        jobs = []
        for slot, count, w, col in SHIFT_RUNS:
            jobs.append(([rows[:, col + w * i:col + w * i + w] for i in range(count)],
                         [(lambda b, w=w, n=count: b[0:w, 0:NB * n].rearrange("p (i s) -> p i s", s=NB), first[0:w, slot:slot + count, :])]))
        width = {s: (LORA if s in (WL_SLOT, AL_SLOT) else P) for s in range(14)}
        at = 0
        for slots in (range(0, 4), range(4, 8), range(8, 12), range(12, 14)):
            w = sum(width[s] for s in slots)
            jobs.append(([ft[0:width[s], s, NP - 1:NP] for s in slots], [(lambda b, w=w: b[0:1, 0:w], last_p[:, at:at + w])]))
            jobs.append(([ft[0:width[s], s, NP + DS - 1:NT:DS] for s in slots], [(lambda b, w=w: b[0:NB, 0:w], last_s[:, at:at + w])]))
            at += w
        turn(nc, k, "ts", jobs)
        with stage(nc, k.signals) as block:
            @block.sync
            def _(sp):
                store = Loads(sp, loaded)
                store(k.p_shift[bass.ds(l, 1)].rearrange("a n w -> (a n) w"), last_p[:, :])
                store(k.s_shift[bass.ds(l, 1)].rearrange("a n w -> (a n) w"), last_s[:, :])
                store.wait()

            @block.vector
            def _(dve):
                step = Steps(dve, stepped)
                for slot, n, w, col in SHIFT_RUNS:
                    x, d = ft[0:w, slot:slot + n, :], diff[0:w, 0:n, :]
                    seqs = lambda t, i: t[:, i, NP:NT].rearrange("p (s t) -> p s t", t=DS)
                    dve.tensor_tensor(d[:, :, 1:NP], x[:, :, 0:NP - 1], x[:, :, 1:NP], ALU.subtract)
                    dve.tensor_scalar(d[:, :, 0:1], x[:, :, 0:1], -1.0, None, ALU.mult)
                    for i in range(n):
                        dve.tensor_tensor(seqs(d, i)[:, :, 1:DS], seqs(x, i)[:, :, 0:DS - 1], seqs(x, i)[:, :, 1:DS], ALU.subtract)
                        last = dve.tensor_tensor(seqs(d, i)[:, :, 0], first[0:w, slot + i, :], seqs(x, i)[:, :, 0], ALU.subtract)
                    step.then(last)
                    for i in range(n):
                        last = dve.scalar_tensor_tensor(x[:, i, :], d[:, i, :], k.prm[0:w, ROW_MU + slot + i:ROW_MU + slot + i + 1], x[:, i, :], ALU.mult, ALU.add)
                    step.then(last)


def rwkv_vectors(nc, k, l, outer):
    ft = k.ft
    sb, _ = scope(nc, outer)
    logw = sb("rv_logw", [P, 4, NT])
    beta = sb("rv_beta", [P, 4, NT])
    kap = sb("rv_kap", [P, 4, NT])
    lora = sb("rv_lora", [LORA, 2, GW])
    minus = sb("rv_minus", [P, 8])
    with ExitStack() as ctx:
        sb2, ps = scope(nc, ctx)
        tmp = sb2("rv_tmp", [P, 2, NT])
        prod = ps("rv_prod", [P, 2, 2, 512])
        loaded, negated, doubled, stepped, opened, multiplied, halved = k.signals[:7]
        th = ft[0:LORA, WL_SLOT, :]
        with stage(nc, k.signals) as block:
            @block.sync
            def _(sp):
                load = Loads(sp, loaded)
                load(lora[:, 0, :], k.rw_w2[bass.ds(l, 1)].rearrange("a r c -> (a r) c"))
                load(lora[:, 1, :], k.rw_a2[bass.ds(l, 1)].rearrange("a r c -> (a r) c"))

            @block.scalar
            def _(act):
                act.activation(th, th, ACT.Exp, scale=2.0).then_inc(doubled, 1)
                act.wait_ge(negated, 2)
                for u in range(8):
                    act.wait_ge(multiplied, u + 1)
                    out, i = (logw, beta)[u % 2], u // 2
                    bias = minus[:, 4 * (u % 2) + i:4 * (u % 2) + i + 1]
                    act.activation(out[:, i, 0:NP], prod[:, u % 2, 0, :], ACT.Exp, scale=-1.0, bias=bias).then_inc(opened, 1)
                    act.activation(out[:, i, NP:NT], prod[:, u % 2, 1, 0:NS], ACT.Exp, scale=-1.0, bias=bias).then_inc(opened, 1)

            @block.tensor
            def _(pe):
                pe.wait_ge(loaded, 32)
                pe.wait_ge(halved, 1)
                for u in range(8):
                    if u >= 2:
                        pe.wait_ge(opened, 2 * (u - 1))
                    x = ft[0:LORA, (WL_SLOT, AL_SLOT)[u % 2], :]
                    w = lora[:, u % 2, P * (u // 2):P * (u // 2) + P]
                    pe.matmul(prod[:, u % 2, 0, :], w, x[:, 0:NP], start=True, stop=True)
                    pe.matmul(prod[:, u % 2, 1, 0:NS], w, x[:, NP:NT], start=True, stop=True).then_inc(multiplied, 1)

            @block.vector
            def _(dve):
                step = Steps(dve, stepped)
                dve.tensor_scalar(minus[:, 0:4], k.prm[:, ROW_W0:ROW_W0 + 4], -1.0, None, ALU.mult).then_inc(negated, 1)
                dve.tensor_scalar(minus[:, 4:8], k.prm[:, ROW_A0:ROW_A0 + 4], -1.0, None, ALU.mult).then_inc(negated, 1)
                dve.wait_ge(doubled, 1)
                step.then(dve.tensor_scalar(th, th, 1.0, None, ALU.add))
                step.then(dve.reciprocal(th, th))
                dve.tensor_scalar(th, th, -2.0, 1.0, ALU.mult, ALU.add).then_inc(halved, 1)
                for u in range(8):
                    x = (logw, beta)[u % 2][:, u // 2, :]
                    dve.wait_ge(opened, 2 * u + 2)
                    step.then(dve.tensor_scalar(x, x, 1.0, None, ALU.add))
                    step.then(dve.reciprocal(x, x))
                    if u % 2 == 0:
                        step.then(dve.tensor_scalar(x, x, -float(np.exp(-0.5)), None, ALU.mult))

        def col(row, i):
            return k.prm[:, row + i:row + i + 1]

        squared, summed, bounded, inverted, stepped, logged, bonused = k.signals[:7]
        prod_s = ps("rv_prod_s", [P, 2, 512])
        norms = sb2("rv_norms", [P, 4, NT])
        with stage(nc, k.signals) as block:
            @block.vector
            def _(dve):
                step = Steps(dve, stepped)
                for i in range(4):
                    kx, z = ft[:, K_SLOT + i, :], tmp[:, i % 2, :]
                    step.then(dve.tensor_scalar(kap[:, i, :], kx, col(ROW_KK, i), None, ALU.mult))
                    dve.tensor_tensor(norms[:, i, :], kap[:, i, :], kap[:, i, :], ALU.mult).then_inc(squared, 1)
                    if i >= 2:
                        dve.wait_ge(summed, 2 * (i - 1))
                    step.then(dve.tensor_scalar(z, beta[:, i, :], -1.0, col(ROW_KA, i), ALU.add, ALU.mult))
                    step.then(dve.scalar_tensor_tensor(kx, z, 1.0, kx, ALU.add, ALU.mult))
                    dve.scalar_tensor_tensor(z, ft[:, R_SLOT + i, :], col(ROW_RK, i), kx, ALU.mult, ALU.mult).then_inc(bonused, 1)
                    dve.wait_ge(summed, 2 * i + 1)
                    for cols, total in ((slice(0, NP), prod[:, i % 2, 0, :]), (slice(NP, NT), prod_s[:, 0, NS * i:NS * i + NS])):
                        dve.tensor_scalar(norms[:, i, cols], total, 1e-24, None, ALU.max).then_inc(bounded, 1)
                    dve.wait_ge(summed, 2 * i + 2)
                    for cols, total in ((slice(0, NP), prod[:, i % 2, 1, :]), (slice(NP, NT), prod_s[:, 1, NS * i:NS * i + NS])):
                        last = dve.tensor_tensor(k.bonus[:, i, cols], total, ft[:, V_SLOT + i, cols], ALU.mult)
                    step(last)
                for i in range(4):
                    dve.wait_ge(inverted, i + 1)
                    step.then(dve.scalar_tensor_tensor(kap[:, i, :], kap[:, i, :], -KK_SCALE ** 0.5, norms[:, i, :], ALU.mult, ALU.mult))
                    dve.scalar_tensor_tensor(beta[:, i, :], kap[:, i, :], -1.0, beta[:, i, :], ALU.mult, ALU.mult)

            @block.tensor
            def _(pe):
                for i in range(4):
                    for kind, x, ready in ((0, norms[:, i, :], squared), (1, tmp[:, i % 2, :], bonused)):
                        pe.wait_ge(ready, i + 1)
                        if i >= 1:
                            pe.wait_ge(bounded, 2 * i)
                            pe.wait_ge(stepped, 4 * i)
                        pe.matmul(prod[:, i % 2, kind, :], k.c("head_ones"), x[:, 0:NP], start=True, stop=True)
                        pe.matmul(prod_s[:, kind, NS * i:NS * i + NS], k.c("head_ones"), x[:, NP:NT], start=True, stop=True).then_inc(summed, 1)

            @block.scalar
            def _(act):
                inverse_roots(act, bounded, logged, inverted, norms, scale=KK_SCALE)

        lam = sb2("rv_lam", [P, 2, NP])
        exps = sb2("rv_exps", [P, 2, 3, NP])
        summed, shifted, exped, used, ended = k.signals[:5]
        with stage(nc, k.signals) as block:
            @block.vector
            def _(dve):
                for i in range(5):
                    if i < 4:
                        w = logw[:, i, 0:NP]
                        if i >= 2:
                            dve.wait_ge(exped, 3 * (i - 1))
                        dve.tensor_tensor_scan(lam[:, i % 2, :], k.c("chunk_in"), w, 0.0, ALU.mult, ALU.add).then_inc(summed, 1)
                        dve.wait_ge(summed, i + 1)
                        dve.tensor_tensor(tmp[:, i % 2, 0:NP], lam[:, i % 2, :], w, ALU.subtract).then_inc(shifted, 1)
                    if i >= 1:
                        j = i - 1
                        up, down, before = (exps[:, j % 2, x, :].rearrange("p (c t) -> p c t", t=C) for x in range(3))
                        tok = lambda t: t[:, 0:NP].rearrange("p (c t) -> p c t", t=C)
                        dve.wait_ge(exped, 3 * j + 3)
                        dve.tensor_tensor(k.kr[:, j, :, 0, :], tok(kap[:, j, :]), before, ALU.mult)
                        dve.tensor_tensor(k.kr[:, j, :, 1, :], tok(ft[:, R_SLOT + j, :]), up, ALU.mult)
                        dve.tensor_tensor(k.bk[:, j, :, 0, :], tok(beta[:, j, :]), down, ALU.mult)
                        dve.tensor_tensor(k.bk[:, j, :, 1, :], tok(ft[:, K_SLOT + j, :]), down, ALU.mult)
                        dve.tensor_copy(k.ends[:, j, :], up[:, :, C - 1]).then_inc(used, 1)

            @block.scalar
            def _(act):
                for i in range(4):
                    if i >= 2:
                        act.wait_ge(used, i - 1)
                    act.wait_ge(summed, i + 1)
                    act.activation(exps[:, i % 2, 0, :], lam[:, i % 2, :], ACT.Exp).then_inc(exped, 1)
                    act.activation(exps[:, i % 2, 1, :], lam[:, i % 2, :], ACT.Exp, scale=-1.0).then_inc(exped, 1)
                    act.wait_ge(shifted, i + 1)
                    act.activation(exps[:, i % 2, 2, :], tmp[:, i % 2, 0:NP], ACT.Exp).then_inc(exped, 1)
                act.activation(logw[:, :, NP:NT], logw[:, :, NP:NT], ACT.Exp).then_inc(ended, 1)
    k.sample_sources = (ft[:, R_SLOT:R_SLOT + 4], logw, ft[:, K_SLOT:K_SLOT + 4], ft[:, V_SLOT:V_SLOT + 4], kap, beta)


def store_sample_rows(nc, k):
    with ExitStack() as ctx:
        sb, _ = scope(nc, ctx)
        rows = sb("rs_rows", [NS, 6, GW])
        turn(nc, k, "rs", [([t[:, i, NP:NT] for i in range(4)], [(lambda b: b[0:NS, :], rows[:, n, :])])
                           for n, t in enumerate(k.sample_sources)])
        with stage(nc, k.signals) as block:
            @block.sync
            def _(sp):
                sp.dma_start(k.sample_rows, rows[:, :, :].rearrange("p v c -> p (v c)")).then_inc(k.signals[0], 16)
                sp.wait_ge(k.signals[0], 16)


class Samples:

    def __init__(self, nc, k, l, sb):
        self.k, self.l = k, l
        self.vec = sb("rs_vec", [P, DS, 6, C])
        self.state = k.mixT[:, 12:16, :].rearrange("p k t -> p (k t)")[:, 0:HALF * C].rearrange("p (i j) -> p i j", j=C)
        self.tmp = sb("rs_tmp", [P, HALF, C])
        self.mine = sb("rs_mine", [P, DS, HALF])
        self.other = sb("rs_other", [P, DS, HALF])
        self.sa = sb("rs_sa", [P, HALF])
        self.y = sb("rs_y", [P, DS, HALF])

    def load(self, load, halves):
        k = self.k
        if 0 in halves:
            load(self.state, k.state_wkv[bass.ds(self.l, 1)].rearrange("a s h (b i) j -> (a s h b) i j", b=2))
        for s in range(NB):
            for half in halves:
                load(self.vec[16 * s + half:16 * s + 16:2], k.sample_rows.rearrange("(s t) (v h d) -> s h t v d", t=DS, v=6, h=H8)[s])
        load.wait()

    def choose(self, dve, step):
        step.then(dve.tensor_scalar(self.mine[:, :, :], self.vec[:, :, 3, 0:HALF], self.k.c("half0"), None, ALU.mult))
        step.then(dve.tensor_scalar(self.other[:, :, :], self.vec[:, :, 3, HALF:C], self.k.c("half1"), None, ALU.mult))
        dve.tensor_tensor(self.mine[:, :, :], self.mine[:, :, :], self.other[:, :, :], ALU.add)

    def advance(self, pool, step, reduced, t):
        S, Z = self.state, self.tmp[:, :, :]
        over_i = lambda n: self.vec[:, t, n, :].unsqueeze(1).to_broadcast([P, HALF, C])
        over_j = lambda v: v.unsqueeze(2).to_broadcast([P, HALF, C])
        step.then(pool.tensor_tensor(Z, S, over_i(4), ALU.mult))
        step(pool.tensor_tensor(S, S, over_i(1), ALU.mult))
        pool.wait_ge(reduced, 1)
        step.then(pool.tensor_tensor(Z, over_j(self.sa[:, :]), over_i(5), ALU.mult))
        step.then(pool.tensor_tensor(S, S, Z, ALU.add))
        step.then(pool.tensor_tensor(Z, over_j(self.mine[:, t, :]), over_i(2), ALU.mult))
        step.then(pool.tensor_tensor(S, S, Z, ALU.add))
        step.then(pool.tensor_tensor(Z, S, over_i(0), ALU.mult))

    def store_states(self, store):
        store(self.k.s_wkv[bass.ds(self.l, 1)].rearrange("a s h (b i) j -> (a s h b) i j", b=2), self.state)

    def store(self, store, back, row):
        k = self.k
        for s in range(NB):
            store(k.sample_y.rearrange("(s t) (g i) -> s g t i", t=DS, i=HALF)[s], self.y[16 * s:16 * s + 16])
        store.wait()
        back(row, k.sample_y)
        back.wait()


def rwkv_chunks(nc, k, l):
    ft = k.ft
    with ExitStack() as ctx:
        sb, ps = scope(nc, ctx)
        state = sb("rc_state", [P, 2, 4, P])
        x_mat, u_mat = sb("rc_x", [P, 4, P]), sb("rc_u", [P, 4, P])
        own = {n: sb(f"rc_{n}", [P, 2, 4, P]) for n in "a b c e f g k_kappa v_rows beta_rows k_rows".split()}
        samples = Samples(nc, k, l, sb)
        zeroed = [own[n][:] for n in ("a", "b", "c", "e", "f", "k_kappa")]
        spare = ft[:, WL_SLOT:V_SLOT, :].rearrange("p s t -> p (s t)")
        spare = [spare[:, 8 * P * i:8 * P * (i + 1)].rearrange("p (q j t) -> p q j t", q=2, j=4) for i in range(2)]
        zeroed += spare
        held = dict(beta="a", n4="a", rT="a", k="b", n4T="b", dT="b", v="c", inv="c",
                    blockT="e", n2="e", n8T="e", r1="e", block="f", n2T="f", r="f", d="g", total="g")
        mats = {n: own[b] for n, b in held.items()} | {n: own[n] for n in ("k_kappa", "v_rows", "beta_rows", "k_rows")}
        mats.update(kappa=spare[0], restT=spare[1], r2T=spare[1])
        beta_r, k_r = sb("rc_beta_r", [P, 2, 4, C]), sb("rc_k_r", [P, 2, 4, C])
        banks = ExitStack()
        _, ps = scope(nc, banks)
        bank = [[ps(f"rc_p{q}{n}", [P, 512]) for n in "wxyz"] for q in range(2)]
        pairs = lambda t: t[:, :].rearrange("p (j f) -> p j f", j=4)
        mask = lambda name: k.c(name).unsqueeze(1).to_broadcast([P, 4, C])
        eye = k.c("ident").unsqueeze(1).to_broadcast([P, 4, P])
        LOW, UP = slice(0, C), slice(C, P)
        loaded, loaded_too, chosen = k.signals[:3]
        with stage(nc, k.signals) as block:
            @block.sync
            def _(sp):
                samples.load(Loads(sp, loaded), (0,))

            @block.scalar
            def _(act):
                samples.load(Loads(act, loaded_too), (1,))

            @block.vector
            def _(dve):
                dve.memset(state[:], 0.0)
                for t in zeroed[0::2]:
                    dve.memset(t, 0.0)
                dve.wait_ge(loaded, 16 * (1 + NB))
                dve.wait_ge(loaded_too, 16 * NB)
                samples.choose(dve, Steps(dve, chosen))

            @block.gpsimd
            def _(pool):
                for t in zeroed[1::2]:
                    pool.memset(t, 0.0)

        made, by_v, by_s, by_p = (k.signals[2 * i:2 * i + 2] for i in range(4))
        advanced, advanced_v, advanced_s, stepped, reduced = k.signals[8:13]

        def spread(copy, dst, src):
            for rows in (LOW, UP):
                last = copy(dst[rows, :, rows], src[rows])
            return last

        for c in range(0, NC, 2):
            with stage(nc, k.signals) as block:
                @block.tensor
                def _(pe):
                    done = [Steps(pe, s) for s in made]
                    moved = Steps(pe, advanced)

                    def products(q, n, left, right):
                        pe_in, pe_by = mats[left], mats[right]
                        for j in range(4):
                            last = pe.matmul(bank[q][n][:, P * j:P * j + P], pe_in[:, q, j, :], pe_by[:, q, j, :], start=True, stop=True)
                        done[q](last)

                    def turned(q, n, name):
                        for j in range(4):
                            last = pe.transpose(bank[q][n][:, P * j:P * j + P], mats[name][:, q, j, :], k.c("ident"))
                        done[q](last)

                    def against(q, n, name):
                        for j in range(4):
                            last = pe.matmul(bank[q][n][:, P * j:P * j + P], mats[name][:, q, j, :],
                                             k.kr[:, j, c + q].rearrange("p x t -> p (x t)"), start=True, stop=True)
                        done[q](last)

                    def summed(out, width, terms):
                        for j in range(4):
                            for i, (left, right) in enumerate(terms):
                                last = pe.matmul(out[:, width * j:width * j + width], left[:, j, :], right(j), start=(i == 0), stop=(i == len(terms) - 1))
                        moved(last)

                    def full(t):
                        return lambda j: t[:, j, :]

                    def x_products(q):
                        summed(bank[q][1], P, ((mats["kappa"][:, q], full(state[:, q])), (mats["k_kappa"][:, q], full(mats["v_rows"][:, q]))))

                    for q in range(2):
                        pe.wait_ge(by_v[q], 1)
                        against(q, 0, "beta")
                    for q in range(2):
                        pe.wait_ge(by_s[q], 1)
                        against(q, 1, "k")
                    for q in range(2):
                        pe.wait_ge(by_s[q], 2)
                        turned(q, 2, "v")
                    for q in range(2):
                        pe.wait_ge(by_v[q], 2)
                        turned(q, 3, "blockT")
                    for q in range(2):
                        pe.wait_ge(by_v[q], 3)
                        pe.wait_ge(by_s[q], 3)
                        products(q, 2, "blockT", "block")
                        pe.wait_ge(by_v[q], 4)
                        products(q, 3, "block", "blockT")
                    for q in range(2):
                        pe.wait_ge(by_v[q], 7)
                        pe.wait_ge(by_s[q], 4)
                        products(q, 2, "n2T", "n2")
                        products(q, 3, "n2", "n2T")
                        turned(q, 0, "beta")
                        pe.wait_ge(by_v[q], 9)
                        turned(q, 1, "k")
                    for q in range(2):
                        pe.wait_ge(by_s[q], 6)
                        products(q, 0, "n2T", "d")
                        pe.wait_ge(by_v[q], 10)
                        products(q, 2, "n4", "n4T")
                    for q in range(2):
                        pe.wait_ge(by_v[q], 11)
                        products(q, 3, "n4T", "d")
                    for q in range(2):
                        pe.wait_ge(by_v[q], 12)
                        pe.wait_ge(by_s[q], 8)
                        products(q, 0, "n8T", "d")
                    for q in range(2):
                        pe.wait_ge(by_v[q], 13)
                        products(q, 2, "restT", "d")
                        products(q, 3, "d", "restT")
                        turned(q, 0, "d")
                    for q in range(2):
                        pe.wait_ge(by_s[q], 9)
                        pe.wait_ge(by_v[q], 14)
                        products(q, 2, "r", "rT")
                    pe.wait_ge(by_p[0], 1)
                    x_products(0)
                    for q in range(2):
                        pe.wait_ge(by_v[q], 16)
                        products(q, 3, "r2T", "r1")
                    for q in range(2):
                        pe.wait_ge(by_v[q], 17)
                        pe.wait_ge(by_s[q], 10)
                        products(q, 0, "total", "dT")
                    for q in range(2):
                        if q == 1:
                            pe.wait_ge(advanced_v, 3)
                            pe.wait_ge(by_p[1], 1)
                            x_products(1)
                        pe.wait_ge(by_s[q], 11)
                        pe.wait_ge(advanced_s, 2 * q + 1)
                        summed(bank[q][2], P, ((mats["inv"][:, q], full(x_mat)),))
                        pe.wait_ge(advanced_v, 3 * q + 1)
                        summed(bank[q][3], P, ((mats["beta_rows"][:, q], full(u_mat)), (mats["k_rows"][:, q], full(mats["v_rows"][:, q]))))
                        summed(bank[q][0], C, ((state[:, q], lambda j: k.kr[:, j, c + q, 1, :]), (u_mat, lambda j: beta_r[:, q, j, :]),
                                               (mats["v_rows"][:, q], lambda j: k_r[:, q, j, :])))

                @block.gpsimd
                def _(pool):
                    done = [Steps(pool, s) for s in by_p]
                    for q in range(2):
                        done[q](spread(pool.tensor_copy, mats["kappa"][:, q], k.kr[:, :, c + q, 0, :]))
                    for q in range(2):
                        done[q].wait()
                    samples.advance(pool, Steps(pool, stepped), reduced, c // 2)

                @block.scalar
                def _(act):
                    done = [Steps(act, s) for s in by_s]
                    moved = Steps(act, advanced_s)

                    def keep(q, after, name, n):
                        act.wait_ge(made[q], after)
                        done[q](act.copy(mats[name][:, q], pairs(bank[q][n])))

                    for q in range(2):
                        done[q](spread(act.copy, mats["k"][:, q], k.bk[:, :, c + q, 1, :]))
                    for q in range(2):
                        done[q](spread(act.copy, mats["v"][:, q], ft[:, V_SLOT:V_SLOT + 4, C * (c + q):C * (c + q + 1)]))
                    for q in range(2):
                        keep(q, 3, "v_rows", 2)
                    for q in range(2):
                        keep(q, 6, "n2T", 3)
                    for q in range(2):
                        keep(q, 9, "n4", 2)
                        keep(q, 9, "beta_rows", 0)
                    for q in range(2):
                        keep(q, 10, "k_rows", 1)
                    for q in range(2):
                        keep(q, 12, "n8T", 2)
                    for q in range(2):
                        keep(q, 15, "r", 2)
                    for q in range(2):
                        keep(q, 17, "dT", 0)
                    act.wait_ge(advanced, 1)
                    moved(act.copy(x_mat[:], pairs(bank[0][1])))
                    for q in range(2):
                        keep(q, 20, "inv", 0)
                    for q in range(2):
                        if q == 1:
                            act.wait_ge(advanced, 5)
                            moved(act.copy(x_mat[:], pairs(bank[1][1])))
                        act.wait_ge(advanced, 4 * q + 4)
                        moved(act.copy(ft[:, R_SLOT:R_SLOT + 4, C * (c + q):C * (c + q + 1)], bank[q][0][:, 0:4 * C].rearrange("p (j t) -> p j t", j=4)))

                @block.vector
                def _(dve):
                    done = [Steps(dve, s) for s in by_v]
                    moved = Steps(dve, advanced_v)
                    kappas, rs = (lambda t: pairs(t)[:, :, 0:C]), (lambda t: pairs(t)[:, :, C:P])

                    def masked(q, name, src, m):
                        for rows in (LOW, UP):
                            last = dve.tensor_tensor(mats[name][rows, q, :, rows], kappas(src)[rows], mask(m)[rows], ALU.mult)
                        done[q](last)

                    def keep(q, after, name, n):
                        dve.wait_ge(made[q], after)
                        done[q](dve.tensor_copy(mats[name][:, q], pairs(bank[q][n])))

                    def add(q, after, name, n, other):
                        dve.wait_ge(made[q], after)
                        done[q](dve.tensor_tensor(mats[name][:, q], pairs(bank[q][n]), other, ALU.add))

                    for q in range(2):
                        done[q](spread(dve.tensor_copy, mats["beta"][:, q], k.bk[:, :, c + q, 0, :]))
                    for q in range(2):
                        dve.wait_ge(made[q], 1)
                        masked(q, "blockT", bank[q][0], "block_before")
                    for q in range(2):
                        keep(q, 4, "block", 3)
                        add(q, 4, "d", 3, eye)
                    for q in range(2):
                        masked(q, "restT", bank[q][0], "block_earlier")
                        done[q](dve.tensor_tensor(beta_r[:, q], rs(bank[q][0]), mask("chunk_upto"), ALU.mult))
                        keep(q, 6, "n2", 2)
                    for q in range(2):
                        masked(q, "k_kappa", bank[q][1], "chunk_before")
                        done[q](dve.tensor_tensor(k_r[:, q], rs(bank[q][1]), mask("chunk_upto"), ALU.mult))
                    dve.wait_ge(stepped, 1)
                    dve.tensor_reduce(samples.sa[:, :], samples.tmp[:, :, :], AX.X, ALU.add).then_inc(reduced, 1)
                    for q in range(2):
                        keep(q, 10, "n4T", 3)
                    for q in range(2):
                        add(q, 11, "d", 0, mats["d"][:, q])
                    for q in range(2):
                        add(q, 13, "d", 3, mats["d"][:, q])
                    for q in range(2):
                        add(q, 14, "d", 0, mats["d"][:, q])
                    for q in range(2):
                        keep(q, 16, "rT", 3)
                    for q in range(2):
                        dve.wait_ge(by_s[q], 9)
                        done[q](dve.tensor_tensor(mats["r1"][:, q], mats["r"][:, q], eye, ALU.add))
                    for q in range(2):
                        keep(q, 18, "r2T", 2)
                    for q in range(2):
                        add(q, 19, "total", 3, mats["r1"][:, q])
                    for q in range(2):
                        if q == 1:
                            dve.wait_ge(stepped, 7)
                            dve.tensor_reduce(samples.y[:, c // 2, :], samples.tmp[:, :, :], AX.X, ALU.add)
                        dve.wait_ge(advanced, 4 * q + 2)
                        moved(dve.tensor_copy(u_mat[:], pairs(bank[q][2])))
                        dve.wait_ge(advanced, 4 * q + 3)
                        new = state[:, 1 - q]
                        moved.then(dve.tensor_tensor(new, state[:, q], pairs(bank[q][3]), ALU.add))
                        moved(dve.tensor_tensor(new, new, k.ends[:, :, c + q].unsqueeze(2).to_broadcast([P, 4, P]), ALU.mult))
        banks.close()
        outT = x_mat
        row = own["a"][0:NS].rearrange("p q j f -> p (q j f)")[:, 0:GW]
        turn(nc, k, "rc_state", [([state[:, 0, j, :] for j in range(4)], [(lambda b: b[:, :].rearrange("p (j f) -> p j f", j=4), outT[:, :, :])])])
        with stage(nc, k.signals) as block:
            @block.scalar
            def _(act):
                store = Loads(act, k.signals[0])
                samples.store_states(store)
                for h in range(H8):
                    r = h % 2
                    store(k.p_wkv[bass.ds(l, 1), 0, h].rearrange("a i j -> (a i) j"), outT[C * r:C * r + C, h // 2, C * r:C * r + C])
                store.wait()

            @block.sync
            def _(sp):
                samples.store(Loads(sp, k.signals[1]), Loads(sp, k.signals[2]), row)
        turn(nc, k, "rsy", [([row[:, P * i:P * i + P] for i in range(4)], [(side_by_side(NS, 4), ft[:, R_SLOT:R_SLOT + 4, NP:NT])])])


def rwkv_out(nc, k):
    ft = k.ft
    with ExitStack() as ctx:
        sb, ps = scope(nc, ctx)
        sq = sb("ro_sq", [P, 4, NT])
        sums = ps("ro_sums", [P, 4, 512])
        sums_s = ps("ro_sums_s", [P, 2, 512])
        summed, centered, squared, scaled, powered, stepped, logged = k.signals[:7]
        with stage(nc, k.signals) as block:
            @block.tensor
            def _(pe):
                def sum_up(x, i, kind):
                    pe.matmul(sums[:, i, :], k.c("head_ones"), x[:, 0:NP], start=True, stop=True)
                    pe.matmul(sums_s[:, kind, NS * i:NS * i + NS], k.c("head_ones"), x[:, NP:NT], start=True, stop=True).then_inc(summed, 1)

                for i in range(4):
                    if i >= 1:
                        pe.wait_ge(centered, i)
                    sum_up(ft[:, R_SLOT + i, :], i, 0)
                for i in range(4):
                    pe.wait_ge(squared, i + 1)
                    if i >= 1:
                        pe.wait_ge(scaled, 2 * i)
                    sum_up(sq[:, i, :], i, 1)

            @block.scalar
            def _(act):
                for i in range(4):
                    act.wait_ge(centered, i + 1)
                    act.activation(sq[:, i, :], ft[:, R_SLOT + i, :], ACT.Square).then_inc(squared, 1)
                inverse_roots(act, scaled, logged, powered, sq)

            @block.vector
            def _(dve):
                step = Steps(dve, stepped)
                def both(i, kind):
                    return ((slice(0, NP), sums[:, i, :]), (slice(NP, NT), sums_s[:, kind, NS * i:NS * i + NS]))

                for i in range(4):
                    y = ft[:, R_SLOT + i, :]
                    dve.wait_ge(summed, i + 1)
                    for cols, total in both(i, 0):
                        last = dve.scalar_tensor_tensor(y[:, cols], total, -1.0 / C, y[:, cols], ALU.mult, ALU.add)
                    last.then_inc(centered, 1)
                for i in range(4):
                    dve.wait_ge(summed, 4 + i + 1)
                    for cols, total in both(i, 1):
                        dve.tensor_scalar(sq[:, i, cols], total, 1.0 / C, LN_EPS, ALU.mult, ALU.add).then_inc(scaled, 1)
                for i in range(4):
                    y, out = ft[:, R_SLOT + i, :], k.mixT[:, 12 + i, :]
                    dve.wait_ge(powered, i + 1)
                    step.then(dve.scalar_tensor_tensor(y, y, k.prm[:, ROW_LNW + i:ROW_LNW + i + 1], sq[:, i, :], ALU.mult, ALU.mult))
                    dve.scalar_tensor_tensor(out, y, k.prm[:, ROW_LNB + i:ROW_LNB + i + 1], k.bonus[:, i, :], ALU.add, ALU.add)


INPUTS = ["x_prompt", "x_sample", "cache_sb_kv", "cache_dsa", "state_ret", "state_wkv", "state_shift", "page_table",
          "norm_g", "w_in", "shift_mu", "rw_w0", "rw_w2", "rw_a0", "rw_a2", "rw_kk", "rw_ka", "rw_rk",
          "rw_lnx_w", "rw_lnx_b", "w_out", "final_g"]
OUTPUTS = [("y_prompt", (1, NP, D)), ("y_sample", (NB, DS, D)),
           ("p_sb", (DEPTH, 1, NP, 2, 4, P)), ("p_dsa", (DEPTH, 1, NP, DSA_W)), ("p_ret", (DEPTH, 1, 4, 64, P)),
           ("p_wkv", (DEPTH, 1, H8, 64, 64)), ("p_shift", (DEPTH, 1, SHIFT_W)),
           ("s_sb", (DEPTH, NB, DS, 2, 4, P)), ("s_dsa", (DEPTH, NB, DS, DSA_W)), ("s_ret", (DEPTH, NB, 4, 64, P)),
           ("s_wkv", (DEPTH, NB, H8, 64, 64)), ("s_shift", (DEPTH, NB, SHIFT_W))]


def build(nc, tensors, groups="ABCD", probe=None):
    k = Core(tensors)
    with ExitStack() as ctx, nc.allow_non_contiguous_dma(reason="rows of a few values"):
        sb, _ = scope(nc, ctx)
        k.signals = [ctx.enter_context(nc.semaphore(f"signal_{i}")) for i in range(24)]
        k.table = sb("table", [P, TABLE.shape[1]])
        k.c = lambda name: k.table[:, AT[name][0]:AT[name][0] + AT[name][1]]
        k.prm = sb("prm", [P, PRM_ROWS])
        k.pages = sb("pages", [1, NB * PAGES], I32)
        k.scratch = sb("scratch", [P, 2, NT])
        k.mixT = sb("mixT", [P, KT, NT])
        k.x_spill = nc.dram_tensor("x_spill", (P, KT * NT), F32, kind="Internal").ap()
        k.sample_rows = nc.dram_tensor("sample_rows", (NS, 6 * GW), F32, kind="Internal").ap()
        k.sample_y = nc.dram_tensor("sample_y", (NS, GW), F32, kind="Internal").ap()
        k.sample_w = nc.dram_tensor("sample_w", (NS, 8), F32, kind="Internal").ap()
        arrived, arrived_x = k.signals[:2]
        with ExitStack() as own:
            sb2, _ = scope(nc, own)
            rows = sb2("x_in_rows", [P, TT, D])
            k.xT = sb2("xT_in", [P, KT, NT])
            with stage(nc, k.signals) as block:
                @block.sync
                def _(sp):
                    load = Loads(sp, arrived)
                    load(k.table[:, :], k.consts)
                    load(k.pages[:, :], k.page_table.rearrange("a b -> (a b)").unsqueeze(0))
                    load.wait()

                @block.scalar
                def _(act):
                    load = Loads(act, arrived_x)
                    load(rows[:, 0:QB, :], k.x_prompt.rearrange("b (a p) d -> p (b a) d", p=P))
                    load(rows[0:NS, QB, :], k.x_sample.rearrange("b t d -> (b t) d"))
                    load.wait()

                @block.vector
                def _(dve):
                    dve.memset(k.mixT[:, :, :], 0.0)

            turn_x(nc, k, rows)
            store_x(nc, k)

        with nc.Fori(0, DEPTH) as l:
            with ExitStack() as layer:
                sb2, _ = scope(nc, layer)
                k.ft = sb2("ft", [P, SLOTS, NT])
                with ExitStack() as most:
                    sb3, _ = scope(nc, most)
                    k.h = split_pair(sb3, "h")
                    with ExitStack() as own:
                        k.xT = scope(nc, own)[0]("xT_norm", [P, KT, NT])
                        load_parameters(nc, k, l)
                        norm(nc, k, "norm", k.prm[:, ROW_G:ROW_G + KT], k.h)
                    due = None
                    for letter, name, tiles, mixer, first in (("A", "ret", RET_TILES, retention, 0), ("B", "sb", SB_TILES, stick_breaking, 4),
                                                              ("C", "dsa", DSA_TILES, sparse_attention, 8)):
                        if letter in groups:
                            with ExitStack() as own:
                                weight_buffers(k, name, scope(nc, own)[0])
                                project_group(nc, k, l, name, tiles, list(range(len(tiles) - 4, len(tiles))), due)
                            mixer(nc, k, l)
                            due = (first, len(tiles) - 4)
                    if "D" in groups:
                        weight_buffers(k, "rw", sb3)
                        project_group(nc, k, l, "rw", RW_TILES, list(range(RG_SLOT, RG_SLOT + 4)), due)
                if "D" in groups:
                    rwkv(nc, k, l)
                if probe is not None:
                    moved, = k.signals[:1]
                    with stage(nc, k.signals) as block:
                        @block.sync
                        def _(sp):
                            sp.dma_start(probe[bass.ds(l, 1)].rearrange("a p n -> (a p) n"), k.mixT[:, :, :].rearrange("p k t -> p (k t)")).then_inc(moved, 16)
                            sp.wait_ge(moved, 16)
            with ExitStack() as own:
                k.xT = scope(nc, own)[0]("xT_out", [P, KT, NT])
                project_out(nc, k, l)
        with ExitStack() as own:
            k.xT = scope(nc, own)[0]("xT_last", [P, KT, NT])
            store_y(nc, k)


def kernel(**inputs):
    import numpy as _np
    import concourse.bacc as _bacc
    from concourse.bass_utils import run_bass_kernel_spmd as _run

    nc = _bacc.Bacc("TRN2", target_bir_lowering=False, num_devices=1)
    arrays, tensors = {"in_consts": TABLE}, {}
    for name in INPUTS:
        arrays["in_" + name] = _np.ascontiguousarray(inputs[name])
    for name, a in arrays.items():
        tensors[name[3:]] = nc.dram_tensor(name, a.shape, mybir.dt.from_np(a.dtype), kind="ExternalInput").ap()
    for name, shape in OUTPUTS:
        tensors[name] = nc.dram_tensor("out_" + name, shape, F32, kind="ExternalOutput").ap()
    build(nc, tensors)
    r = _run(nc, [arrays], core_ids=[0])
    return tuple(r.results[0]["out_" + name] for name, _ in OUTPUTS)
```
